# Optimizing a Trainium2 kernel written in Bass

```python
import jax, jax.numpy as jnp
from jax import lax
import numpy as np

D_MODEL = 1024
BATCH = 1
SEQ = 512
DEPTH = 1
DEC_BATCH = 8
DEC_SEQ = 8
PAST_LEN = 4096
PAGE_SIZE = 128

MIX_WIDTH = D_MODEL
SGU_WIDTH = MIX_WIDTH // 2
CONV_WIDTH = MIX_WIDTH - SGU_WIDTH
SGU_HEADS = 4
SGU_HEAD_DIM = SGU_WIDTH // SGU_HEADS
CHUNK = 128
CONV_K = 31
MEM_TOKENS = 256
X_HEADS = 4
X_HEAD_DIM = D_MODEL // X_HEADS
FFN_DIM = 4 * D_MODEL
IN_COLS = 2 * SGU_WIDTH + 2 * CONV_WIDTH
EPS = 1e-6

kernel_name = 'hymba_sgu_conformer_macaron_decoder_step'

def rms_norm(x, g):
    xf = x.astype(jnp.float32)
    y = xf * lax.rsqrt(jnp.mean(xf * xf, axis=-1, keepdims=True) + EPS)
    return (y * g.astype(jnp.float32)).astype(x.dtype)

def layer_norm(x, g, b):
    xf = x.astype(jnp.float32)
    mu = jnp.mean(xf, axis=-1, keepdims=True)
    xc = xf - mu
    y = xc * lax.rsqrt(jnp.mean(xc * xc, axis=-1, keepdims=True) + EPS)
    return (y * g.astype(jnp.float32) + b.astype(jnp.float32)).astype(x.dtype)

def macaron_ffn(x, g_pre, w_gate, w_up, w_down, g_post):
    n = rms_norm(x, g_pre)
    f = (jax.nn.silu(n @ w_gate) * (n @ w_up)) @ w_down
    return x + 0.5 * rms_norm(f, g_post)

def spatial_gate(u, v, w_s, b_s):
    bsz, L, _ = v.shape
    n_chunks = -(-L // CHUNK)
    pad = n_chunks * CHUNK - L
    vp = jnp.pad(v, ((0, 0), (0, pad), (0, 0))).reshape(bsz, n_chunks, CHUNK, SGU_HEADS, SGU_HEAD_DIM)
    causal = jnp.tril(jnp.ones((CHUNK, CHUNK), dtype=bool))
    ws = jnp.where(causal, w_s, jnp.zeros_like(w_s))
    s = jnp.einsum('hij,bnjhd->bnihd', ws, vp) + b_s.T[:, :, None]
    s = s.reshape(bsz, n_chunks * CHUNK, SGU_WIDTH)[:, :L]
    return u * s

def causal_dwconv(a, left, w, b):
    full = jnp.concatenate([left, a], axis=1)
    y = lax.conv_general_dilated(full, w[:, None, :], window_strides=(1,), padding='VALID',
                                 dimension_numbers=('NWC', 'WIO', 'NWC'),
                                 feature_group_count=a.shape[-1])
    return y + b, full[:, -(CONV_K - 1):]

def token_mixing(h, conv_left, g_pre, w_in, sgu_ln_g, sgu_ln_b, w_s, b_s,
                 conv_w, conv_b, conv_ln_g, conv_ln_b, w_out, g_post):
    n = rms_norm(h, g_pre)
    z = n @ w_in
    u, v, a, gate = jnp.split(z, [SGU_WIDTH, 2 * SGU_WIDTH, 2 * SGU_WIDTH + CONV_WIDTH], axis=-1)
    v = layer_norm(v, sgu_ln_g, sgu_ln_b)
    out_a = spatial_gate(u, v, w_s, b_s)
    glu = a * jax.nn.sigmoid(gate)
    c, conv_state = causal_dwconv(glu, conv_left, conv_w, conv_b)
    out_b = jax.nn.silu(layer_norm(c, conv_ln_g, conv_ln_b))
    o = jnp.concatenate([out_a, out_b], axis=-1) @ w_out
    L = v.shape[1]
    rows = L - ((L - 1) // CHUNK) * CHUNK
    return h + rms_norm(o, g_post), conv_state, v[:, L - rows:]

def memory_kv(mem, g_mem, w_k, w_v):
    bsz, m, _ = mem.shape
    mn = rms_norm(mem, g_mem)
    k = (mn @ w_k).reshape(bsz, m, X_HEADS, X_HEAD_DIM)
    v = (mn @ w_v).reshape(bsz, m, X_HEADS, X_HEAD_DIM)
    return k, v

def cross_attend(h, k, v, g_pre, w_q, w_o, g_post):
    bsz, L, _ = h.shape
    n = rms_norm(h, g_pre)
    q = (n @ w_q).reshape(bsz, L, X_HEADS, X_HEAD_DIM)
    s = jnp.einsum('blhd,bmhd->bhlm', q, k).astype(jnp.float32) * (X_HEAD_DIM ** -0.5)
    p = jax.nn.softmax(s, axis=-1).astype(v.dtype)
    o = jnp.einsum('bhlm,bmhd->blhd', p, v).reshape(bsz, L, X_HEADS * X_HEAD_DIM)
    return h + rms_norm(o @ w_o, g_post)

def setup_inputs(seed: int = 0) -> dict:
    key = jax.random.key(seed)
    ks = iter(jax.random.split(key, 48))

    def nrm(shape, scale):
        return jax.random.normal(next(ks), shape, jnp.float32) * scale

    def gain(shape):
        return 1.0 + nrm(shape, 0.02)

    L = DEPTH
    d = D_MODEL
    return {
        'x_prompt': nrm((BATCH, SEQ, d), 1.0),
        'x_sample': nrm((DEC_BATCH, DEC_SEQ, d), 1.0),
        'mem_prompt': nrm((BATCH, MEM_TOKENS, d), 1.0),
        'cache_mem_k': nrm((L, DEC_BATCH, MEM_TOKENS, X_HEADS, X_HEAD_DIM), 1.0),
        'cache_mem_v': nrm((L, DEC_BATCH, MEM_TOKENS, X_HEADS, X_HEAD_DIM), 1.0),
        'state_conv': nrm((L, DEC_BATCH, CONV_K - 1, CONV_WIDTH), 0.5),
        'ffn1_g_pre': gain((L, d)),
        'ffn1_w_gate': nrm((L, d, FFN_DIM), d ** -0.5),
        'ffn1_w_up': nrm((L, d, FFN_DIM), d ** -0.5),
        'ffn1_w_down': nrm((L, FFN_DIM, d), FFN_DIM ** -0.5),
        'ffn1_g_post': gain((L, d)),
        'mix_g_pre': gain((L, d)),
        'mix_w_in': nrm((L, d, IN_COLS), d ** -0.5),
        'sgu_ln_g': gain((L, SGU_WIDTH)),
        'sgu_ln_b': nrm((L, SGU_WIDTH), 0.02),
        'sgu_w_s': nrm((L, SGU_HEADS, CHUNK, CHUNK), CHUNK ** -0.5),
        'sgu_b_s': 1.0 + nrm((L, SGU_HEADS, CHUNK), 0.02),
        'conv_w': nrm((L, CONV_K, CONV_WIDTH), CONV_K ** -0.5),
        'conv_b': nrm((L, CONV_WIDTH), 0.02),
        'conv_ln_g': gain((L, CONV_WIDTH)),
        'conv_ln_b': nrm((L, CONV_WIDTH), 0.02),
        'mix_w_out': nrm((L, MIX_WIDTH, d), MIX_WIDTH ** -0.5),
        'mix_g_post': gain((L, d)),
        'mem_g': gain((L, d)),
        'xattn_g_pre': gain((L, d)),
        'xattn_w_q': nrm((L, d, X_HEADS * X_HEAD_DIM), d ** -0.5),
        'xattn_w_k': nrm((L, d, X_HEADS * X_HEAD_DIM), d ** -0.5),
        'xattn_w_v': nrm((L, d, X_HEADS * X_HEAD_DIM), d ** -0.5),
        'xattn_w_o': nrm((L, X_HEADS * X_HEAD_DIM, d), (X_HEADS * X_HEAD_DIM) ** -0.5),
        'xattn_g_post': gain((L, d)),
        'ffn2_g_pre': gain((L, d)),
        'ffn2_w_gate': nrm((L, d, FFN_DIM), d ** -0.5),
        'ffn2_w_up': nrm((L, d, FFN_DIM), d ** -0.5),
        'ffn2_w_down': nrm((L, FFN_DIM, d), FFN_DIM ** -0.5),
        'ffn2_g_post': gain((L, d)),
    }

def reference(x_prompt, x_sample, mem_prompt, cache_mem_k, cache_mem_v, state_conv,
              ffn1_g_pre, ffn1_w_gate, ffn1_w_up, ffn1_w_down, ffn1_g_post,
              mix_g_pre, mix_w_in, sgu_ln_g, sgu_ln_b, sgu_w_s, sgu_b_s,
              conv_w, conv_b, conv_ln_g, conv_ln_b, mix_w_out, mix_g_post,
              mem_g, xattn_g_pre, xattn_w_q, xattn_w_k, xattn_w_v, xattn_w_o, xattn_g_post,
              ffn2_g_pre, ffn2_w_gate, ffn2_w_up, ffn2_w_down, ffn2_g_post):

    def run_layer(x, conv_left, mem_k, mem_v, l):
        h = macaron_ffn(x, ffn1_g_pre[l], ffn1_w_gate[l], ffn1_w_up[l], ffn1_w_down[l], ffn1_g_post[l])
        h, conv_state, chunk_v = token_mixing(
            h, conv_left, mix_g_pre[l], mix_w_in[l], sgu_ln_g[l], sgu_ln_b[l], sgu_w_s[l], sgu_b_s[l],
            conv_w[l], conv_b[l], conv_ln_g[l], conv_ln_b[l], mix_w_out[l], mix_g_post[l])
        h = cross_attend(h, mem_k, mem_v, xattn_g_pre[l], xattn_w_q[l], xattn_w_o[l], xattn_g_post[l])
        h = macaron_ffn(h, ffn2_g_pre[l], ffn2_w_gate[l], ffn2_w_up[l], ffn2_w_down[l], ffn2_g_post[l])
        return h, conv_state, chunk_v

    hp, hs = x_prompt, x_sample
    mk_p, mv_p, cs_p, cs_s, cv_p, cv_s = [], [], [], [], [], []
    for l in range(DEPTH):
        k_p, v_p = memory_kv(mem_prompt, mem_g[l], xattn_w_k[l], xattn_w_v[l])
        left_p = jnp.zeros((hp.shape[0], CONV_K - 1, CONV_WIDTH), hp.dtype)
        hp, conv_p, chunk_p = run_layer(hp, left_p, k_p, v_p, l)
        hs, conv_s, chunk_s = run_layer(hs, state_conv[l], cache_mem_k[l], cache_mem_v[l], l)
        mk_p.append(k_p)
        mv_p.append(v_p)
        cs_p.append(conv_p)
        cs_s.append(conv_s)
        cv_p.append(chunk_p)
        cv_s.append(chunk_s)

    return (hp, hs, jnp.stack(mk_p), jnp.stack(mv_p), jnp.stack(cs_p), jnp.stack(cs_s),
            jnp.stack(cv_p), jnp.stack(cv_s))


_drawn_inputs = setup_inputs


def setup_inputs(seed=0):
    import zlib

    import numpy as np

    out = dict(_drawn_inputs(seed))
    spreads = {}
    factors = {'ffn1_g_pre': 3.885,
     'ffn1_g_post': 5.909,
     'sgu_ln_g': 8.091,
     'sgu_ln_b': 8.57,
     'sgu_b_s': 4.702,
     'conv_b': 4.197,
     'conv_ln_g': 7.084,
     'conv_ln_b': 8.0,
     'mix_g_post': 4.064,
     'mem_g': 2.911,
     'xattn_g_pre': 4.992,
     'xattn_g_post': 18.973,
     'ffn2_g_pre': 28.985,
     'ffn2_g_post': 47.087}
    for name, (base, spread) in spreads.items():
        noise = np.random.default_rng([zlib.crc32(name.encode()), seed]).standard_normal(out[name].shape)
        drawn = base * np.exp(spread * noise) if base else spread * noise
        out[name] = __import__('jax').numpy.asarray(drawn.astype(out[name].dtype))
    for name, factor in factors.items():
        out[name] = (out[name] * factor).astype(out[name].dtype)
    return out
```

```python
from contextlib import ExitStack

import concourse.bass as bass
from concourse import mybir

F32 = mybir.dt.float32
F32R = mybir.dt.float32r
ACT = mybir.ActivationFunctionType
ALU = mybir.AluOpType
AX_X = mybir.AxisListType.X
ds = bass.ds

SPLIT = True
PARTS = 2 if SPLIT else 1
PDT = F32R if SPLIT else F32
PRODUCTS = [(0, 0), (0, 1), (1, 0)] if SPLIT else [(0, 0)]

P = 128
D = 1024
KT = D // P
FFN = 4096
SEQ = 512
NB = 8
DEC = 8
T = SEQ + NB * DEC
HALF = T // 2
BLOCKS = FFN // D
MEM = 256
MT = MEM // P
HEADS = 4
SGW = 512
CW = 512
CT = CW // P
TAPS = 31
LEFT = TAPS - 1
GLU_S = LEFT + SEQ
GLU_W = GLU_S + NB * (LEFT + DEC)
EPS = 1e-6
TT = 5
JOBS_PER_BLOCK = 3 * KT
RAW = 2 if SPLIT else 4


def token_tile(i):
    return i * P, (P if i < 4 else NB * DEC)


class Plan:

    def __init__(self):
        self.n = 0
        self.jobs = 0
        self.aux = {}
        self.base = {}

    def job_run(self, name, count):
        self.base[name] = (self.jobs, self.n)
        self.jobs += count
        self.n += count

    def use(self, *names):
        for name in names:
            self.aux[name] = (len(self.aux), self.n)
            self.n += 1


def make_plan():
    pl = Plan()
    pl.use("gains", "convw", "spatial", "mem0", "mem1", *[f"x{i}" for i in range(TT)])
    pl.job_run("k", 8)
    pl.use("pre1")
    pl.job_run("v", 8)
    pl.use("ktok0", "ktok1", "vtok0", "vtok1")
    pl.job_run("ffn1", BLOCKS * JOBS_PER_BLOCK)
    pl.use("post1", "pre2", "state0", "state1")
    pl.job_run("glu0", 4)
    pl.job_run("glu1", 4)
    pl.job_run("sv0", 1)
    pl.job_run("sv1", 1)
    pl.use("vt0")
    pl.job_run("sv2", 1)
    pl.use("vt1")
    pl.job_run("sv3", 1)
    pl.use("vt2")
    pl.job_run("u0", 1)
    pl.use("vt3")
    pl.job_run("u1", 1)
    pl.job_run("u2", 1)
    pl.job_run("u3", 1)
    pl.use("sg0", "sg1", "sg2", "sg3", "glup", "glus", "cmean", "cvar")
    pl.job_run("out", 8)
    pl.use("post2", "pre3")
    pl.job_run("q", 8)
    for i in range(4):
        pl.use(f"sc{i}")
        for b in (2 * i, 2 * i + 1):
            pl.use(f"kta{b}", f"ktb{b}")
            if b:
                pl.use(f"ss{b - 1}")
        if i:
            pl.use(f"pt{i - 1}")
    pl.use("ss7", "pt3", "sroll", "pv0", "pv1", "sprob", *[f"pv{o}" for o in range(2, 8)], "pvs")
    pl.job_run("o", 8)
    pl.use("post3", "pre4")
    pl.job_run("ffn2", BLOCKS * JOBS_PER_BLOCK)
    pl.use("post4", *[f"y{i}" for i in range(TT)])
    return pl


def build(nc, a, out):
    pl = make_plan()
    y_prompt, y_sample, mem_k_o, mem_v_o, cs_p, cs_s, cv_p, cv_s = out
    w2 = {n: a[n].rearrange("l r c -> (l r) c") for n in (
        "ffn1_w_gate", "ffn1_w_up", "ffn1_w_down", "ffn2_w_gate", "ffn2_w_up", "ffn2_w_down", "mix_w_in",
        "mix_w_out", "xattn_w_q", "xattn_w_k", "xattn_w_v", "xattn_w_o")}
    x_p = a["x_prompt"].rearrange("b s d -> (b s) d")
    x_s = a["x_sample"].rearrange("b s d -> (b s) d")
    ck = a["cache_mem_k"].rearrange("l b m h d -> (l b) m (h d)")
    cv = a["cache_mem_v"].rearrange("l b m h d -> (l b) m (h d)")

    ctx = ExitStack()
    with ctx:
        def sb(name, shape, dt=F32):
            return ctx.enter_context(nc.sbuf_tensor(name, shape, dt))

        def views(name, *tiles):
            size = 0
            found = {}
            for group in tiles:
                used = 0
                with ExitStack() as inner:
                    for n, shape, dt in group:
                        found[n] = inner.enter_context(nc.sbuf_tensor(n, shape, dt))
                        words = 1
                        for s in shape[1:]:
                            words *= s
                        used += words
                size = max(size, used)
            sb(name, [P, size])
            return found

        def sem(name):
            return ctx.enter_context(nc.semaphore(name))

        ident = sb("ident", [P, P])
        ones = sb("ones", [P, P])
        epst = sb("epst", [P, 2])
        gvec = sb("gvec", [P, 84])
        convw = sb("convw", [P, CT, TAPS + 1])
        wsT = sb("wsT", [P, 4, P])
        bd = sb("bd", [NB * DEC, 4, NB * DEC])
        bsb = sb("bsb", [P, 4, P])
        osm = sb("osm", [P, CW])
        gsm = sb("gsm", [P, CT, NB * DEC])
        small = sb("small", [P, 96])
        mx, sm = small[:, 0:16], small[:, 16:32]
        smx, ssm = small[:, 32:34], small[:, 34:36]
        mss = small[:, 36:38]
        bst, bag = small[:, 40:70], small[:, 70:80]
        vrs = small[:, 80:85]
        h = sb("h", [P, KT, T])
        kT = sb("kT", [P, KT, MEM])
        vtok = sb("vtok", [P, MT, D])
        R = sb("R", [P, T])
        raw = sb("raw", [P, RAW, KT, 256])
        wp = sb("wp", [P, 2, PARTS, KT, P], PDT) if SPLIT else None
        rn = views("region_n", [("n", [P, PARTS, KT, T], PDT)],
                   [("pT", [P, 8, SEQ], F32), ("kts", [P, 2, KT, MEM], F32)],
                   [("pT_", [P, 8, SEQ], F32), ("vx", [P, 2, MT, D], F32)], [("memraw", [P, MT, D], F32)])
        rm = views("region_mid", [("mid", [P, PARTS, KT, T], PDT)],
                   [("prob", [P, 2, HEADS, MEM], F32), ("k3", [P, MT, D], F32)],
                   [("memT", [P, PARTS, KT, MEM], PDT)],
                   [("lng", [P, SGW], F32), ("lnb", [P, SGW], F32), ("straw", [120, 2, CW], F32)])
        rf = views("region_f", [("f", [P, KT, T], F32)], [("vT", [P, KT, MEM], F32), ("ktok", [P, MT, D], F32)],
                   [("memF", [P, KT, MEM], F32), ("wsr", [P, 4, P], F32), ("graw", [84, P], F32), ("cwraw", [TAPS, CW], F32)])
        rx = views("region_x", [("xin", [P, TT, D], F32)],
                   [("sv", [P, TT, SGW], F32), ("glu", [P, CT, GLU_W], F32)],
                   [("kring", [P, 3, MT, D], F32)], [("ytok", [P, 3, D], F32)])
        rt = views("region_t", [("sq", [P, 2, T], F32), ("sil", [P, 2, T], F32)],
                   [("sT", [P, MT, NB * 32], F32), ("psm", [P, 2, MEM], F32), ("pTs", [P, MT, NB * 32], F32)])
        n, pT, kts, vx, memraw = rn["n"], rn["pT"], rn["kts"], rn["vx"], rn["memraw"]
        mid, prob, k3, memT = rm["mid"], rm["prob"], rm["k3"], rm["memT"]
        lng, lnb, straw = rm["lng"], rm["lnb"], rm["straw"]
        f, vT, ktok, memF, wsr, graw, cwraw = (rf[k] for k in ("f", "vT", "ktok", "memF", "wsr", "graw", "cwraw"))
        xin, sv, glu, kring, ytok = (rx[k] for k in ("xin", "sv", "glu", "kring", "ytok"))
        sq, sil, sT, psm, pTs = (rt[k] for k in ("sq", "sil", "sT", "psm", "pTs"))
        slots = [ctx.enter_context(nc.psum_tensor(f"slot{i}", [P, 2, 512], F32)) for i in range(4)]

        HI0 = {"ffn1": 0, "mix": KT * BLOCKS, "att": KT * BLOCKS + 8, "ffn2": KT * BLOCKS + 8 + KT + 1}
        MID0 = {"ffn1": MT, "mix": MT + KT * BLOCKS, "ffn2": MT + KT * BLOCKS + 8}
        memjunk = sq[:, :, :].rearrange("p a b -> p (a b)")[:, 0:D]
        epst4 = epst[:, 1:2]
        GAINS = ["ffn1_g_pre", "ffn1_g_post", "mix_g_pre", "mix_g_post", "mem_g", "xattn_g_pre",
                 "xattn_g_post", "ffn2_g_pre", "ffn2_g_post"]
        gain = {name: [gvec[:, 8 * i + t:8 * i + t + 1] for t in range(KT)] for i, name in enumerate(GAINS)}
        CV0 = 8 * len(GAINS)
        convb, clg, clb = ([gvec[:, CV0 + 4 * i + t:CV0 + 4 * i + t + 1] for t in range(CT)] for i in range(3))

        slot_free = [sem(f"slot_free{i}") for i in range(4)]
        job_done = sem("job_done")
        filled = sem("filled")
        loaded = [sem(f"loaded{i}") for i in range(RAW)]
        whi, wlo = sem("whi"), sem("wlo")
        ld_small, ld_cw, ld_ws, ld_bs, ld_ln, ld_st = (sem(f"ld_{x}") for x in ("small", "cw", "ws", "bs", "ln", "st"))
        ld_mem, ld_xs, ld_bd = sem("ld_mem"), sem("ld_xs"), sem("ld_bd")
        ld_x = [sem(f"ld_x{i}") for i in range(2)]
        ld_k = [sem(f"ld_k{i}") for i in range(4)]
        ld_v = [sem(f"ld_v{i}") for i in range(5)]
        id_set, const_set, masked, bd_zero, glu_zero, eps_set = (
            sem(x) for x in ("id_set", "const_set", "masked", "bd_zero", "glu_zero", "eps_set"))
        mem_sq, mem_rt, mem_rs, mem_n, memhi = (sem(x) for x in ("mem_sq", "mem_rt", "mem_rs", "mem_n", "memhi"))
        f_zero = sem("f_zero")
        gated, mid_hi, mid_ready = sem("gated"), sem("mid_hi"), sem("mid_ready")
        sums = {}
        for s in ("pre1", "post1", "pre2", "cmean", "cvar", "post2", "pre3", "post3", "pre4", "post4"):
            parts = ["squared", "summed", "recip"]
            if s.startswith("p"):
                parts.append("done")
            if s.startswith("post") or (SPLIT and s.startswith("pre")):
                parts.append("scaled")
            if SPLIT and s.startswith("pre"):
                parts.append("hi")
            sums[s] = {x: sem(f"{s}_{x}") for x in parts}
        sv_st, sv_mv, sv_rt, sv_rs, sv_n, sv_g, sv_b = (
            sem(x) for x in ("sv_st", "sv_mv", "sv_rt", "sv_rs", "sv_n", "sv_g", "sv_b"))
        conv_step, cc_ready, cn_ready, act_b = (sem(x) for x in ("conv_step", "cc_ready", "cn_ready", "act_b"))
        mx_ready, rs_ready, p_ready = sem("mx_ready"), sem("rs_ready"), sem("p_ready")
        smx_ready, srs_ready, sp_ready = sem("smx_ready"), sem("srs_ready"), sem("sp_ready")
        vs_used, gs_ready = sem("vs_used"), sem("gs_ready")
        stored, y_stored = sem("stored"), [sem(f"y_stored{i}") for i in range(3)]

        def slot(u):
            return slots[u % 4]

        def aux(name):
            return slot(pl.aux[name][1])

        def flat(s):
            return s[:, :, :].rearrange("p a b -> p (a b)")

        def eight(s):
            return flat(s).rearrange("p (t c) -> p t c", c=P)

        def halves(ap):
            return ap.rearrange("p (a b) -> p a b", a=2)

        def wait_aux(eng, name):
            eng.wait_ge(filled, pl.aux[name][0] + 1)

        def wait_slot(pe, u, plus=0):
            if u >= 4:
                pe.wait_ge(slot_free[u % 4], u // 4 + plus)

        def wait_use_freed(eng, u):
            eng.wait_ge(slot_free[u % 4], u // 4 + 1)

        def wait_freed(eng, name):
            wait_use_freed(eng, pl.aux[name][1])

        def free(ins, u):
            ins.then_inc(slot_free[u % 4], 1)

        def free_aux(ins, name):
            free(ins, pl.aux[name][1])

        mix_in_cols = [1536, 1024, 1792, 1280, 512, 768, 0, 256]
        before = [("xattn_w_k", c * 256) for c in range(4)] + [("xattn_w_v", c * 256) for c in range(4)]
        between = ([("mix_w_in", c) for c in mix_in_cols] + [("mix_w_out", c * 256) for c in range(4)]
                   + [("xattn_w_q", c * 256) for c in range(4)] + [("xattn_w_o", c * 256) for c in range(4)])
        N_SLABS = pl.jobs // 2


        def static_slab(s):
            k0, m0 = pl.base["k"][0] // 2, pl.base["glu0"][0] // 2
            o0 = pl.base["o"][0] // 2
            name, c = before[s - k0] if s < m0 else between[s - m0]
            assert s < len(before) or m0 <= s < o0 + 4
            return w2[name].rearrange("(t p) c -> p t c", p=P)[:, :, c:c + 256]

        def per_body(b, j, per_block, per_pair):
            return b * per_block + j * per_pair

        block = ctx.enter_context(nc.Block())

        @block.sync
        def _(sp):
            def load_slab(s, src, b=0, j=0):
                if s >= RAW:
                    sp.wait_ge(wlo if SPLIT else job_done, 2 * (s - RAW) + 2 + per_body(b, j, JOBS_PER_BLOCK, 8))
                sp.dma_start(raw[:, s % RAW], src).then_inc(loaded[s % RAW], 16)

            def load_static(name, count):
                s0 = pl.base[name][0] // 2
                for s in range(s0, s0 + count):
                    load_slab(s, static_slab(s))

            def load_ffn(name):
                s0 = pl.base[name][0] // 2
                gate, up = (w2[f"{name}_w_{x}"].rearrange("(t p) c -> p t c", p=P) for x in ("gate", "up"))
                down = w2[f"{name}_w_down"].rearrange("(b t p) c -> p b t c", p=P, t=KT)
                with sp.Fori(0, BLOCKS) as b:
                    with sp.Fori(0, 2) as j:
                        for i in range(4):
                            w = up if i % 2 else gate
                            load_slab(s0 + i, w[:, :, ds(b * D + j * 512 + 256 * (i // 2), 256)], b, j)
                    for i in range(4):
                        src = down[:, ds(b, 1), :, 256 * i:256 * i + 256].rearrange("p o t c -> p (o t) c")
                        load_slab(s0 + 8 + i, src, b)

            sp.dma_start(memraw[:, :, :], a["mem_prompt"].rearrange("b (t p) d -> p (b t) d", p=P)).then_inc(ld_mem, 16)
            for i in range(2):
                sp.dma_start(xin[:, 2 * i:2 * i + 2], x_p[256 * i:256 * i + 256, :].rearrange("(t p) d -> p t d", p=P))\
                    .then_inc(ld_x[i], 16)
            sp.dma_start(xin[0:NB * DEC, 4], x_s).then_inc(ld_xs, 16)
            load_static("k", 8)
            load_ffn("ffn1")
            load_static("glu0", 20)
            load_ffn("ffn2")
            for i in range(TT):
                m = token_tile(i)[1]
                wait_freed(sp, f"y{i}")
                dst = y_sample.rearrange("b s d -> (b s) d") if i == 4 else y_prompt[0, i * P:(i + 1) * P, :]
                sp.dma_start(dst, ytok[0:m, i % 3]).then_inc(y_stored[i % 3], 16)
            for i in range(3):
                sp.wait_ge(y_stored[i], 16 * len(range(i, TT, 3)))
            sp.wait_ge(stored, 16 * 7)

        @block.gpsimd
        def _(pool):
            nc.gpsimd.memset(ident[:, :], 0.0).then_inc(id_set, 1)
            nc.gpsimd.memset(ones[:, :], 1.0).then_inc(const_set, 1)
            nc.gpsimd.memset(epst[:, 1:2], 4.0 * EPS).then_inc(eps_set, 1)
            nc.gpsimd.memset(epst[:, 0:1], EPS).then_inc(eps_set, 1)
            nc.gpsimd.memset(bd[:, :, :], 0.0).then_inc(bd_zero, 1)
            pool.wait_ge(id_set, 1)
            nc.gpsimd.affine_select(out=ident[:, :], in_=ident[:, :], compare_op=ALU.not_equal, fill=1.0, base=0,
                                    pattern=[[-1, P]], channel_multiplier=1).then_inc(id_set, 1)
            pool.wait_ge(ld_ws, 16)
            nc.gpsimd.affine_select(out=wsr[:, :, :], in_=wsr[:, :, :], compare_op=ALU.is_ge, fill=0.0, base=0,
                                    pattern=[[0, 4], [-1, P]], channel_multiplier=1).then_inc(masked, 1)
            wait_freed(pool, "spatial")
            pool.wait_ge(bd_zero, 1)
            for b in range(NB):
                o = slice(b * DEC, (b + 1) * DEC)
                pool.dma_start(bd[o, :, o], wsT[0:DEC, :, 0:DEC]).then_inc(ld_bd, 16)
            wait_freed(pool, "ktok1")
            pool.dma_start(mem_k_o.rearrange("l b (t p) h d -> p (l b t) (h d)", p=P), ktok[:, :, :]).then_inc(stored, 16)
            wait_freed(pool, "vtok1")
            pool.dma_start(mem_v_o.rearrange("l b (t p) h d -> p (l b t) (h d)", p=P), vtok[:, :, :]).then_inc(stored, 16)
            pool.wait_ge(stored, 32)
            nc.gpsimd.memset(f[:, :, :], 0.0).then_inc(f_zero, 1)
            nc.gpsimd.memset(glu[:, :, 0:LEFT], 0.0).then_inc(glu_zero, 1)
            pool.wait_ge(job_done, pl.base["glu0"][0])
            pool.dma_start(straw[:, :, :], a["state_conv"].rearrange("l (g b) k c -> (b k) (l g) c", g=2)).then_inc(ld_st, 16)
            pool.dma_start(lng[:, :], a["sgu_ln_g"].partition_broadcast(P).rearrange("p l c -> p (l c)")).then_inc(ld_ln, 16)
            pool.dma_start(lnb[:, :], a["sgu_ln_b"].partition_broadcast(P).rearrange("p l c -> p (l c)")).then_inc(ld_ln, 16)
            pool.dma_start(cs_s[0, :, 0:LEFT - DEC, :], a["state_conv"][0, :, DEC:LEFT, :]).then_inc(stored, 16)
            pool.wait_ge(ld_ln, 32)
            for i in range(TT):
                m = token_tile(i)[1]
                pool.wait_ge(sv_n, i + 1)
                nc.gpsimd.tensor_tensor(sv[0:m, i], sv[0:m, i], lng[0:m, :], ALU.mult).then_inc(sv_g, 1)
                pool.wait_ge(sv_g, i + 1)
                nc.gpsimd.tensor_tensor(sv[0:m, i], sv[0:m, i], lnb[0:m, :], ALU.add).then_inc(sv_b, 1)
            pool.wait_ge(sv_b, TT)
            pool.dma_start(cv_p[0, 0, :, :], sv[:, 3]).then_inc(stored, 16)
            pool.dma_start(cv_s.rearrange("l b s c -> (l b s) c"), sv[0:NB * DEC, 4]).then_inc(stored, 16)
            wait_freed(pool, "glup")
            pool.dma_start(cs_p[0, 0, :, :], osm[64:64 + LEFT, :]).then_inc(stored, 16)
            wait_freed(pool, "glus")
            pool.dma_start(cs_s[0, :, LEFT - DEC:LEFT, :], osm[0:NB * DEC, :]).then_inc(stored, 16)
            pool.wait_ge(stored, 16 * 7)
            for b in range(NB):
                if b < 3:
                    pool.wait_ge(job_done, pl.base["out"][0] + 1)
                elif b == 3:
                    pool.wait_ge(job_done, pl.base["out"][0] + 8)
                else:
                    wait_aux(pool, f"ktb{b - 4}")
                dst = kring[:, b % 4] if b % 4 < 3 else k3[:, :, :]
                pool.dma_start(dst, ck[b].rearrange("(t p) d -> p t d", p=P)).then_inc(ld_k[b % 4], 16)
            for b in range(NB):
                if b < 3:
                    wait_aux(pool, f"ktb{4 + b}")
                elif b < 5:
                    wait_aux(pool, f"ss{3 + b}")
                else:
                    pool.wait_ge(vs_used, b - 5 + 1)
                dst = vx[:, b - 3] if 3 <= b < 5 else kring[:, b % 5]
                pool.dma_start(dst, cv[b].rearrange("(t p) d -> p t d", p=P)).then_inc(ld_v[b % 5], 16)
            pool.wait_ge(sums["post3"]["done"], KT)
            if SPLIT:
                pass
            nc.gpsimd.memset(f[:, :, :], 0.0).then_inc(f_zero, 1)

        @block.scalar
        def _(act):
            def prepare(J, b=0, j=0):
                if not SPLIT or (isinstance(b, int) and J + JOBS_PER_BLOCK * b >= pl.jobs):
                    return
                s = J // 2
                act.wait_ge(loaded[s % RAW], 16 * (s // RAW + 1) + per_body(b, j, 16 * 12 // RAW, 16 * 4 // RAW))
                if J >= 2:
                    act.wait_ge(job_done, J - 1 + per_body(b, j, JOBS_PER_BLOCK, 8))
                nc.scalar.activation(wp[:, J % 2, 0], raw[:, s % RAW, :, (J % 2) * P:(J % 2 + 1) * P], ACT.Copy)\
                    .then_inc(whi, 1)

            def copy_job(name, i, dst, cols=None, scale=1.0):
                J, u = pl.base[name][0] + i, pl.base[name][1] + i
                prepare(J + 1)
                act.wait_ge(job_done, J + 1)
                src = slot(u)[:, 0, 0:cols] if cols else slot(u)[:, :, 0:HALF]
                free(nc.scalar.activation(dst if cols else halves(dst), src, ACT.Copy, scale=scale), u)

            def squares(name, src, ready):
                for t in range(KT):
                    ready(t)
                    if t >= 2:
                        act.wait_ge(sums[name]["summed"], t - 1)
                    nc.scalar.activation(sq[:, t % 2], src(t), ACT.Square).then_inc(sums[name]["squared"], 1)

            def root(name, n_features, half=False):
                k = 4.0 if half else 1.0
                wait_aux(act, name)
                free_aux(nc.scalar.activation(halves(R[:, :]), aux(name)[:, :, 0:HALF], ACT.Sqrt, scale=k / n_features,
                                              bias=epst4[:, 0:1] if half else epst[:, 0:1]), name)

            def norm_high(name, tiles=range(KT)):
                for t in tiles if SPLIT else ():
                    act.wait_ge(sums[name]["scaled"], t + 1)
                    nc.scalar.activation(n[:, 0, t], sil[:, t % 2], ACT.Copy).then_inc(sums[name]["hi"], 1)

            def gate_pair(name, i, func, b=0, j=0, after=None):
                J, u = pl.base[name][0] + i, pl.base[name][1] + i
                for e in range(2):
                    prepare(J + e + 1, b, j)
                    act.wait_ge(job_done, J + e + 1 + per_body(b, j, JOBS_PER_BLOCK, 8))
                    before_u = u + 2 + e - 4
                    if SPLIT:
                        act.wait_ge(mid_ready, MID0[name] + i // 2 + e - 1 + per_body(b, j, KT, 4))
                    elif after is None:
                        act.wait_ge(slot_free[before_u % 4], before_u // 4 + 1 + per_body(b, j, 6, 2))
                    free(nc.scalar.activation(halves(sil[:, e]), slot(u + e)[:, :, 0:HALF], func), u + e)

            def ffn(name):
                J0 = pl.base[name][0]

                def blk(b):
                    with act.Fori(0, 2) as j:
                        for i in (0, 4):
                            gate_pair(name, i, ACT.Silu, b, j)
                            for e in range(2):
                                prepare(J0 + i + 2 + e + 1, b, j)
                                if SPLIT:
                                    vu = pl.base[name][1] + i + 2 + e
                                    act.wait_ge(slot_free[vu % 4], vu // 4 + 1 + per_body(b, j, 6, 2))
                                    nc.scalar.activation(mid[:, 0, ds(j * 4 + (i // 2 + e), 1)].rearrange("p o t -> p (o t)"),
                                                         sil[:, e], ACT.Copy).then_inc(mid_hi, 1)
                    for i in range(KT):
                        prepare(J0 + 16 + i + 1, b)
                peel = SPLIT and name == "ffn2"
                with act.Fori(0, BLOCKS - peel) as b:
                    blk(b)
                if peel:
                    blk(BLOCKS - 1)

            act.dma_start(wsr[:, :, :], a["sgu_w_s"].rearrange("l h i j -> i (l h) j")).then_inc(ld_ws, 16)
            for k, name in enumerate(GAINS):
                act.dma_start(graw[8 * k:8 * k + 8, :], a[name].rearrange("l (t p) -> (l t) p", p=P)).then_inc(ld_small, 16)
            for k, name in enumerate(("conv_b", "conv_ln_g", "conv_ln_b")):
                o = CV0 + 4 * k
                act.dma_start(graw[o:o + 4, :], a[name].rearrange("l (t p) -> (l t) p", p=P)).then_inc(ld_small, 16)
            act.dma_start(cwraw[:, :], a["conv_w"].rearrange("l k c -> (l k) c")).then_inc(ld_cw, 16)
            act.dma_start(bsb[:, :, :], a["sgu_b_s"].partition_broadcast(P).rearrange("p l h i -> p (l h) i")).then_inc(ld_bs, 16)
            wait_aux(act, "gains")
            free_aux(nc.scalar.activation(gvec[:, :], aux("gains")[:, 0, 0:84], ACT.Copy), "gains")
            wait_aux(act, "convw")
            free_aux(nc.scalar.activation(convw[:, :, 0:TAPS], eight(aux("convw"))[:, 0:CT, 0:TAPS], ACT.Copy), "convw")
            wait_aux(act, "spatial")
            free_aux(nc.scalar.activation(wsT[:, :, :], eight(aux("spatial"))[:, 0:4, :], ACT.Copy), "spatial")
            act.wait_ge(ld_mem, 16)
            act.wait_ge(eps_set, 2)
            for t in range(MT):
                if t:
                    act.wait_ge(mem_sq, t)
                nc.scalar.activation(memjunk, memraw[:, t], ACT.Square, accum_out=mss[:, t:t + 1]).then_inc(mem_sq, 1)
            act.wait_ge(mem_sq, MT)
            nc.scalar.activation(mss, mss, ACT.Sqrt, scale=1.0 / D, bias=epst[:, 0:1]).then_inc(mem_rt, 1)
            if SPLIT:
                for t in range(MT):
                    wait_freed(act, f"mem{t}")
                    nc.scalar.activation(memT[:, 0, :, t * P:(t + 1) * P], memF[:, :, t * P:(t + 1) * P], ACT.Copy)\
                        .then_inc(memhi, 1)
            prepare(0)
            for i in range(TT):
                o, m = token_tile(i)
                wait_aux(act, f"x{i}")
                free_aux(nc.scalar.activation(h[:, :, o:o + m], eight(aux(f"x{i}"))[:, :, 0:m], ACT.Copy), f"x{i}")
            for t in range(6):
                copy_job("k", t, kT[:, t], MEM)

            def h_turned(t):
                if t == 0:
                    for i in range(TT):
                        wait_freed(act, f"x{i}")
            h_turned(0)
            for t in range(2):
                nc.scalar.activation(sq[:, t], h[:, t], ACT.Square).then_inc(sums["pre1"]["squared"], 1)
            for t in range(6, 8):
                copy_job("k", t, kT[:, t], MEM)
            for t in range(2, KT):
                act.wait_ge(sums["pre1"]["summed"], t - 1)
                nc.scalar.activation(sq[:, t % 2], h[:, t], ACT.Square).then_inc(sums["pre1"]["squared"], 1)
            root("pre1", D)
            for t in range(KT):
                copy_job("v", t, vT[:, t], MEM)
                norm_high("pre1", [t])
            ffn("ffn1")

            def down_added(name):
                def wait(t):
                    wait_use_freed(act, pl.base[name][1] + (BLOCKS - 1) * JOBS_PER_BLOCK + 16 + t)
                return wait

            def applied(name):
                def wait(t):
                    act.wait_ge(sums[name]["done"], t + 1)
                return wait

            squares("post1", lambda t: f[:, t], down_added("ffn1"))
            root("post1", D, half=True)
            squares("pre2", lambda t: h[:, t], applied("post1"))
            root("pre2", D)
            norm_high("pre2")
            for r in range(2):
                wait_aux(act, f"state{r}")
                if r == 0:
                    act.wait_ge(glu_zero, 1)
                for ct in range(CT):
                    dst = glu[:, ct, GLU_S + 38 * 4 * r:GLU_S + 38 * 4 * (r + 1)].rearrange("p (b k) -> p b k", b=4)[:, :, 0:LEFT]
                    src = aux(f"state{r}")[:, 0, ct * P:ct * P + 120].rearrange("p (b k) -> p b k", b=4)
                    ins = nc.scalar.activation(dst, src, ACT.Copy)
                free_aux(ins, f"state{r}")
            act.wait_ge(sums["pre2"]["done"], KT)
            for g in range(2):
                name = f"glu{g}"
                J, u = pl.base[name]
                for e in range(2):
                    prepare(J + e + 1)
                    act.wait_ge(job_done, J + e + 1)
                    if g:
                        wait_use_freed(act, pl.base["glu0"][1] + 2 + e)
                    free(nc.scalar.activation(halves(sil[:, e]), slot(u + e)[:, :, 0:HALF], ACT.Sigmoid), u + e)
                for e in range(2):
                    prepare(J + e + 3)
            def v_turned(t):
                wait_aux(act, f"vt{t}")
                src = flat(aux(f"vt{t}"))
                nc.scalar.activation(sv[:, 0:4, t * P:(t + 1) * P], src[:, 0:512].rearrange("p (t c) -> p t c", c=P), ACT.Copy)
                free_aux(nc.scalar.activation(sv[0:NB * DEC, 4, t * P:(t + 1) * P], src[0:NB * DEC, 512:640], ACT.Copy), f"vt{t}")

            for t in range(4):
                if t >= 2:
                    wait_aux(act, f"vt{t - 2}")
                copy_job(f"sv{t}", 0, sq[:, t % 2])
                if t:
                    v_turned(t - 1)
            copy_job("u0", 0, f[:, 0])
            v_turned(3)
            act.wait_ge(sv_mv, TT)
            nc.scalar.activation(vrs[:, 0:4], bag[:, 1:8:2], ACT.Sqrt, bias=epst[:, 0:1])
            nc.scalar.activation(vrs[0:64, 4:5], bag[0:64, 9:10], ACT.Sqrt, bias=epst[0:64, 0:1]).then_inc(sv_rt, 1)
            for t in range(1, 4):
                copy_job(f"u{t}", 0, f[:, t])
            if SPLIT:
                for t in range(4):
                    act.wait_ge(gated, t + 1)
                    nc.scalar.activation(mid[:, 0, t], sil[:, t % 2], ACT.Copy).then_inc(mid_hi, 1)
            for e in range(2, 4):
                wait_use_freed(act, pl.base["glu1"][1] + e)
            for ct in range(CT):
                src = glu[:, ct, GLU_S:GLU_W].rearrange("p (b k) -> p b k", b=NB)[:, :, LEFT:LEFT + DEC]
                ins = nc.scalar.activation(gsm[:, ct].rearrange("p (b k) -> p b k", b=NB), src, ACT.Copy)
            ins.then_inc(gs_ready, 1)
            wait_aux(act, "glup")
            free_aux(nc.scalar.activation(osm[64:64 + LEFT, :], aux("glup")[0:LEFT, 0, :], ACT.Copy), "glup")
            wait_aux(act, "glus")
            free_aux(nc.scalar.activation(osm[0:NB * DEC, :], aux("glus")[0:NB * DEC, 0, :], ACT.Copy), "glus")
            for t in range(CT):
                if t < CT - 1:
                    act.wait_ge(cc_ready, t + 1)
                else:
                    wait_freed(act, "cmean")
                if t >= 2:
                    act.wait_ge(sums["cvar"]["summed"], t - 1)
                nc.scalar.activation(sq[:, t % 2], f[:, 4 + t], ACT.Square).then_inc(sums["cvar"]["squared"], 1)
            root("cvar", CW)
            for t in range(CT):
                act.wait_ge(cn_ready, t + 1)
                dst = f[:, 4 + t] if SPLIT else mid[:, 0, 4 + t]
                nc.scalar.activation(dst, f[:, 4 + t], ACT.Silu, scale=clg[t], bias=clb[t]).then_inc(act_b, 1)
            for t in range(CT if SPLIT else 0):
                act.wait_ge(act_b, t + 1)
                nc.scalar.activation(mid[:, 0, 4 + t], f[:, 4 + t], ACT.Copy).then_inc(mid_hi, 1)

            def project_and_norm(job, post, pre):
                for t in range(KT):
                    copy_job(job, t, f[:, t])

                def copied(t):
                    wait_use_freed(act, pl.base[job][1] + t)
                squares(post, lambda t: f[:, t], copied)
                root(post, D)
                squares(pre, lambda t: h[:, t], applied(post))
                root(pre, D)
                norm_high(pre)

            project_and_norm("out", "post2", "pre3")
            for t in range(KT):
                copy_job("q", t, f[:, t], scale=float(D // HEADS) ** -0.5)

            def keys_turned(b):
                wait_aux(act, f"kta{b}")
                free_aux(nc.scalar.activation(kts[:, b % 2, :, 0:P], eight(aux(f"kta{b}")), ACT.Copy), f"kta{b}")

            def probs_turned(i):
                wait_aux(act, f"pt{i}")
                free_aux(nc.scalar.activation(pT[:, :, i * P:(i + 1) * P], eight(aux(f"pt{i}")), ACT.Copy), f"pt{i}")

            for i in range(4):
                act.wait_ge(mx_ready, i + 1)
                if i >= 2:
                    wait_aux(act, f"pt{i - 2}")
                for hd in range(HEADS):
                    ins = nc.scalar.activation(prob[:, i % 2, hd], aux(f"sc{i}")[:, hd // 2, (hd % 2) * MEM:(hd % 2 + 1) * MEM],
                                               ACT.Exp, bias=mx[:, 4 * i + hd:4 * i + hd + 1],
                                               accum_out=sm[:, 4 * i + hd:4 * i + hd + 1])
                free_aux(ins, f"sc{i}")
                for b in (2 * i, 2 * i + 1):
                    if b >= 2:
                        wait_aux(act, f"ss{b - 2}")
                    keys_turned(b)
                if i:
                    probs_turned(i - 1)
            probs_turned(3)

            def out_high(o):
                wait_aux(act, f"pv{o}")
                ins = nc.scalar.activation(mid[:, 0, o, 0:SEQ], aux(f"pv{o}")[:, 0, :], ACT.Copy)
                if SPLIT:
                    ins.then_inc(mid_hi, 1)
                else:
                    free_aux(ins, f"pv{o}")

            act.wait_ge(smx_ready, 1)
            for r in range(2):
                ins = nc.scalar.activation(psm[:, r], aux("sroll")[:, r, 0:MEM], ACT.Exp, bias=smx[:, r:r + 1],
                                           accum_out=ssm[:, r:r + 1])
            free_aux(ins, "sroll")
            out_high(0)
            out_high(1)
            wait_aux(act, "sprob")
            free_aux(nc.scalar.activation(pTs[:, :, :], aux("sprob")[:, :, 0:MEM], ACT.Copy), "sprob")
            for o in range(2, 8):
                out_high(o)
            wait_aux(act, "pvs")
            ins = nc.scalar.activation(mid[:, 0, :, SEQ:T], aux("pvs")[:, 0, :].rearrange("p (o t) -> p o t", o=KT), ACT.Copy)
            if SPLIT:
                ins.then_inc(mid_hi, 1)
            else:
                free_aux(ins, "pvs")
            project_and_norm("o", "post3", "pre4")
            ffn("ffn2")
            squares("post4", lambda t: f[:, t], down_added("ffn2"))
            root("post4", D, half=True)
            for i in range(TT):
                m = token_tile(i)[1]
                wait_aux(act, f"y{i}")
                if i >= 3:
                    act.wait_ge(y_stored[i % 3], 16)
                free_aux(nc.scalar.activation(ytok[0:m, i % 3], flat(aux(f"y{i}"))[0:m, :], ACT.Copy), f"y{i}")

        @block.vector
        def _(dve):
            V = nc.vector

            def prepare(J, b=0, j=0):
                if not SPLIT or (isinstance(b, int) and J + JOBS_PER_BLOCK * b >= pl.jobs):
                    return
                s = J // 2
                dve.wait_ge(whi, J + 1 + per_body(b, j, JOBS_PER_BLOCK, 8))
                V.tensor_tensor(wp[:, J % 2, 1], raw[:, s % RAW, :, (J % 2) * P:(J % 2 + 1) * P],
                                wp[:, J % 2, 0].bitcast(F32), ALU.subtract).then_inc(wlo, 1)

            def prepare_run(name, count):
                for i in range(count):
                    prepare(pl.base[name][0] + i + 1)

            def reciprocal(name):
                wait_freed(dve, name)
                V.reciprocal(R[:, :], R[:, :]).then_inc(sums[name]["recip"], 1)
                dve.wait_ge(sums[name]["recip"], 1)

            def post_norm(name, g):
                reciprocal(name)
                for t in range(KT + 1):
                    if t < KT:
                        V.scalar_tensor_tensor(out=f[:, t], in0=f[:, t], scalar=gain[g][t], in1=R[:, :],
                                               op0=ALU.mult, op1=ALU.mult).then_inc(sums[name]["scaled"], 1)
                    if t:
                        dve.wait_ge(sums[name]["scaled"], t)
                        V.tensor_tensor(h[:, t - 1], h[:, t - 1], f[:, t - 1], ALU.add).then_inc(sums[name]["done"], 1)

            def pre_norm(name, g, beside=None):
                reciprocal(name)
                s = sums[name]
                for t in range(KT):
                    if beside:
                        prepare(pl.base[beside][0] + t + 1)
                    if not SPLIT:
                        V.scalar_tensor_tensor(out=n[:, 0, t], in0=h[:, t], scalar=gain[g][t], in1=R[:, :],
                                               op0=ALU.mult, op1=ALU.mult).then_inc(s["done"], 1)
                        continue
                    if t >= 2:
                        dve.wait_ge(s["done"], t - 1)
                    V.scalar_tensor_tensor(out=sil[:, t % 2], in0=h[:, t], scalar=gain[g][t], in1=R[:, :],
                                           op0=ALU.mult, op1=ALU.mult).then_inc(s["scaled"], 1)
                    if t:
                        norm_low(s, t - 1)
                if SPLIT:
                    norm_low(s, KT - 1)

            def norm_low(s, t):
                dve.wait_ge(s["hi"], t + 1)
                V.tensor_tensor(n[:, 1, t], sil[:, t % 2], n[:, 0, t].bitcast(F32), ALU.subtract).then_inc(s["done"], 1)

            def ffn(name):
                J0, u0 = pl.base[name]

                def blk(b):
                    with dve.Fori(0, 2) as j:
                        for i in (0, 4):
                            for e in range(2):
                                prepare(J0 + i + e + 1, b, j)
                            for e in range(2):
                                prepare(J0 + i + 2 + e + 1, b, j)
                                J, u = J0 + i + 2 + e, u0 + i + 2 + e
                                tile = ds(j * 4 + (i // 2 + e), 1)
                                gu = u0 + i + e
                                dve.wait_ge(slot_free[gu % 4], gu // 4 + 1 + per_body(b, j, 6, 2))
                                dve.wait_ge(job_done, J + 1 + per_body(b, j, JOBS_PER_BLOCK, 8))
                                if SPLIT:
                                    free(V.tensor_tensor(halves(sil[:, e]), slot(u)[:, :, 0:HALF], halves(sil[:, e]), ALU.mult), u)
                                    dve.wait_ge(mid_hi, HI0[name] + i // 2 + e + 1 + per_body(b, j, KT, 4))
                                    V.tensor_tensor(mid[:, 1, tile].rearrange("p o t -> p (o t)"), sil[:, e],
                                                    mid[:, 0, tile].rearrange("p o t -> p (o t)").bitcast(F32), ALU.subtract).then_inc(mid_ready, 1)
                                else:
                                    dst = mid[:, 0, tile, :].rearrange("p o (a c) -> p (o a) c", a=2)
                                    free(V.tensor_tensor(dst, slot(u)[:, :, 0:HALF], halves(sil[:, e]), ALU.mult), u)
                    for i in range(KT):
                        J, u = J0 + 16 + i, u0 + 16 + i
                        prepare(J + 1, b)
                        dve.wait_ge(job_done, J + 1 + per_body(b, 0, JOBS_PER_BLOCK, 8))
                        dve.wait_ge(slot_free[(u0 + 15) % 4], (u0 + 15) // 4 + 1 + per_body(b, 0, 6, 2))
                        free(V.tensor_tensor(halves(f[:, i]), slot(u)[:, :, 0:HALF], halves(f[:, i]), ALU.add), u)
                peel = SPLIT and name == "ffn2"
                with dve.Fori(0, BLOCKS - peel) as b:
                    blk(b)
                if peel:
                    blk(BLOCKS - 1)

            dve.wait_ge(mem_rt, 1)
            V.reciprocal(mss, mss).then_inc(mem_rs, 1)
            dve.wait_ge(mem_rs, 1)
            for t in range(MT):
                V.tensor_scalar(memraw[:, t], memraw[:, t], mss[:, t:t + 1], None, ALU.mult).then_inc(mem_n, 1)
            wait_freed(dve, "gains")
            for t in range(MT):
                wait_aux(dve, f"mem{t}")
                dst = (memF if SPLIT else memT[:, 0])[:, :, t * P:(t + 1) * P]
                free_aux(V.tensor_tensor(dst, eight(aux(f"mem{t}")), gvec[:, 32:40].unsqueeze(2).to_broadcast([P, KT, P]),
                                         ALU.mult), f"mem{t}")
            if SPLIT:
                for t in range(MT):
                    c = slice(t * P, (t + 1) * P)
                    dve.wait_ge(memhi, t + 1)
                    V.tensor_tensor(memT[:, 1, :, c], memF[:, :, c], memT[:, 0, :, c].bitcast(F32), ALU.subtract)\
                        .then_inc(mid_ready, 1)
            prepare(0)
            prepare_run("k", 8)
            pre_norm("pre1", "ffn1_g_pre", beside="v")
            for name, dst in (("ktok", ktok), ("vtok", vtok)):
                for t in range(MT):
                    wait_aux(dve, f"{name}{t}")
                    free_aux(V.tensor_copy(dst[:, t], flat(aux(f"{name}{t}"))), f"{name}{t}")
            dve.wait_ge(f_zero, 1)
            ffn("ffn1")
            wait_use_freed(dve, pl.base["ffn1"][1] + BLOCKS * JOBS_PER_BLOCK - 1)
            post_norm("post1", "ffn1_g_post")
            dve.wait_ge(sums["post1"]["done"], KT)
            pre_norm("pre2", "mix_g_pre")

            def glu_pair(g):
                J, u = pl.base[f"glu{g}"]
                for e in range(4 if g == 0 else 0):
                    prepare(J + e + 1)
                for e in range(2):
                    ct = 2 * g + e
                    src = slot(u + 2 + e)
                    wait_use_freed(dve, u + e)
                    dve.wait_ge(job_done, J + 2 + e + 1)
                    V.tensor_tensor(glu[:, ct, LEFT:LEFT + HALF], src[:, 0, 0:HALF], sil[:, e, 0:HALF], ALU.mult)
                    rest = SEQ - HALF
                    V.tensor_tensor(glu[:, ct, LEFT + HALF:LEFT + SEQ], src[:, 1, 0:rest], sil[:, e, HALF:SEQ], ALU.mult)
                    dst = glu[:, ct, GLU_S:GLU_W].rearrange("p (b k) -> p b k", b=NB)[:, :, LEFT:LEFT + DEC]
                    free(V.tensor_tensor(dst, src[:, 1, rest:HALF].rearrange("p (b k) -> p b k", b=NB),
                                         sil[:, e, SEQ:T].rearrange("p (b k) -> p b k", b=NB), ALU.mult), u + 2 + e)

            def conv(ct):
                first = pl.base["glu1"][0] + 1 + 4 * ct
                wait_use_freed(dve, pl.base[f"glu{ct // 2}"][1] + 2 + ct % 2)
                samples = glu[:, ct, GLU_S:GLU_W].rearrange("p (b k) -> p b k", b=NB)
                for k in range(TAPS):
                    if ct < 3 and k % 8 == 4:
                        prepare(first + k // 8)
                    done = 2 * (ct * TAPS + k)
                    w = convw[:, ct, k:k + 1]
                    ps_ = [(f[:, 4 + ct, 0:SEQ], glu[:, ct, k:k + SEQ]),
                           (f[:, 4 + ct, SEQ:T].rearrange("p (b k) -> p b k", b=NB), samples[:, :, k:k + DEC])]
                    for e, (dst, src) in enumerate(ps_):
                        if k == 0:
                            V.tensor_scalar(dst, src, w, convb[ct], ALU.mult, ALU.add).then_inc(conv_step, 1)
                        else:
                            dve.wait_ge(conv_step, done - 2 + e + 1)
                            V.scalar_tensor_tensor(out=dst, in0=src, scalar=w, in1=dst, op0=ALU.mult, op1=ALU.add)\
                                .then_inc(conv_step, 1)

            glu_pair(0)
            wait_freed(dve, "state1")
            dve.wait_ge(glu_zero, 1)
            wait_freed(dve, "convw")
            conv(0)
            glu_pair(1)
            conv(1)
            wait_freed(dve, "vt3")
            for i in range(TT):
                m = token_tile(i)[1]
                V.bn_stats(bst[0:m, 6 * i:6 * i + 6], sv[0:m, i]).then_inc(sv_st, 1)
            for i in range(TT):
                m = token_tile(i)[1]
                dve.wait_ge(sv_st, i + 1)
                V.bn_aggr(bag[0:m, 2 * i:2 * i + 2], bst[0:m, 6 * i:6 * i + 6]).then_inc(sv_mv, 1)
            dve.wait_ge(sv_rt, 1)
            V.reciprocal(vrs[:, 0:4], vrs[:, 0:4])
            V.reciprocal(vrs[0:64, 4:5], vrs[0:64, 4:5]).then_inc(sv_rs, 1)
            dve.wait_ge(sv_rs, 1)
            for i in range(TT):
                m = token_tile(i)[1]
                V.tensor_scalar(sv[0:m, i], sv[0:m, i], bag[0:m, 2 * i:2 * i + 1], vrs[0:m, i:i + 1], ALU.subtract, ALU.mult)\
                    .then_inc(sv_n, 1)
            conv(2)
            dve.wait_ge(ld_bs, 16)
            for t in range(4):
                wait_aux(dve, f"sg{t}")
                s = sil[:, t % 2]
                V.tensor_tensor(s[:, 0:SEQ].rearrange("p (c i) -> p c i", c=4), aux(f"sg{t}")[:, 0, :].rearrange("p (c i) -> p c i", c=4),
                                bsb[:, t:t + 1, :].to_broadcast([P, 4, P]), ALU.add)
                free_aux(V.tensor_tensor(s[:, SEQ:T].rearrange("p (b i) -> p b i", b=NB),
                                         aux(f"sg{t}")[:, 1, 0:NB * DEC].rearrange("p (b i) -> p b i", b=NB),
                                         bsb[:, t:t + 1, 0:DEC].to_broadcast([P, NB, DEC]), ALU.add), f"sg{t}")
                wait_freed(dve, f"sg{t}")
                if SPLIT:
                    V.tensor_tensor(s, s, f[:, t], ALU.mult).then_inc(gated, 1)
                    dve.wait_ge(mid_hi, HI0["mix"] + t + 1)
                    V.tensor_tensor(mid[:, 1, t], s, mid[:, 0, t].bitcast(F32), ALU.subtract).then_inc(mid_ready, 1)
                else:
                    if t == 0:
                        wait_use_freed(dve, pl.base["u3"][1])
                    V.tensor_tensor(mid[:, 0, t], s, f[:, t], ALU.mult).then_inc(mid_ready, 1)
            conv(3)
            wait_aux(dve, "cmean")
            for t in range(CT):
                ins = V.scalar_tensor_tensor(out=halves(f[:, 4 + t]), in0=aux("cmean")[:, :, 0:HALF], scalar=-1.0 / CW,
                                             in1=halves(f[:, 4 + t]), op0=ALU.mult, op1=ALU.add)
                if t < CT - 1:
                    ins.then_inc(cc_ready, 1)
                else:
                    free_aux(ins, "cmean")
            reciprocal("cvar")
            for t in range(CT):
                V.tensor_tensor(f[:, 4 + t], f[:, 4 + t], R[:, :], ALU.mult).then_inc(cn_ready, 1)
            for t in range(CT if SPLIT else 0):
                dve.wait_ge(mid_hi, HI0["mix"] + 4 + t + 1)
                V.tensor_tensor(mid[:, 1, 4 + t], f[:, 4 + t], mid[:, 0, 4 + t].bitcast(F32), ALU.subtract)\
                    .then_inc(mid_ready, 1)

            def project_and_norm(job, post, pre, gpost, gpre):
                prepare_run(job, 8)
                post_norm(post, gpost)
                dve.wait_ge(sums[post]["done"], KT)
                pre_norm(pre, gpre)

            project_and_norm("out", "post2", "pre3", "mix_g_post", "xattn_g_pre")
            prepare_run("q", 8)

            def keys_turned(b):
                wait_aux(dve, f"ktb{b}")
                free_aux(V.tensor_copy(kts[:, b % 2, :, P:2 * P], eight(aux(f"ktb{b}"))), f"ktb{b}")

            def sample_scores(b):
                wait_aux(dve, f"ss{b}")
                free_aux(V.tensor_copy(sT[:, :, b * 32:(b + 1) * 32], aux(f"ss{b}")[:, :, 0:32]), f"ss{b}")

            def scale_rows(i):
                c = slice(4 * i, 4 * i + 4)
                wait_freed(dve, f"sc{i}")
                V.reciprocal(sm[:, c], sm[:, c]).then_inc(rs_ready, 1)
                dve.wait_ge(rs_ready, i + 1)
                for hd in range(HEADS):
                    V.tensor_scalar(prob[:, i % 2, hd], prob[:, i % 2, hd], sm[:, 4 * i + hd:4 * i + hd + 1], None, ALU.mult)\
                        .then_inc(p_ready, 1)

            for i in range(4):
                wait_aux(dve, f"sc{i}")
                V.tensor_reduce(mx[:, 4 * i:4 * i + 4], flat(aux(f"sc{i}")).rearrange("p (h m) -> p h m", h=HEADS),
                                AX_X, ALU.max, negate=True).then_inc(mx_ready, 1)
                for b in (2 * i, 2 * i + 1):
                    if b >= 2:
                        wait_aux(dve, f"ss{b - 2}")
                    keys_turned(b)
                    if b % 2 == 0:
                        scale_rows(i)
                    if b:
                        sample_scores(b - 1)
            sample_scores(7)
            wait_aux(dve, "sroll")
            V.tensor_reduce(smx, aux("sroll")[:, :, 0:MEM], AX_X, ALU.max, negate=True).then_inc(smx_ready, 1)
            wait_freed(dve, "sroll")
            V.reciprocal(ssm, ssm).then_inc(srs_ready, 1)
            dve.wait_ge(srs_ready, 1)
            for r in range(2):
                V.tensor_scalar(psm[:, r], psm[:, r], ssm[:, r:r + 1], None, ALU.mult).then_inc(sp_ready, 1)
            if SPLIT:
                for o in range(KT):
                    dve.wait_ge(mid_hi, HI0["att"] + o + 1)
                    free_aux(V.tensor_tensor(mid[:, 1, o, 0:SEQ], aux(f"pv{o}")[:, 0, :], mid[:, 0, o, 0:SEQ].bitcast(F32),
                                             ALU.subtract), f"pv{o}")
                dve.wait_ge(mid_hi, HI0["att"] + KT + 1)
                free_aux(V.tensor_tensor(mid[:, 1, :, SEQ:T], aux("pvs")[:, 0, :].rearrange("p (o t) -> p o t", o=KT),
                                         mid[:, 0, :, SEQ:T].bitcast(F32), ALU.subtract), "pvs")
            project_and_norm("o", "post3", "pre4", "xattn_g_post", "ffn2_g_pre")
            dve.wait_ge(f_zero, 2)
            ffn("ffn2")
            wait_use_freed(dve, pl.base["ffn2"][1] + BLOCKS * JOBS_PER_BLOCK - 1)
            post_norm("post4", "ffn2_g_post")

        @block.tensor
        def _(pe):
            def job(name, i, X, need=None, b=0, j=0, cols=HALF):
                J, u = pl.base[name][0] + i, pl.base[name][1] + i
                wait_slot(pe, u, per_body(b, j, 6, 2))
                s = J // 2
                if SPLIT:
                    pe.wait_ge(wlo, J + 1 + per_body(b, j, JOBS_PER_BLOCK, 8))
                else:
                    pe.wait_ge(loaded[s % RAW], 16 * (s // RAW + 1) + per_body(b, j, 16 * 12 // RAW, 16 * 4 // RAW))
                n_half = 2 if cols == HALF else 1
                for kt in range(KT):
                    if need:
                        need(kt)
                    for k, (wi, xi) in enumerate(PRODUCTS):
                        w = wp[:, J % 2, wi, kt] if SPLIT else raw[:, s % RAW, kt, (J % 2) * P:(J % 2 + 1) * P]
                        for half in range(n_half):
                            ins = pe.matmul(slot(u)[:, half, 0:cols], w, X(xi, kt, half), start=kt == 0 and k == 0,
                                            stop=kt == KT - 1 and k == len(PRODUCTS) - 1)
                ins.then_inc(job_done, 1)

            def half_of(tile):
                return lambda part, kt, half: tile[:, part, kt, half * HALF:(half + 1) * HALF]

            def jobs(name, X, need=None, count=KT, **kw):
                for i in range(count):
                    job(name, i, X, need if i == 0 else None, **kw)

            def turn(name, tiles):
                wait_slot(pe, pl.aux[name][1])
                for dst, src in tiles:
                    m = src.shape[0]
                    ins = pe.transpose(dst, src, ident[0:m, 0:m])
                ins.then_inc(filled, 1)

            def sum_squares(name, count=KT, src=None):
                wait_slot(pe, pl.aux[name][1])
                for t in range(count):
                    if src is None:
                        pe.wait_ge(sums[name]["squared"], t + 1)
                    for half in range(2):
                        x = (src(t) if src else sq[:, t % 2])[:, half * HALF:(half + 1) * HALF]
                        ins = pe.matmul(aux(name)[:, half, 0:HALF], ones[:, :], x, start=t == 0, stop=t == count - 1)
                    if t < count - 1:
                        ins.then_inc(sums[name]["summed"], 1)
                    else:
                        ins.then_inc(filled, 1)

            def normed(name):
                return lambda kt: pe.wait_ge(sums[name]["done"], kt + 1)

            def ffn(name):
                J0, u0 = pl.base[name]
                pe.wait_ge(sums["pre1" if name == "ffn1" else "pre4"]["done"], KT)
                with pe.Fori(0, BLOCKS) as b:
                    with pe.Fori(0, 2) as j:
                        for i in range(8):
                            job(name, i, half_of(n), b=b, j=j)

                    def product_ready(kt):
                        if SPLIT:
                            pe.wait_ge(mid_ready, MID0[name] + kt + 1 + per_body(b, 0, KT, 4))
                        else:
                            i = 8 * (kt // 4) + 4 * (kt % 4 // 2) + 2 + kt % 2
                            pe.wait_ge(slot_free[(u0 + i) % 4], (u0 + i) // 4 + 1 + per_body(b, 0, 6, 2))
                    for i in range(KT):
                        job(name, 16 + i, half_of(mid), product_ready if i == 0 else None, b=b)

            pe.wait_ge(id_set, 2)
            pe.wait_ge(const_set, 1)
            pe.wait_ge(ld_small, 16 * 12)
            turn("gains", [(aux("gains")[:, 0, 0:84], graw[:, :])])
            pe.wait_ge(ld_cw, 16)
            turn("convw", [(eight(aux("convw"))[:, ct, 0:TAPS], cwraw[:, ct * P:(ct + 1) * P]) for ct in range(CT)])
            pe.wait_ge(masked, 1)
            turn("spatial", [(eight(aux("spatial"))[:, hd, :], wsr[:, hd, :]) for hd in range(4)])
            for t in range(MT):
                pe.wait_ge(mem_n, t + 1)
                turn(f"mem{t}", [(eight(aux(f"mem{t}"))[:, kt, :], memraw[:, t, kt * P:(kt + 1) * P]) for kt in range(KT)])
            for i in range(TT):
                m = token_tile(i)[1]
                if i < 4:
                    pe.wait_ge(ld_x[i // 2], 16)
                else:
                    pe.wait_ge(ld_xs, 16)
                turn(f"x{i}", [(eight(aux(f"x{i}"))[:, kt, 0:m], xin[0:m, i, kt * P:(kt + 1) * P]) for kt in range(KT)])

            def memory(part, kt, half):
                return memT[:, part, kt, :]

            def memory_ready(kt):
                if kt == 0:
                    if SPLIT:
                        pe.wait_ge(mid_ready, MT)
                    else:
                        wait_freed(pe, "mem0")
                        wait_freed(pe, "mem1")
            jobs("k", memory, memory_ready, cols=MEM)
            sum_squares("pre1")
            jobs("v", memory, cols=MEM)
            for name, src, last in (("ktok", kT, "k"), ("vtok", vT, "v")):
                for e in range(4):
                    wait_use_freed(pe, pl.base[last][1] + 4 + e)
                for t in range(MT):
                    turn(f"{name}{t}", [(eight(aux(f"{name}{t}"))[:, ft, :], src[:, ft, t * P:(t + 1) * P]) for ft in range(KT)])
            ffn("ffn1")
            sum_squares("post1")
            sum_squares("pre2")
            pe.wait_ge(ld_st, 16)
            for r in range(2):
                turn(f"state{r}", [(eight(aux(f"state{r}"))[:, ct, 0:120], straw[:, r, ct * P:(ct + 1) * P]) for ct in range(CT)])
            jobs("glu0", half_of(n), normed("pre2"), 4)
            jobs("glu1", half_of(n), None, 4)

            def turn_v(t):
                wait_use_freed(pe, pl.base[f"sv{t}"][1])
                pieces = []
                for i in range(TT):
                    o, m = token_tile(i)
                    pieces.append((flat(aux(f"vt{t}"))[0:m, i * P:(i + 1) * P], sq[:, t % 2, o:o + m]))
                turn(f"vt{t}", pieces)

            jobs("sv0", half_of(n), None, 1)
            for t in range(1, 4):
                jobs(f"sv{t}", half_of(n), None, 1)
                turn_v(t - 1)
            jobs("u0", half_of(n), None, 1)
            turn_v(3)
            for t in range(1, 4):
                jobs(f"u{t}", half_of(n), None, 1)
            pe.wait_ge(sv_b, TT)
            pe.wait_ge(ld_bd, 16 * NB)
            for hd in range(4):
                name, cols = f"sg{hd}", slice(hd * P, (hd + 1) * P)
                wait_slot(pe, pl.aux[name][1])
                for c in range(4):
                    pe.matmul(aux(name)[:, 0, c * P:(c + 1) * P], sv[:, c, cols], wsT[:, hd, :], start=True, stop=True)
                pe.matmul(aux(name)[:, 1, 0:NB * DEC], sv[0:NB * DEC, 4, cols], bd[:, hd, :], start=True, stop=True)\
                    .then_inc(filled, 1)
            for e in range(4):
                wait_use_freed(pe, pl.base["glu1"][1] + e)
            turn("glup", [(aux("glup")[0:LEFT, 0, ct * P:(ct + 1) * P], glu[:, ct, SEQ:SEQ + LEFT]) for ct in range(CT)])
            pe.wait_ge(gs_ready, 1)
            turn("glus", [(aux("glus")[0:NB * DEC, 0, ct * P:(ct + 1) * P], gsm[:, ct, :]) for ct in range(CT)])
            pe.wait_ge(conv_step, 2 * CT * TAPS)
            sum_squares("cmean", CT, lambda t: f[:, 4 + t])
            sum_squares("cvar", CT)

            def mixed(kt):
                if SPLIT:
                    pe.wait_ge(mid_ready, MID0["mix"] + kt + 1)
                elif kt < 4:
                    pe.wait_ge(mid_ready, kt + 1)
                else:
                    pe.wait_ge(act_b, kt - 3)
            jobs("out", half_of(mid), mixed)
            sum_squares("post2")
            sum_squares("pre3")
            jobs("q", half_of(n), normed("pre3"))
            for e in range(4):
                wait_use_freed(pe, pl.base["q"][1] + 4 + e)

            def sample_scores(b):
                name = f"ss{b}"
                wait_slot(pe, pl.aux[name][1])
                wait_freed(pe, f"kta{b}")
                wait_freed(pe, f"ktb{b}")
                for t in range(MT):
                    for hd in range(HEADS):
                        for d in range(2):
                            ins = pe.matmul(aux(name)[:, t, hd * DEC:(hd + 1) * DEC], kts[:, b % 2, 2 * hd + d, t * P:(t + 1) * P],
                                            f[:, 2 * hd + d, SEQ + b * DEC:SEQ + (b + 1) * DEC], start=d == 0, stop=d == 1)
                ins.then_inc(filled, 1)

            def turn_probs(i):
                pe.wait_ge(p_ready, 4 * i + 4)
                turn(f"pt{i}", [(eight(aux(f"pt{i}"))[:, 2 * hd + t, :], prob[:, i % 2, hd, t * P:(t + 1) * P])
                                for hd in range(HEADS) for t in range(MT)])

            for i in range(4):
                name = f"sc{i}"
                wait_slot(pe, pl.aux[name][1])
                for hd in range(HEADS):
                    for d in range(2):
                        ins = pe.matmul(aux(name)[:, hd // 2, (hd % 2) * MEM:(hd % 2 + 1) * MEM],
                                        f[:, 2 * hd + d, i * P:(i + 1) * P], kT[:, 2 * hd + d, :], start=d == 0, stop=d == 1)
                ins.then_inc(filled, 1)
                for b in (2 * i, 2 * i + 1):
                    pe.wait_ge(ld_k[b % 4], 16 * (b // 4 + 1))
                    keys = kring[:, b % 4] if b % 4 < 3 else k3[:, :, :]
                    for t, x in enumerate("ab"):
                        turn(f"kt{x}{b}", [(eight(aux(f"kt{x}{b}"))[:, ft, :], keys[:, t, ft * P:(ft + 1) * P]) for ft in range(KT)])
                    if b:
                        sample_scores(b - 1)
                if i:
                    turn_probs(i - 1)
            sample_scores(7)
            turn_probs(3)
            wait_freed(pe, "ss7")
            turn("sroll", [(aux("sroll")[:, r, t * P:(t + 1) * P], sT[:, t, r * P:(r + 1) * P]) for r in range(2) for t in range(MT)])

            def head_out(o):
                name = f"pv{o}"
                wait_slot(pe, pl.aux[name][1])
                for t in range(MT):
                    ins = pe.matmul(aux(name)[:, 0, :], vtok[:, t, o * P:(o + 1) * P], pT[:, o // 2 * 2 + t, :], start=t == 0, stop=t == 1)
                ins.then_inc(filled, 1)

            for i in range(4):
                wait_freed(pe, f"pt{i}")
            head_out(0)
            head_out(1)
            pe.wait_ge(sp_ready, 2)
            turn("sprob", [(aux("sprob")[:, t, r * P:(r + 1) * P], psm[:, r, t * P:(t + 1) * P]) for r in range(2) for t in range(MT)])
            for o in range(2, 8):
                head_out(o)
            wait_slot(pe, pl.aux["pvs"][1])
            wait_freed(pe, "sprob")
            for b in range(NB):
                pe.wait_ge(ld_v[b % 5], 16 * (b // 5 + 1))
                vals = vx[:, b - 3] if 3 <= b < 5 else kring[:, b % 5]
                for o in range(KT):
                    c = o * NB * DEC + b * DEC
                    p0 = b * 32 + (o // 2) * DEC
                    for t in range(MT):
                        ins = pe.matmul(aux("pvs")[:, 0, c:c + DEC], vals[:, t, o * P:(o + 1) * P], pTs[:, t, p0:p0 + DEC],
                                        start=t == 0, stop=t == 1)
                ins.then_inc(vs_used if b < NB - 1 else filled, 1)

            def attended(kt):
                wait_freed(pe, f"pv{kt}")
                if kt == 0:
                    wait_freed(pe, "pvs")
            jobs("o", half_of(mid), attended)
            sum_squares("post3")
            sum_squares("pre4")
            ffn("ffn2")
            sum_squares("post4")
            pe.wait_ge(sums["post4"]["done"], KT)
            for i in range(TT):
                o, m = token_tile(i)
                turn(f"y{i}", [(flat(aux(f"y{i}"))[0:m, kt * P:(kt + 1) * P], h[:, kt, o:o + m]) for kt in range(KT)])


_INS = ["x_prompt", "x_sample", "mem_prompt", "cache_mem_k", "cache_mem_v", "state_conv",
        "ffn1_g_pre", "ffn1_w_gate", "ffn1_w_up", "ffn1_w_down", "ffn1_g_post",
        "mix_g_pre", "mix_w_in", "sgu_ln_g", "sgu_ln_b", "sgu_w_s", "sgu_b_s",
        "conv_w", "conv_b", "conv_ln_g", "conv_ln_b", "mix_w_out", "mix_g_post",
        "mem_g", "xattn_g_pre", "xattn_w_q", "xattn_w_k", "xattn_w_v", "xattn_w_o", "xattn_g_post",
        "ffn2_g_pre", "ffn2_w_gate", "ffn2_w_up", "ffn2_w_down", "ffn2_g_post"]
_OUTS = [(1, 512, 1024), (8, 8, 1024), (1, 1, 256, 4, 256), (1, 1, 256, 4, 256), (1, 1, 30, 512), (1, 8, 30, 512),
         (1, 1, 128, 512), (1, 8, 8, 512)]


def kernel(**inputs):
    import numpy as _np
    import concourse.bacc as _bacc
    from concourse import mybir as _mybir
    from concourse.bass_utils import run_bass_kernel_spmd as _run

    nc = _bacc.Bacc("TRN2", target_bir_lowering=False, num_devices=1)
    arrays, aps = {}, {}
    for name in _INS:
        x = _np.ascontiguousarray(inputs[name])
        arrays[f"in_{name}_dram"] = x
        aps[name] = nc.dram_tensor(f"in_{name}_dram", x.shape, _mybir.dt.from_np(x.dtype), kind="ExternalInput").ap()
    outs = [nc.dram_tensor(f"out_{i}_dram", shape, _mybir.dt.float32, kind="ExternalOutput").ap()
            for i, shape in enumerate(_OUTS)]
    build(nc, aps, outs)
    r = _run(nc, [arrays], core_ids=[0])
    return tuple(r.results[0][f"out_{i}_dram"] for i in range(len(_OUTS)))
```

```python
from contextlib import ExitStack

import concourse.bass as bass
from concourse import mybir

F32 = mybir.dt.float32
F32R = mybir.dt.float32r
ACT = mybir.ActivationFunctionType
ALU = mybir.AluOpType
AX_X = mybir.AxisListType.X
ds = bass.ds

PARTS = 2
PDT = F32R
PRODUCTS = [(0, 0), (0, 1), (1, 0)]

P = 128
D = 1024
KT = D // P
FFN = 4096
SEQ = 512
NB = 8
DEC = 8
T = SEQ + NB * DEC
HALF = T // 2
BLOCKS = FFN // D
MEM = 256
MT = MEM // P
HEADS = 4
SGW = 512
CW = 512
CT = CW // P
TAPS = 31
LEFT = TAPS - 1
GLU_S = LEFT + SEQ
GLU_W = GLU_S + NB * (LEFT + DEC)
EPS = 1e-6
TT = 5
JOBS_PER_BLOCK = 3 * KT
RAW = 2


def token_tile(i):
    return i * P, (P if i < 4 else NB * DEC)


class Plan:

    def __init__(self):
        self.n = 0
        self.jobs = 0
        self.aux = {}
        self.base = {}

    def job_run(self, name, count):
        self.base[name] = (self.jobs, self.n)
        self.jobs += count
        self.n += count

    def use(self, *names):
        for name in names:
            self.aux[name] = (len(self.aux), self.n)
            self.n += 1


def make_plan():
    pl = Plan()
    pl.use("x0", "x1", "gains", "x2", "x3", "x4", "convw", "spatial", "pre1")
    pl.job_run("ffn1", BLOCKS * JOBS_PER_BLOCK)
    pl.use("post1", "pre2")
    pl.job_run("glu0", 4)
    pl.use("mem0", "mem1", "state0", "state1")
    pl.job_run("glu1", 4)
    pl.use("rcol")
    pl.job_run("sv0", 1)
    pl.job_run("sv1", 1)
    pl.use("vt0")
    pl.job_run("sv2", 1)
    pl.use("vt1")
    pl.job_run("sv3", 1)
    pl.use("vt2")
    pl.job_run("u0", 1)
    pl.use("vt3")
    pl.job_run("u1", 1)
    pl.job_run("u2", 1)
    pl.job_run("u3", 1)
    pl.job_run("k", 8)
    pl.job_run("v0", 4)
    pl.use("cmean", "sg0", "sg1")
    pl.job_run("v4", 2)
    pl.use("cvar", "sg2", "sg3")
    pl.job_run("v6", 2)
    pl.use("ktok0", "ktok1", "vtok0", "vtok1", "glup", "glus")
    pl.job_run("out", 8)
    pl.use("post2", "pre3")
    pl.job_run("q", 8)
    for i in range(4):
        pl.use(f"sc{i}")
        for b in (2 * i, 2 * i + 1):
            pl.use(f"kta{b}", f"ktb{b}")
            if b:
                pl.use(f"ss{b - 1}")
        if i:
            pl.use(f"pt{i - 1}")
    pl.use("ss7", "pt3", "sroll", "pv0", "pv1", "sprob", *[f"pv{o}" for o in range(2, 8)], "pvs")
    pl.job_run("o", 8)
    pl.use("post3", "pre4")
    pl.job_run("ffn2", BLOCKS * JOBS_PER_BLOCK)
    pl.use("post4", *[f"y{i}" for i in range(TT)])
    return pl


def build(nc, a, out):
    pl = make_plan()
    y_prompt, y_sample, mem_k_o, mem_v_o, cs_p, cs_s, cv_p, cv_s = out
    w2 = {n: a[n].rearrange("l r c -> (l r) c") for n in (
        "ffn1_w_gate", "ffn1_w_up", "ffn1_w_down", "ffn2_w_gate", "ffn2_w_up", "ffn2_w_down", "mix_w_in",
        "mix_w_out", "xattn_w_q", "xattn_w_k", "xattn_w_v", "xattn_w_o")}
    x_p = a["x_prompt"].rearrange("b s d -> (b s) d")
    x_s = a["x_sample"].rearrange("b s d -> (b s) d")
    ck = a["cache_mem_k"].rearrange("l b m h d -> (l b) m (h d)")
    cv = a["cache_mem_v"].rearrange("l b m h d -> (l b) m (h d)")

    ctx = ExitStack()
    with ctx:
        def sb(name, shape, dt=F32):
            return ctx.enter_context(nc.sbuf_tensor(name, shape, dt))

        def views(name, *tiles):
            size = 0
            found = {}
            for group in tiles:
                used = 0
                with ExitStack() as inner:
                    for n, shape, dt in group:
                        found[n] = inner.enter_context(nc.sbuf_tensor(n, shape, dt))
                        words = 1
                        for s in shape[1:]:
                            words *= s
                        used += words
                size = max(size, used)
            sb(name, [P, size])
            return found

        def sem(name):
            return ctx.enter_context(nc.semaphore(name))

        ident = sb("ident", [P, P])
        ones = sb("ones", [P, P])
        epst = sb("epst", [P, 3])
        gvec = sb("gvec", [P, 84])
        convw = sb("convw", [P, CT, TAPS + 1])
        wsT = sb("wsT", [P, 4, P])
        bd = sb("bd", [NB * DEC, 4, NB * DEC])
        bsb = sb("bsb", [P, 4, P])
        osm = sb("osm", [P, CW])
        gsm = sb("gsm", [P, CT, NB * DEC])
        small = sb("small", [P, 112])
        mx, sm = small[:, 0:16], small[:, 16:32]
        smx, ssm = small[:, 32:34], small[:, 34:36]
        mss = small[:, 36:38]
        bst, bag = small[:, 40:70], small[:, 70:80]
        vrs, rc = small[:, 80:85], small[:, 85:90]
        h = sb("h", [P, KT, T])
        kT = sb("kT", [P, KT, MEM])
        vtok = sb("vtok", [P, MT, D])
        R = sb("R", [P, T])
        acc = sb("acc", [P, T])
        raw = sb("raw", [P, RAW, KT, 256])
        wp = sb("wp", [P, 2, PARTS, KT, P], PDT)
        rn = views("region_n", [("n", [P, PARTS, KT, T], PDT)],
                   [("pT", [P, 8, SEQ], F32), ("kts", [P, 2, KT, MEM], F32)],
                   [("pT_", [P, 8, SEQ], F32), ("vx", [P, 2, MT, D], F32)],
                   [("vT", [P, KT, MEM], F32), ("ktok", [P, MT, D], F32)])
        rm = views("region_mid", [("mid", [P, PARTS, KT, T], PDT)],
                   [("prob", [P, 2, HEADS, MEM], F32), ("k3", [P, MT, D], F32)],
                   [("spare0", [P, 4, T], F32), ("lng", [P, SGW], F32), ("lnb", [P, SGW], F32), ("straw", [120, 2, CW], F32),
                    ("spare1", [P, 8 * T - 2 * SGW - 2 * CW], F32), ("memT", [P, KT, MEM], F32)])
        rf = views("region_f", [("f", [P, KT, T], F32)],                    [("wsr", [P, 4, P], F32), ("graw", [84, P], F32), ("cwraw", [TAPS, CW], F32)])
        rx = views("region_x", [("xin", [P, TT, D], F32)],
                   [("sv", [P, TT, SGW], F32), ("glu", [P, CT, GLU_W], F32)],
                   [("memraw", [P, MT, D], F32)], [("kring", [P, 3, MT, D], F32)], [("ytok", [P, TT, D], F32)])
        rt = views("region_t", [("sq", [P, 2, T], F32), ("sil", [P, 2, T], F32)],
                   [("sT", [P, MT, NB * 32], F32), ("psm", [P, 2, MEM], F32), ("pTs", [P, MT, NB * 32], F32)])
        n, pT, kts, vx, vT, ktok = (rn[k] for k in ("n", "pT", "kts", "vx", "vT", "ktok"))
        mid, prob, k3, memT = rm["mid"], rm["prob"], rm["k3"], rm["memT"]
        lng, lnb, straw = rm["lng"], rm["lnb"], rm["straw"]
        f, wsr, graw, cwraw = (rf[k] for k in ("f", "wsr", "graw", "cwraw"))
        xin, memraw, sv, glu, kring, ytok = (rx[k] for k in ("xin", "memraw", "sv", "glu", "kring", "ytok"))
        sq, sil, sT, psm, pTs = (rt[k] for k in ("sq", "sil", "sT", "psm", "pTs"))
        slots = [ctx.enter_context(nc.psum_tensor(f"slot{i}", [P, 2, 512], F32)) for i in range(4)]

        HI0 = {"ffn1": 0, "mix": KT * BLOCKS, "att": KT * BLOCKS + 8, "ffn2": KT * BLOCKS + 8 + KT + 1}
        MID0 = {"ffn1": 0, "mix": KT * BLOCKS, "ffn2": KT * BLOCKS + 8}
        GATE0 = {"ffn1": 0, "glu0": KT * BLOCKS, "glu1": KT * BLOCKS + 2, "ffn2": KT * BLOCKS + 4}
        memjunk = sq[:, :, :].rearrange("p a b -> p (a b)")[:, 0:D]
        ROOTS = {"plain": (1.0, 0), "half": (4.0, 1), "query": (float(D // HEADS), 2)}
        GAINS = ["ffn1_g_pre", "ffn1_g_post", "mix_g_pre", "mix_g_post", "mem_g", "xattn_g_pre",
                 "xattn_g_post", "ffn2_g_pre", "ffn2_g_post"]
        gain = {name: [gvec[:, 8 * i + t:8 * i + t + 1] for t in range(KT)] for i, name in enumerate(GAINS)}
        CV0 = 8 * len(GAINS)
        convb, clg, clb = ([gvec[:, CV0 + 4 * i + t:CV0 + 4 * i + t + 1] for t in range(CT)] for i in range(3))

        slot_free = [sem(f"slot_free{i}") for i in range(4)]
        job_done = sem("job_done")
        filled = sem("filled")
        loaded = [sem(f"loaded{i}") for i in range(RAW)]
        whi, wlo = sem("whi"), sem("wlo")
        ld_small, ld_cw, ld_ws, ld_bs, ld_ln, ld_st = (sem(f"ld_{x}") for x in ("small", "cw", "ws", "bs", "ln", "st"))
        ld_mem, ld_xs, ld_bd = sem("ld_mem"), sem("ld_xs"), sem("ld_bd")
        ld_x = [sem(f"ld_x{i}") for i in range(4)]
        ld_k = [sem(f"ld_k{i}") for i in range(4)]
        ld_v = [sem(f"ld_v{i}") for i in range(5)]
        id_set, const_set, masked, bd_zero, glu_zero, eps_set = (
            sem(x) for x in ("id_set", "const_set", "masked", "bd_zero", "glu_zero", "eps_set"))
        mem_sq, mem_rt, mem_rs, mem_n = (sem(x) for x in ("mem_sq", "mem_rt", "mem_rs", "mem_n"))
        gate_out, gate_scaled, kv_stored = sem("gate_out"), sem("gate_scaled"), sem("kv_stored")
        rc_ready, root_done = sem("rc_ready"), sem("root_done")
        f_zero = sem("f_zero")
        gated, mid_hi, mid_ready = sem("gated"), sem("mid_hi"), sem("mid_ready")
        sums = {}
        for s in ("pre1", "post1", "pre2", "cmean", "cvar", "post2", "pre3", "post3", "pre4", "post4"):
            parts = ["squared", "recip"] + (["added"] if s.startswith("post") else ["summed"])
            if s.startswith("post"):
                parts += ["scaled", "done"]
            if s.startswith("pre"):
                parts += ["hi", "ready"]
            sums[s] = {x: sem(f"{s}_{x}") for x in parts}
        sv_st, sv_mv, sv_rt, sv_rs, sv_n, sv_g, sv_b = (
            sem(x) for x in ("sv_st", "sv_mv", "sv_rt", "sv_rs", "sv_n", "sv_g", "sv_b"))
        conv_step, cc_ready, cn_ready, act_b = (sem(x) for x in ("conv_step", "cc_ready", "cn_ready", "act_b"))
        mx_ready, rs_ready, p_ready = sem("mx_ready"), sem("rs_ready"), sem("p_ready")
        smx_ready, srs_ready, sp_ready = sem("smx_ready"), sem("srs_ready"), sem("sp_ready")
        vs_used, gs_ready = sem("vs_used"), sem("gs_ready")
        stored, y_stored = sem("stored"), sem("y_stored")

        def slot(u):
            return slots[u % 4]

        def aux(name):
            return slot(pl.aux[name][1])

        def flat(s):
            return s[:, :, :].rearrange("p a b -> p (a b)")

        def eight(s):
            return flat(s).rearrange("p (t c) -> p t c", c=P)

        def halves(ap):
            return ap.rearrange("p (a b) -> p a b", a=2)

        def wait_aux(eng, name):
            eng.wait_ge(filled, pl.aux[name][0] + 1)

        def wait_slot(pe, u, plus=0):
            if u >= 4:
                pe.wait_ge(slot_free[u % 4], u // 4 + plus)

        def wait_use_freed(eng, u):
            eng.wait_ge(slot_free[u % 4], u // 4 + 1)

        def wait_freed(eng, name):
            wait_use_freed(eng, pl.aux[name][1])

        def free(ins, u):
            ins.then_inc(slot_free[u % 4], 1)

        def free_aux(ins, name):
            free(ins, pl.aux[name][1])

        mix_in_cols = [1536, 1024, 1792, 1280, 512, 768, 0, 256]
        between = ([("mix_w_in", c) for c in mix_in_cols]
                   + [("xattn_w_k", c * 256) for c in range(4)] + [("xattn_w_v", c * 256) for c in range(4)]
                   + [("mix_w_out", c * 256) for c in range(4)]
                   + [("xattn_w_q", c * 256) for c in range(4)] + [("xattn_w_o", c * 256) for c in range(4)])
        def static_slab(s):
            name, c = between[s - pl.base["glu0"][0] // 2]
            return w2[name].rearrange("(t p) c -> p t c", p=P)[:, :, c:c + 256]

        KV0 = pl.base["k"][0]

        def is_kv(J):
            return KV0 <= J < KV0 + 16

        def prepared(J):
            return J if J < KV0 else J - 16

        def per_body(b, j, per_block, per_pair):
            return b * per_block + j * per_pair

        block = ctx.enter_context(nc.Block())

        @block.sync
        def _(sp):
            def load_slab(s, src, b=0, j=0):
                if not (s < RAW and isinstance(b, int) and isinstance(j, int) and b + j == 0):
                    before = 2 * (s - RAW)
                    if is_kv(before):
                        sp.wait_ge(job_done, before + 2)
                    else:
                        sp.wait_ge(wlo, prepared(before) + 2 + per_body(b, j, JOBS_PER_BLOCK, 8))
                sp.dma_start(raw[:, s % RAW], src).then_inc(loaded[s % RAW], 16)

            def load_static(name, count):
                s0 = pl.base[name][0] // 2
                for s in range(s0, s0 + count):
                    load_slab(s, static_slab(s))

            def load_ffn(name):
                s0 = pl.base[name][0] // 2
                gate, up = (w2[f"{name}_w_{x}"].rearrange("(t p) c -> p t c", p=P) for x in ("gate", "up"))
                down = w2[f"{name}_w_down"].rearrange("(b t p) c -> p b t c", p=P, t=KT)

                def gate_up(b, j):
                    for i in range(4):
                        w = up if i % 2 else gate
                        load_slab(s0 + i, w[:, :, ds(b * D + j * 512 + 256 * (i // 2), 256)], b, j)

                def down_slabs(b):
                    for i in range(4):
                        src = down[:, ds(b, 1), :, 256 * i:256 * i + 256].rearrange("p o t c -> p (o t) c")
                        load_slab(s0 + 8 + i, src, b)

                gate_up(0, 0)
                if name == "ffn1":
                    for i in range(TT):
                        wait_freed(sp, f"x{i}")
                    sp.dma_start(memraw[:, :, :], a["mem_prompt"].rearrange("b (t p) d -> p (b t) d", p=P))\
                        .then_inc(ld_mem, 16)
                gate_up(0, 1)
                down_slabs(0)
                with sp.Fori(1, BLOCKS) as b:
                    with sp.Fori(0, 2) as j:
                        gate_up(b, j)
                    down_slabs(b)

            for i in range(4):
                sp.dma_start(xin[:, i], x_p[i * P:(i + 1) * P, :]).then_inc(ld_x[i], 16)
            sp.dma_start(xin[0:NB * DEC, 4], x_s).then_inc(ld_xs, 16)
            load_ffn("ffn1")
            load_static("glu0", 28)
            load_ffn("ffn2")
            for i in range(TT):
                m = token_tile(i)[1]
                wait_freed(sp, f"y{i}")
                dst = y_sample.rearrange("b s d -> (b s) d") if i == 4 else y_prompt[0, i * P:(i + 1) * P, :]
                sp.dma_start(dst, ytok[0:m, i]).then_inc(y_stored, 16)
            sp.wait_ge(y_stored, 16 * TT)
            sp.wait_ge(stored, 16 * 5)
            sp.wait_ge(kv_stored, 16 * 2)

        @block.gpsimd
        def _(pool):
            nc.gpsimd.memset(ident[:, :], 0.0).then_inc(id_set, 1)
            nc.gpsimd.memset(ones[:, :], 1.0).then_inc(const_set, 1)
            nc.gpsimd.memset(epst[:, 1:2], 4.0 * EPS).then_inc(eps_set, 1)
            nc.gpsimd.memset(epst[:, 2:3], EPS * (D // HEADS)).then_inc(eps_set, 1)
            nc.gpsimd.memset(epst[:, 0:1], EPS).then_inc(eps_set, 1)
            nc.gpsimd.memset(bd[:, :, :], 0.0).then_inc(bd_zero, 1)
            pool.wait_ge(id_set, 1)
            nc.gpsimd.affine_select(out=ident[:, :], in_=ident[:, :], compare_op=ALU.not_equal, fill=1.0, base=0,
                                    pattern=[[-1, P]], channel_multiplier=1).then_inc(id_set, 1)
            pool.wait_ge(ld_ws, 16)
            nc.gpsimd.affine_select(out=wsr[:, :, :], in_=wsr[:, :, :], compare_op=ALU.is_ge, fill=0.0, base=0,
                                    pattern=[[0, 4], [-1, P]], channel_multiplier=1).then_inc(masked, 1)
            wait_freed(pool, "spatial")
            pool.wait_ge(bd_zero, 1)
            for b in range(NB):
                o = slice(b * DEC, (b + 1) * DEC)
                pool.dma_start(bd[o, :, o], wsT[0:DEC, :, 0:DEC]).then_inc(ld_bd, 16)
            for name in ("gains", "convw", "spatial"):
                wait_freed(pool, name)
            nc.gpsimd.memset(f[:, :, :], 0.0).then_inc(f_zero, 1)
            for i in range(TT):
                wait_freed(pool, f"x{i}")
            nc.gpsimd.memset(glu[:, :, 0:LEFT], 0.0).then_inc(glu_zero, 1)
            pool.wait_ge(job_done, pl.base["glu0"][0])
            pool.dma_start(straw[:, :, :], a["state_conv"].rearrange("l (g b) k c -> (b k) (l g) c", g=2)).then_inc(ld_st, 16)
            pool.dma_start(lng[:, :], a["sgu_ln_g"].partition_broadcast(P).rearrange("p l c -> p (l c)")).then_inc(ld_ln, 16)
            pool.dma_start(lnb[:, :], a["sgu_ln_b"].partition_broadcast(P).rearrange("p l c -> p (l c)")).then_inc(ld_ln, 16)
            pool.dma_start(cs_s[0, :, 0:LEFT - DEC, :], a["state_conv"][0, :, DEC:LEFT, :]).then_inc(stored, 16)
            pool.wait_ge(ld_ln, 32)
            for i in range(TT):
                m = token_tile(i)[1]
                pool.wait_ge(sv_n, i + 1)
                nc.gpsimd.tensor_tensor(sv[0:m, i], sv[0:m, i], lng[0:m, :], ALU.mult).then_inc(sv_g, 1)
                pool.wait_ge(sv_g, i + 1)
                nc.gpsimd.tensor_tensor(sv[0:m, i], sv[0:m, i], lnb[0:m, :], ALU.add).then_inc(sv_b, 1)
            pool.wait_ge(sv_b, TT)
            pool.dma_start(cv_p[0, 0, :, :], sv[:, 3]).then_inc(stored, 16)
            pool.dma_start(cv_s.rearrange("l b s c -> (l b s) c"), sv[0:NB * DEC, 4]).then_inc(stored, 16)
            for name, dst, rows in (("ktok", mem_k_o, ktok), ("vtok", mem_v_o, vtok)):
                for t in range(MT):
                    wait_freed(pool, f"{name}{t}")
                pool.dma_start(dst.rearrange("l b (t p) h d -> p (l b t) (h d)", p=P), rows[:, :, :]).then_inc(kv_stored, 16)
            wait_freed(pool, "glup")
            pool.dma_start(cs_p[0, 0, :, :], osm[64:64 + LEFT, :]).then_inc(stored, 16)
            wait_freed(pool, "glus")
            pool.dma_start(cs_s[0, :, LEFT - DEC:LEFT, :], osm[0:NB * DEC, :]).then_inc(stored, 16)
            pool.wait_ge(stored, 16 * 5)
            for b in range(NB):
                if b < 3:
                    pool.wait_ge(job_done, pl.base["out"][0] + 1)
                elif b == 3:
                    pool.wait_ge(job_done, pl.base["out"][0] + 8)
                else:
                    wait_aux(pool, f"ktb{b - 4}")
                dst = kring[:, b % 4] if b % 4 < 3 else k3[:, :, :]
                pool.dma_start(dst, ck[b].rearrange("(t p) d -> p t d", p=P)).then_inc(ld_k[b % 4], 16)
            for b in range(NB):
                if b < 3:
                    wait_aux(pool, f"ktb{4 + b}")
                elif b < 5:
                    wait_aux(pool, f"ss{3 + b}")
                else:
                    pool.wait_ge(vs_used, b - 5 + 1)
                dst = vx[:, b - 3] if 3 <= b < 5 else kring[:, b % 5]
                pool.dma_start(dst, cv[b].rearrange("(t p) d -> p t d", p=P)).then_inc(ld_v[b % 5], 16)
            pool.wait_ge(sums["post3"]["done"], KT)
            nc.gpsimd.memset(f[:, :, :], 0.0).then_inc(f_zero, 1)

        @block.scalar
        def _(act):
            def prepare(J, b=0, j=0):
                if is_kv(J) or isinstance(b, int) and J + JOBS_PER_BLOCK * b >= pl.jobs:
                    return
                s = J // 2
                act.wait_ge(loaded[s % RAW], 16 * (s // RAW + 1) + per_body(b, j, 16 * 12 // RAW, 16 * 4 // RAW))
                if J >= 2:
                    two_before = J - 18 if is_kv(J - 2) else J - 2
                    act.wait_ge(job_done, two_before + 1 + per_body(b, j, JOBS_PER_BLOCK, 8))
                nc.scalar.activation(wp[:, J % 2, 0], raw[:, s % RAW, :, (J % 2) * P:(J % 2 + 1) * P], ACT.Copy)\
                    .then_inc(whi, 1)

            def copy_job(name, i, dst, cols=None):
                J, u = pl.base[name][0] + i, pl.base[name][1] + i
                prepare(J + 2)
                act.wait_ge(job_done, J + 1)
                src = slot(u)[:, 0, 0:cols] if cols else slot(u)[:, :, 0:HALF]
                free(nc.scalar.activation(dst if cols else halves(dst), src, ACT.Copy), u)

            def square(name, t, src):
                if t >= 2:
                    act.wait_ge(sums[name]["added"], max(t - 2, 1))
                nc.scalar.activation(sq[:, t % 2] if src.ndim == 2 else halves(sq[:, t % 2]), src, ACT.Square)\
                    .then_inc(sums[name]["squared"], 1)

            def root(name, n_features, kind="plain"):
                k, col = ROOTS[kind]
                wait_aux(act, name)
                free_aux(nc.scalar.activation(halves(R[:, :]), aux(name)[:, :, 0:HALF], ACT.Sqrt, scale=k / n_features,
                                              bias=epst[:, col:col + 1]), name)

            def warm(func):
                i = warmed[0] = warmed[0] + 1
                nc.scalar.activation(small[:, 90 + i:91 + i], epst[:, 0:1], func)

            warmed = [0]

            def pre_norm(post, pre, g, job, kind="plain"):
                for t in range(KT):
                    if post:
                        act.wait_ge(sums[post]["done"], t + 1)
                    elif t in (2, 4):
                        prepare(t // 2 - 1)
                    nc.scalar.activation(n[:, 0, t], h[:, t], ACT.Copy, scale=gain[g][t]).then_inc(sums[pre]["hi"], 1)
                    if t >= 2:
                        act.wait_ge(sums[pre]["summed"], t - 1)
                    nc.scalar.activation(sq[:, t % 2], h[:, t], ACT.Square).then_inc(sums[pre]["squared"], 1)
                prepare(pl.base[job][0] + 2)
                root(pre, D, kind)

            def gates(name, i, func, b=0, j=0, ahead=False):
                J, u = pl.base[name][0] + i, pl.base[name][1] + i
                for e in range(2):
                    if e or not ahead:
                        prepare(J + e + 2, b, j)
                    act.wait_ge(slot_free[(u + e) % 4], (u + e) // 4 + 1 + per_body(b, j, 6, 2))
                    nc.scalar.activation(sil[:, e], sil[:, e], func).then_inc(gate_out, 1)

            def ffn(name, post, beside=None):
                J0, u0 = pl.base[name]

                def gate_up(b, j, ahead=False):
                    for i in (0, 4):
                        gates(name, i, ACT.Silu, b, j, ahead and i == 0)
                        for e in range(2):
                            prepare(J0 + i + e + 4, b, j)
                            vu = u0 + i + 2 + e
                            act.wait_ge(slot_free[vu % 4], vu // 4 + 1 + per_body(b, j, 6, 2))
                            nc.scalar.activation(mid[:, 0, ds(j * 4 + (i // 2 + e), 1)].rearrange("p o t -> p (o t)"),
                                                 sil[:, e], ACT.Copy).then_inc(mid_hi, 1)

                def down(b):
                    for i in range(KT):
                        prepare(J0 + 16 + i + 2, b)

                gate_up(0, 0, True)
                gate_up(0, 1)
                if beside:
                    beside()
                down(0)
                with act.Fori(1, BLOCKS - 1) as b:
                    with act.Fori(0, 2) as j:
                        gate_up(b, j)
                    down(b)
                with act.Fori(0, 2) as j:
                    gate_up(BLOCKS - 1, j)
                for i in range(KT):
                    prepare(J0 + 16 + i + 2, BLOCKS - 1)
                    wait_use_freed(act, u0 + (BLOCKS - 1) * JOBS_PER_BLOCK + 16 + i)
                    square(post, i, f[:, i])
                    if i == 0:
                        warm(ACT.Sqrt)
                root(post, D, "half")

            act.dma_start(wsr[:, :, :], a["sgu_w_s"].rearrange("l h i j -> i (l h) j")).then_inc(ld_ws, 16)
            for k, name in enumerate(GAINS):
                act.dma_start(graw[8 * k:8 * k + 8, :], a[name].rearrange("l (t p) -> (l t) p", p=P)).then_inc(ld_small, 16)
            for k, name in enumerate(("conv_b", "conv_ln_g", "conv_ln_b")):
                o = CV0 + 4 * k
                act.dma_start(graw[o:o + 4, :], a[name].rearrange("l (t p) -> (l t) p", p=P)).then_inc(ld_small, 16)
            act.dma_start(cwraw[:, :], a["conv_w"].rearrange("l k c -> (l k) c")).then_inc(ld_cw, 16)
            act.dma_start(bsb[:, :, :], a["sgu_b_s"].partition_broadcast(P).rearrange("p l h i -> p (l h) i")).then_inc(ld_bs, 16)
            for i in range(TT):
                o, m = token_tile(i)
                if i % 2 == 0:
                    wait_aux(act, f"x{i}")
                    free_aux(nc.scalar.activation(h[:, :, o:o + m], eight(aux(f"x{i}"))[:, :, 0:m], ACT.Copy), f"x{i}")
                if i == 1:
                    wait_aux(act, "gains")
                    free_aux(nc.scalar.activation(gvec[:, :], aux("gains")[:, 0, 0:84], ACT.Copy), "gains")
            for i in (1, 3):
                wait_freed(act, f"x{i}")
            wait_freed(act, "x4")
            act.wait_ge(eps_set, 3)
            wait_aux(act, "convw")
            free_aux(nc.scalar.activation(convw[:, :, 0:TAPS], eight(aux("convw"))[:, 0:CT, 0:TAPS], ACT.Copy), "convw")
            wait_aux(act, "spatial")
            free_aux(nc.scalar.activation(wsT[:, :, :], eight(aux("spatial"))[:, 0:4, :], ACT.Copy), "spatial")
            pre_norm(None, "pre1", "ffn1_g_pre", "ffn1")

            def memory_roots():
                act.wait_ge(ld_mem, 16)
                for t in range(MT):
                    if t:
                        act.wait_ge(mem_sq, t)
                    nc.scalar.activation(memjunk, memraw[:, t], ACT.Square, accum_out=mss[:, t:t + 1]).then_inc(mem_sq, 1)
                act.wait_ge(mem_sq, MT)
                nc.scalar.activation(mss, mss, ACT.Sqrt, scale=1.0 / D, bias=epst[:, 0:1]).then_inc(mem_rt, 1)
            ffn("ffn1", "post1", memory_roots)
            pre_norm("post1", "pre2", "mix_g_pre", "glu0")
            gates("glu0", 0, ACT.Sigmoid, ahead=True)
            for e in range(2):
                prepare(pl.base["glu0"][0] + 4 + e)
            for r in range(2):
                wait_aux(act, f"state{r}")
                if r == 0:
                    act.wait_ge(glu_zero, 1)
                for ct in range(CT):
                    dst = glu[:, ct, GLU_S + 38 * 4 * r:GLU_S + 38 * 4 * (r + 1)].rearrange("p (b k) -> p b k", b=4)[:, :, 0:LEFT]
                    src = aux(f"state{r}")[:, 0, ct * P:ct * P + 120].rearrange("p (b k) -> p b k", b=4)
                    ins = nc.scalar.activation(dst, src, ACT.Copy)
                free_aux(ins, f"state{r}")
            gates("glu1", 0, ACT.Sigmoid)
            for e in range(2):
                prepare(pl.base["glu1"][0] + 4 + e)
            wait_aux(act, "rcol")
            ins = nc.scalar.activation(rc[:, 0:4].unsqueeze(2), aux("rcol")[:, 0, :].rearrange("p (t c) -> p t c", c=P)[:, :, 0:1],
                                       ACT.Copy)
            free_aux(nc.scalar.activation(rc[0:NB * DEC, 4:5], aux("rcol")[0:NB * DEC, 1, 0:1], ACT.Copy), "rcol")
            def v_turned(t):
                wait_aux(act, f"vt{t}")
                if t == 0:
                    wait_freed(act, "rcol")
                for i in range(TT):
                    m = token_tile(i)[1]
                    ins = nc.scalar.activation(sv[0:m, i, t * P:(t + 1) * P], flat(aux(f"vt{t}"))[0:m, i * P:(i + 1) * P],
                                               ACT.Copy, scale=rc[0:m, i:i + 1])
                free_aux(ins, f"vt{t}")

            for t in range(4):
                if t >= 2:
                    wait_aux(act, f"vt{t - 2}")
                copy_job(f"sv{t}", 0, sq[:, t % 2])
                if t:
                    v_turned(t - 1)
            prepare(pl.base["u0"][0] + 2)
            v_turned(3)
            for t in range(1, 4):
                prepare(pl.base[f"u{t}"][0] + 2)
            for e in range(2, 4):
                wait_use_freed(act, pl.base["glu1"][1] + e)
            for ct in range(CT):
                src = glu[:, ct, GLU_S:GLU_W].rearrange("p (b k) -> p b k", b=NB)[:, :, LEFT:LEFT + DEC]
                ins = nc.scalar.activation(gsm[:, ct].rearrange("p (b k) -> p b k", b=NB), src, ACT.Copy)
            ins.then_inc(gs_ready, 1)
            copy_job("k", 0, kT[:, 0], MEM)
            act.wait_ge(sv_mv, TT)
            nc.scalar.activation(vrs[:, 0:4], bag[:, 1:8:2], ACT.Sqrt, bias=epst[:, 0:1])
            nc.scalar.activation(vrs[0:64, 4:5], bag[0:64, 9:10], ACT.Sqrt, bias=epst[0:64, 0:1]).then_inc(sv_rt, 1)
            for t in range(1, KT):
                copy_job("k", t, kT[:, t], MEM)
            for t in range(4):
                copy_job("v0", t, vT[:, t], MEM)
            for t in range(CT):
                if t < CT - 1:
                    act.wait_ge(cc_ready, t + 1)
                else:
                    wait_freed(act, "cmean")
                if t >= 2:
                    act.wait_ge(sums["cvar"]["summed"], t - 1)
                nc.scalar.activation(sq[:, t % 2], f[:, 4 + t], ACT.Square).then_inc(sums["cvar"]["squared"], 1)
            for t in range(2):
                copy_job("v4", t, vT[:, 4 + t], MEM)
            for t in range(4):
                if t == 2:
                    root("cvar", CW)
                act.wait_ge(gated, t + 1)
                nc.scalar.activation(mid[:, 0, t], sil[:, t % 2], ACT.Copy).then_inc(mid_hi, 1)
            for t in range(2):
                copy_job("v6", t, vT[:, 6 + t], MEM)
            for t in range(CT):
                act.wait_ge(cn_ready, t + 1)
                nc.scalar.activation(f[:, 4 + t], f[:, 4 + t], ACT.Silu, scale=clg[t], bias=clb[t]).then_inc(act_b, 1)
            for t in range(CT):
                act.wait_ge(act_b, t + 1)
                nc.scalar.activation(mid[:, 0, 4 + t], f[:, 4 + t], ACT.Copy).then_inc(mid_hi, 1)
            for name, rows in (("ktok", ktok), ("vtok", vtok)):
                for t in range(MT):
                    wait_aux(act, f"{name}{t}")
                    free_aux(nc.scalar.activation(rows[:, t], flat(aux(f"{name}{t}")), ACT.Copy), f"{name}{t}")
            wait_aux(act, "glup")
            free_aux(nc.scalar.activation(osm[64:64 + LEFT, :], aux("glup")[0:LEFT, 0, :], ACT.Copy), "glup")
            wait_aux(act, "glus")
            free_aux(nc.scalar.activation(osm[0:NB * DEC, :], aux("glus")[0:NB * DEC, 0, :], ACT.Copy), "glus")

            def project(job, post):
                for t in range(KT):
                    J, u = pl.base[job][0] + t, pl.base[job][1] + t
                    prepare(J + 2)
                    act.wait_ge(job_done, J + 1)
                    square(post, t, slot(u)[:, :, 0:HALF])
                    if t == 0:
                        warm(ACT.Sqrt)
                    free(nc.scalar.activation(halves(f[:, t]), slot(u)[:, :, 0:HALF], ACT.Copy), u)
                root(post, D)

            project("out", "post2")
            act.wait_ge(kv_stored, 32)
            pre_norm("post2", "pre3", "xattn_g_pre", "q", "query")
            warm(ACT.Exp)
            for t in range(1, KT):
                prepare(pl.base["q"][0] + t + 2)

            def keys_turned(b):
                wait_aux(act, f"kta{b}")
                free_aux(nc.scalar.activation(kts[:, b % 2, :, 0:P], eight(aux(f"kta{b}")), ACT.Copy), f"kta{b}")

            def probs_turned(i):
                wait_aux(act, f"pt{i}")
                free_aux(nc.scalar.activation(pT[:, :, i * P:(i + 1) * P], eight(aux(f"pt{i}")), ACT.Copy), f"pt{i}")

            for i in range(4):
                act.wait_ge(mx_ready, i + 1)
                if i >= 2:
                    wait_aux(act, f"pt{i - 2}")
                for hd in range(HEADS):
                    ins = nc.scalar.activation(prob[:, i % 2, hd], aux(f"sc{i}")[:, hd // 2, (hd % 2) * MEM:(hd % 2 + 1) * MEM],
                                               ACT.Exp, bias=mx[:, 4 * i + hd:4 * i + hd + 1],
                                               accum_out=sm[:, 4 * i + hd:4 * i + hd + 1])
                free_aux(ins, f"sc{i}")
                for b in (2 * i, 2 * i + 1):
                    if b >= 2:
                        wait_aux(act, f"ss{b - 2}")
                    keys_turned(b)
                if i:
                    probs_turned(i - 1)
            probs_turned(3)

            def out_high(o):
                wait_aux(act, f"pv{o}")
                ins = nc.scalar.activation(mid[:, 0, o, 0:SEQ], aux(f"pv{o}")[:, 0, :], ACT.Copy)
                ins.then_inc(mid_hi, 1)

            act.wait_ge(smx_ready, 1)
            for r in range(2):
                ins = nc.scalar.activation(psm[:, r], aux("sroll")[:, r, 0:MEM], ACT.Exp, bias=smx[:, r:r + 1],
                                           accum_out=ssm[:, r:r + 1])
            free_aux(ins, "sroll")
            out_high(0)
            out_high(1)
            wait_aux(act, "sprob")
            free_aux(nc.scalar.activation(pTs[:, :, :], aux("sprob")[:, :, 0:MEM], ACT.Copy), "sprob")
            for o in range(2, 8):
                out_high(o)
            wait_aux(act, "pvs")
            ins = nc.scalar.activation(mid[:, 0, :, SEQ:T], aux("pvs")[:, 0, :].rearrange("p (o t) -> p o t", o=KT), ACT.Copy)
            ins.then_inc(mid_hi, 1)
            project("o", "post3")
            pre_norm("post3", "pre4", "ffn2_g_pre", "ffn2")
            ffn("ffn2", "post4")
            for i in (0, 2, 4):
                m = token_tile(i)[1]
                wait_aux(act, f"y{i}")
                free_aux(nc.scalar.activation(ytok[0:m, i], flat(aux(f"y{i}"))[0:m, :], ACT.Copy), f"y{i}")

        @block.vector
        def _(dve):
            V = nc.vector

            def prepare(J, b=0, j=0):
                if is_kv(J) or isinstance(b, int) and J + JOBS_PER_BLOCK * b >= pl.jobs:
                    return
                s = J // 2
                dve.wait_ge(whi, prepared(J) + 1 + per_body(b, j, JOBS_PER_BLOCK, 8))
                V.tensor_tensor(wp[:, J % 2, 1], raw[:, s % RAW, :, (J % 2) * P:(J % 2 + 1) * P],
                                wp[:, J % 2, 0].bitcast(F32), ALU.subtract).then_inc(wlo, 1)

            def add_square(name, t):
                if t == 0:
                    return
                dve.wait_ge(sums[name]["squared"], t + 1)
                if t > 1:
                    dve.wait_ge(sums[name]["added"], t - 1)
                V.tensor_tensor(acc[:, :], sq[:, 0] if t == 1 else acc[:, :], sq[:, t % 2], ALU.add)\
                    .then_inc(sums[name]["added"], 1)

            def reciprocal(name):
                wait_freed(dve, name)
                V.reciprocal(R[:, :], R[:, :]).then_inc(sums[name]["recip"], 1)
                dve.wait_ge(sums[name]["recip"], 1)

            def low_part(pre, g, t):
                dve.wait_ge(sums[pre]["hi"], t + 1)
                V.scalar_tensor_tensor(out=n[:, 1, t], in0=h[:, t], scalar=gain[g][t], in1=n[:, 0, t].bitcast(F32),
                                       op0=ALU.mult, op1=ALU.subtract).then_inc(sums[pre]["ready"], 1)

            def post_norm(post, g, pre=None, gpre=None):
                reciprocal(post)
                for t in range(KT + 2):
                    if t < KT:
                        V.scalar_tensor_tensor(out=f[:, t], in0=f[:, t], scalar=gain[g][t], in1=R[:, :],
                                               op0=ALU.mult, op1=ALU.mult).then_inc(sums[post]["scaled"], 1)
                    if 1 <= t <= KT:
                        dve.wait_ge(sums[post]["scaled"], t)
                        V.tensor_tensor(h[:, t - 1], h[:, t - 1], f[:, t - 1], ALU.add).then_inc(sums[post]["done"], 1)
                    if pre and t >= 2:
                        low_part(pre, gpre, t - 2)

            def pre_sum(pre, job):
                prepare(pl.base[job][0] + 2)
                reciprocal(pre)

            def take_scaled(dst, J, u, b=0, j=0):
                dve.wait_ge(job_done, J + 1 + per_body(b, j, JOBS_PER_BLOCK, 8))
                free(V.tensor_tensor(halves(dst), slot(u)[:, :, 0:HALF], halves(R[:, :]), ALU.mult), u)

            def scale_gate(name, i, e, b=0, j=0):
                dve.wait_ge(gate_out, GATE0[name] + i // 2 + e + 1 + per_body(b, j, KT, 4))
                V.tensor_tensor(sil[:, e], sil[:, e], R[:, :], ALU.mult).then_inc(gate_scaled, 1)

            def ffn(name, post, beside=None):
                J0, u0 = pl.base[name]

                def gate_up(b, j, first=False, ahead=False):
                    for i in (0, 4):
                        for e in range(2):
                            if i or not first:
                                dve.wait_ge(mid_ready, MID0[name] + i // 2 + e - 1 + per_body(b, j, KT, 4))
                            take_scaled(sil[:, e], J0 + i + e, u0 + i + e, b, j)
                            if i or e or not ahead:
                                prepare(J0 + i + e + 2, b, j)
                        for e in range(2):
                            scale_gate(name, i, e, b, j)
                        for e in range(2):
                            J, u = J0 + i + 2 + e, u0 + i + 2 + e
                            tile = ds(j * 4 + (i // 2 + e), 1)
                            dve.wait_ge(gate_scaled, GATE0[name] + i // 2 + e + 1 + per_body(b, j, KT, 4))
                            dve.wait_ge(job_done, J + 1 + per_body(b, j, JOBS_PER_BLOCK, 8))
                            free(V.tensor_tensor(halves(sil[:, e]), slot(u)[:, :, 0:HALF], halves(sil[:, e]), ALU.mult), u)
                            prepare(J + 2, b, j)
                            dve.wait_ge(mid_hi, HI0[name] + i // 2 + e + 1 + per_body(b, j, KT, 4))
                            V.tensor_tensor(mid[:, 1, tile].rearrange("p o t -> p (o t)"), sil[:, e],
                                            mid[:, 0, tile].rearrange("p o t -> p (o t)").bitcast(F32), ALU.subtract)\
                                .then_inc(mid_ready, 1)

                def down(b, last=False):
                    for i in range(KT):
                        J, u = J0 + 16 + i, u0 + 16 + i
                        dve.wait_ge(job_done, J + 1 + per_body(b, 0, JOBS_PER_BLOCK, 8))
                        dve.wait_ge(slot_free[(u0 + 15) % 4], (u0 + 15) // 4 + 1 + per_body(b, 0, 6, 2))
                        free(V.tensor_tensor(halves(f[:, i]), slot(u)[:, :, 0:HALF], halves(f[:, i]), ALU.add), u)
                        prepare(J + 2, b)
                        if last:
                            add_square(post, i)

                gate_up(0, 0, name == "ffn1", True)
                gate_up(0, 1)
                down(0)
                if beside:
                    beside()
                with dve.Fori(1, BLOCKS - 1) as b:
                    with dve.Fori(0, 2) as j:
                        gate_up(b, j)
                    down(b)
                with dve.Fori(0, 2) as j:
                    gate_up(BLOCKS - 1, j)
                down(BLOCKS - 1, True)

            for i in (1, 3):
                o, m = token_tile(i)
                wait_aux(dve, f"x{i}")
                free_aux(V.tensor_copy(h[:, :, o:o + m], eight(aux(f"x{i}"))[:, :, 0:m]), f"x{i}")
            for i in range(TT):
                wait_freed(dve, f"x{i}")
            wait_freed(dve, "gains")
            for t in range(KT):
                if t in (2, 4):
                    prepare(t // 2 - 1)
                low_part("pre1", "ffn1_g_pre", t)
            pre_sum("pre1", "ffn1")

            def memory_rows():
                dve.wait_ge(mem_rt, 1)
                V.reciprocal(mss, mss).then_inc(mem_rs, 1)
                dve.wait_ge(mem_rs, 1)
                for t in range(MT):
                    V.tensor_scalar(memraw[:, t], memraw[:, t], mss[:, t:t + 1], None, ALU.mult).then_inc(mem_n, 1)
            dve.wait_ge(f_zero, 1)
            ffn("ffn1", "post1", memory_rows)
            post_norm("post1", "ffn1_g_post", "pre2", "mix_g_pre")
            pre_sum("pre2", "glu0")

            def glu_gate(g, e):
                J, u = pl.base[f"glu{g}"]
                take_scaled(sil[:, e], J + e, u + e)
                if g or e:
                    prepare(J + e + 2)

            def glu_value(g, e):
                J, u = pl.base[f"glu{g}"]
                ct = 2 * g + e
                src = slot(u + 2 + e)
                dve.wait_ge(gate_scaled, GATE0[f"glu{g}"] + e + 1)
                dve.wait_ge(job_done, J + 2 + e + 1)
                V.tensor_tensor(glu[:, ct, LEFT:LEFT + HALF], src[:, 0, 0:HALF], sil[:, e, 0:HALF], ALU.mult)
                rest = SEQ - HALF
                V.tensor_tensor(glu[:, ct, LEFT + HALF:LEFT + SEQ], src[:, 1, 0:rest], sil[:, e, HALF:SEQ], ALU.mult)
                dst = glu[:, ct, GLU_S:GLU_W].rearrange("p (b k) -> p b k", b=NB)[:, :, LEFT:LEFT + DEC]
                free(V.tensor_tensor(dst, src[:, 1, rest:HALF].rearrange("p (b k) -> p b k", b=NB),
                                     sil[:, e, SEQ:T].rearrange("p (b k) -> p b k", b=NB), ALU.mult), u + 2 + e)
                prepare(J + 2 + e + 2)

            def scale_gates(g):
                for e in range(2):
                    scale_gate(f"glu{g}", 0, e)

            def conv(ct, beside):
                wait_use_freed(dve, pl.base[f"glu{ct // 2}"][1] + 2 + ct % 2)
                samples = glu[:, ct, GLU_S:GLU_W].rearrange("p (b k) -> p b k", b=NB)
                for k in range(TAPS):
                    for step in beside.get(k, ()):
                        step()
                    done = 2 * (ct * TAPS + k)
                    w = convw[:, ct, k:k + 1]
                    ps_ = [(f[:, 4 + ct, 0:SEQ], glu[:, ct, k:k + SEQ]),
                           (f[:, 4 + ct, SEQ:T].rearrange("p (b k) -> p b k", b=NB), samples[:, :, k:k + DEC])]
                    for e, (dst, src) in enumerate(ps_):
                        if k == 0:
                            V.tensor_scalar(dst, src, w, convb[ct], ALU.mult, ALU.add).then_inc(conv_step, 1)
                        else:
                            dve.wait_ge(conv_step, done - 2 + e + 1)
                            V.scalar_tensor_tensor(out=dst, in0=src, scalar=w, in1=dst, op0=ALU.mult, op1=ALU.add)\
                                .then_inc(conv_step, 1)

            def after(name, i=0):
                return lambda: prepare(pl.base[name][0] + i + 2)

            def take_u(t):
                def step():
                    J, u = pl.base[f"u{t}"]
                    take_scaled(f[:, t], J, u)
                    prepare(J + 2)
                return step

            for e in range(2):
                glu_gate(0, e)
            scale_gates(0)
            for e in range(2):
                glu_value(0, e)
            for t in range(MT):
                wait_aux(dve, f"mem{t}")
                free_aux(V.tensor_tensor(memT[:, :, t * P:(t + 1) * P], eight(aux(f"mem{t}")),
                                         gvec[:, 32:40].unsqueeze(2).to_broadcast([P, KT, P]), ALU.mult), f"mem{t}")
            wait_freed(dve, "state1")
            dve.wait_ge(glu_zero, 1)
            wait_freed(dve, "convw")
            conv(0, {3: [lambda: glu_gate(1, 0)], 11: [lambda: glu_gate(1, 1)], 15: [lambda: scale_gates(1)],
                     19: [lambda: glu_value(1, 0)], 27: [lambda: glu_value(1, 1)]})
            conv(1, {4: [after("sv0")], 11: [after("sv1")], 19: [after("sv2")], 27: [after("sv3")]})
            conv(2, {4: [take_u(0)], 11: [take_u(1)], 19: [take_u(2)], 27: [take_u(3)]})
            wait_freed(dve, "vt3")
            for i in range(TT):
                m = token_tile(i)[1]
                V.bn_stats(bst[0:m, 6 * i:6 * i + 6], sv[0:m, i]).then_inc(sv_st, 1)
            for i in range(TT):
                m = token_tile(i)[1]
                dve.wait_ge(sv_st, i + 1)
                V.bn_aggr(bag[0:m, 2 * i:2 * i + 2], bst[0:m, 6 * i:6 * i + 6]).then_inc(sv_mv, 1)
            dve.wait_ge(sv_rt, 1)
            V.reciprocal(vrs[:, 0:4], vrs[:, 0:4])
            V.reciprocal(vrs[0:64, 4:5], vrs[0:64, 4:5]).then_inc(sv_rs, 1)
            dve.wait_ge(sv_rs, 1)
            for i in range(TT):
                m = token_tile(i)[1]
                V.tensor_scalar(sv[0:m, i], sv[0:m, i], bag[0:m, 2 * i:2 * i + 1], vrs[0:m, i:i + 1], ALU.subtract, ALU.mult)\
                    .then_inc(sv_n, 1)
            conv(3, {})
            wait_aux(dve, "cmean")
            for t in range(CT):
                ins = V.scalar_tensor_tensor(out=halves(f[:, 4 + t]), in0=aux("cmean")[:, :, 0:HALF], scalar=-1.0 / CW,
                                             in1=halves(f[:, 4 + t]), op0=ALU.mult, op1=ALU.add)
                if t < CT - 1:
                    ins.then_inc(cc_ready, 1)
                else:
                    free_aux(ins, "cmean")

            def gated_low(t):
                dve.wait_ge(mid_hi, HI0["mix"] + t + 1)
                V.tensor_tensor(mid[:, 1, t], sil[:, t % 2], mid[:, 0, t].bitcast(F32), ALU.subtract).then_inc(mid_ready, 1)

            dve.wait_ge(ld_bs, 16)
            for t in range(4):
                wait_aux(dve, f"sg{t}")
                if t >= 2:
                    dve.wait_ge(mid_ready, MID0["mix"] + t - 1)
                s = sil[:, t % 2]
                V.tensor_tensor(s[:, 0:SEQ].rearrange("p (c i) -> p c i", c=4), aux(f"sg{t}")[:, 0, :].rearrange("p (c i) -> p c i", c=4),
                                bsb[:, t:t + 1, :].to_broadcast([P, 4, P]), ALU.add)
                free_aux(V.tensor_tensor(s[:, SEQ:T].rearrange("p (b i) -> p b i", b=NB),
                                         aux(f"sg{t}")[:, 1, 0:NB * DEC].rearrange("p (b i) -> p b i", b=NB),
                                         bsb[:, t:t + 1, 0:DEC].to_broadcast([P, NB, DEC]), ALU.add), f"sg{t}")
                wait_freed(dve, f"sg{t}")
                V.tensor_tensor(s, s, f[:, t], ALU.mult).then_inc(gated, 1)
                if t:
                    gated_low(t - 1)
            gated_low(3)
            reciprocal("cvar")
            for t in range(CT):
                V.tensor_tensor(f[:, 4 + t], f[:, 4 + t], R[:, :], ALU.mult).then_inc(cn_ready, 1)
            for t in range(2):
                prepare(pl.base["out"][0] + t)
            for t in range(CT):
                dve.wait_ge(mid_hi, HI0["mix"] + 4 + t + 1)
                V.tensor_tensor(mid[:, 1, 4 + t], f[:, 4 + t], mid[:, 0, 4 + t].bitcast(F32), ALU.subtract)\
                    .then_inc(mid_ready, 1)

            def project(job, post):
                for t in range(KT):
                    prepare(pl.base[job][0] + t + 2)
                    add_square(post, t)

            project("out", "post2")
            post_norm("post2", "mix_g_post", "pre3", "xattn_g_pre")
            pre_sum("pre3", "q")
            for t in range(KT):
                J, u = pl.base["q"]
                take_scaled(f[:, t], J + t, u + t)
                if t:
                    prepare(J + t + 2)

            def keys_turned(b):
                wait_aux(dve, f"ktb{b}")
                free_aux(V.tensor_copy(kts[:, b % 2, :, P:2 * P], eight(aux(f"ktb{b}"))), f"ktb{b}")

            def sample_scores(b):
                wait_aux(dve, f"ss{b}")
                free_aux(V.tensor_copy(sT[:, :, b * 32:(b + 1) * 32], aux(f"ss{b}")[:, :, 0:32]), f"ss{b}")

            def scale_rows(i):
                c = slice(4 * i, 4 * i + 4)
                wait_freed(dve, f"sc{i}")
                V.reciprocal(sm[:, c], sm[:, c]).then_inc(rs_ready, 1)
                dve.wait_ge(rs_ready, i + 1)
                for hd in range(HEADS):
                    V.tensor_scalar(prob[:, i % 2, hd], prob[:, i % 2, hd], sm[:, 4 * i + hd:4 * i + hd + 1], None, ALU.mult)\
                        .then_inc(p_ready, 1)

            for i in range(4):
                wait_aux(dve, f"sc{i}")
                V.tensor_reduce(mx[:, 4 * i:4 * i + 4], flat(aux(f"sc{i}")).rearrange("p (h m) -> p h m", h=HEADS),
                                AX_X, ALU.max, negate=True).then_inc(mx_ready, 1)
                for b in (2 * i, 2 * i + 1):
                    if b >= 2:
                        wait_aux(dve, f"ss{b - 2}")
                    keys_turned(b)
                    if b % 2 == 0:
                        scale_rows(i)
                    if b:
                        sample_scores(b - 1)
            sample_scores(7)
            wait_aux(dve, "sroll")
            V.tensor_reduce(smx, aux("sroll")[:, :, 0:MEM], AX_X, ALU.max, negate=True).then_inc(smx_ready, 1)
            wait_freed(dve, "sroll")
            V.reciprocal(ssm, ssm).then_inc(srs_ready, 1)
            dve.wait_ge(srs_ready, 1)
            for r in range(2):
                V.tensor_scalar(psm[:, r], psm[:, r], ssm[:, r:r + 1], None, ALU.mult).then_inc(sp_ready, 1)
            for o in range(KT):
                dve.wait_ge(mid_hi, HI0["att"] + o + 1)
                free_aux(V.tensor_tensor(mid[:, 1, o, 0:SEQ], aux(f"pv{o}")[:, 0, :], mid[:, 0, o, 0:SEQ].bitcast(F32),
                                         ALU.subtract), f"pv{o}")
            dve.wait_ge(mid_hi, HI0["att"] + KT + 1)
            free_aux(V.tensor_tensor(mid[:, 1, :, SEQ:T], aux("pvs")[:, 0, :].rearrange("p (o t) -> p o t", o=KT),
                                     mid[:, 0, :, SEQ:T].bitcast(F32), ALU.subtract), "pvs")
            project("o", "post3")
            post_norm("post3", "xattn_g_post", "pre4", "ffn2_g_pre")
            pre_sum("pre4", "ffn2")
            dve.wait_ge(f_zero, 2)
            ffn("ffn2", "post4")
            post_norm("post4", "ffn2_g_post")
            for i in (1, 3):
                wait_aux(dve, f"y{i}")
                free_aux(V.tensor_copy(ytok[:, i], flat(aux(f"y{i}"))), f"y{i}")

        @block.tensor
        def _(pe):
            def job_products(J, u, X, kt):
                for k, (wi, xi) in enumerate(PRODUCTS):
                    for half in range(2):
                        ins = pe.matmul(slot(u)[:, half, 0:HALF], wp[:, J % 2, wi, kt], X(xi, kt, half),
                                        start=kt == 0 and k == 0, stop=kt == KT - 1 and k == len(PRODUCTS) - 1)
                if kt == KT - 1:
                    ins.then_inc(job_done, 1)

            def job(name, i, X, need=None, b=0, j=0):
                J, u = pl.base[name][0] + i, pl.base[name][1] + i
                wait_slot(pe, u, per_body(b, j, 6, 2))
                pe.wait_ge(wlo, prepared(J) + 1 + per_body(b, j, JOBS_PER_BLOCK, 8))
                for kt in range(KT):
                    if need:
                        need(kt)
                    job_products(J, u, X, kt)

            def memory_jobs(name, count):
                for i in range(count):
                    J, u = pl.base[name][0] + i, pl.base[name][1] + i
                    s = J // 2
                    wait_slot(pe, u)
                    pe.wait_ge(loaded[s % RAW], 16 * (s // RAW + 1))
                    for kt in range(KT):
                        ins = pe.matmul(slot(u)[:, 0, 0:MEM], raw[:, s % RAW, kt, (J % 2) * P:(J % 2 + 1) * P], memT[:, kt, :],
                                        start=kt == 0, stop=kt == KT - 1)
                    ins.then_inc(job_done, 1)

            def half_of(tile):
                return lambda part, kt, half: tile[:, part, kt, half * HALF:(half + 1) * HALF]

            def jobs(name, X, need=None, count=KT, **kw):
                for i in range(count):
                    job(name, i, X, need if i == 0 else None, **kw)

            def turn(name, tiles):
                wait_slot(pe, pl.aux[name][1])
                for dst, src in tiles:
                    m = src.shape[0]
                    ins = pe.transpose(dst, src, ident[0:m, 0:m])
                ins.then_inc(filled, 1)

            def sum_tile(name, t, count, src):
                if t == 0:
                    wait_slot(pe, pl.aux[name][1])
                for half in range(2):
                    ins = pe.matmul(aux(name)[:, half, 0:HALF], ones[:, :], src[:, half * HALF:(half + 1) * HALF],
                                    start=t == 0, stop=t == count - 1)
                if t < count - 1:
                    ins.then_inc(sums[name]["summed"], 1)
                else:
                    ins.then_inc(filled, 1)

            def sum_squares(name):
                wait_slot(pe, pl.aux[name][1])
                pe.wait_ge(sums[name]["added"], KT - 1)
                for half in range(2):
                    ins = pe.matmul(aux(name)[:, half, 0:HALF], ones[:, :], acc[:, half * HALF:(half + 1) * HALF],
                                    start=True, stop=True)
                ins.then_inc(filled, 1)

            def jobs_normed(name, pre, count):
                J, u = pl.base[name]
                for t in range(KT + 2):
                    if t in (0, 2):
                        wait_slot(pe, u + t // 2)
                    if t == 0:
                        pe.wait_ge(wlo, prepared(J) + 1)
                    if t < KT:
                        pe.wait_ge(sums[pre]["ready"], t + 1)
                        job_products(J, u, half_of(n), t)
                    if 1 <= t <= KT:
                        pe.wait_ge(sums[pre]["squared"], t)
                        sum_tile(pre, t - 1, KT, sq[:, (t - 1) % 2])
                    if t == 2:
                        pe.wait_ge(wlo, prepared(J + 1) + 1)
                    if t >= 2:
                        job_products(J + 1, u + 1, half_of(n), t - 2)
                for i in range(2, count):
                    job(name, i, half_of(n))

            def ffn(name, pre):
                def product_ready(b):
                    return lambda kt: pe.wait_ge(mid_ready, MID0[name] + kt + 1 + per_body(b, 0, KT, 4))

                def down(b):
                    for i in range(KT):
                        job(name, 16 + i, half_of(mid), product_ready(b) if i == 0 else None, b=b)

                jobs_normed(name, pre, 16)
                down(0)
                with pe.Fori(1, BLOCKS) as b:
                    with pe.Fori(0, 2) as j:
                        for i in range(8):
                            job(name, i, half_of(n), b=b, j=j)
                    down(b)

            pe.wait_ge(id_set, 2)
            pe.wait_ge(const_set, 1)
            for i in range(TT):
                m = token_tile(i)[1]
                pe.wait_ge(ld_x[i] if i < 4 else ld_xs, 16)
                turn(f"x{i}", [(eight(aux(f"x{i}"))[:, kt, 0:m], xin[0:m, i, kt * P:(kt + 1) * P]) for kt in range(KT)])
                if i == 1:
                    pe.wait_ge(ld_small, 16 * 12)
                    turn("gains", [(aux("gains")[:, 0, 0:84], graw[:, :])])
            pe.wait_ge(ld_cw, 16)
            turn("convw", [(eight(aux("convw"))[:, ct, 0:TAPS], cwraw[:, ct * P:(ct + 1) * P]) for ct in range(CT)])
            pe.wait_ge(masked, 1)
            turn("spatial", [(eight(aux("spatial"))[:, hd, :], wsr[:, hd, :]) for hd in range(4)])
            ffn("ffn1", "pre1")
            sum_squares("post1")
            jobs_normed("glu0", "pre2", 4)
            for t in range(MT):
                pe.wait_ge(mem_n, t + 1)
                turn(f"mem{t}", [(eight(aux(f"mem{t}"))[:, kt, :], memraw[:, t, kt * P:(kt + 1) * P]) for kt in range(KT)])
            pe.wait_ge(ld_st, 16)
            for r in range(2):
                turn(f"state{r}", [(eight(aux(f"state{r}"))[:, ct, 0:120], straw[:, r, ct * P:(ct + 1) * P]) for ct in range(CT)])
            jobs("glu1", half_of(n), None, 4)
            pieces = []
            for i in range(TT):
                o, m = token_tile(i)
                pieces.append((flat(aux("rcol"))[0:m, i * P:(i + 1) * P], R[:, o:o + m]))
            pe.wait_ge(sums["pre2"]["recip"], 1)
            turn("rcol", pieces)

            def turn_v(t):
                wait_use_freed(pe, pl.base[f"sv{t}"][1])
                pieces = []
                for i in range(TT):
                    o, m = token_tile(i)
                    pieces.append((flat(aux(f"vt{t}"))[0:m, i * P:(i + 1) * P], sq[:, t % 2, o:o + m]))
                turn(f"vt{t}", pieces)

            jobs("sv0", half_of(n), None, 1)
            for t in range(1, 4):
                jobs(f"sv{t}", half_of(n), None, 1)
                turn_v(t - 1)
            jobs("u0", half_of(n), None, 1)
            turn_v(3)
            for t in range(1, 4):
                jobs(f"u{t}", half_of(n), None, 1)

            wait_freed(pe, "mem0")
            wait_freed(pe, "mem1")
            memory_jobs("k", KT)

            def spatial(heads):
                pe.wait_ge(sv_b, TT)
                pe.wait_ge(ld_bd, 16 * NB)
                for hd in heads:
                    name, cols = f"sg{hd}", slice(hd * P, (hd + 1) * P)
                    wait_slot(pe, pl.aux[name][1])
                    for c in range(4):
                        pe.matmul(aux(name)[:, 0, c * P:(c + 1) * P], sv[:, c, cols], wsT[:, hd, :], start=True, stop=True)
                    pe.matmul(aux(name)[:, 1, 0:NB * DEC], sv[0:NB * DEC, 4, cols], bd[:, hd, :], start=True, stop=True)\
                        .then_inc(filled, 1)

            memory_jobs("v0", 4)
            for t in range(CT):
                pe.wait_ge(conv_step, 2 * (t + 1) * TAPS)
                sum_tile("cmean", t, CT, f[:, 4 + t])
            spatial((0, 1))
            memory_jobs("v4", 2)
            for t in range(CT):
                pe.wait_ge(sums["cvar"]["squared"], t + 1)
                sum_tile("cvar", t, CT, sq[:, t % 2])
            spatial((2, 3))
            memory_jobs("v6", 2)
            for name, src in (("ktok", kT), ("vtok", vT)):
                if src is vT:
                    for last in ("v4", "v6"):
                        for e in range(2):
                            wait_use_freed(pe, pl.base[last][1] + e)
                for t in range(MT):
                    turn(f"{name}{t}", [(eight(aux(f"{name}{t}"))[:, ft, :], src[:, ft, t * P:(t + 1) * P]) for ft in range(KT)])
            for e in range(4):
                wait_use_freed(pe, pl.base["glu1"][1] + e)
            turn("glup", [(aux("glup")[0:LEFT, 0, ct * P:(ct + 1) * P], glu[:, ct, SEQ:SEQ + LEFT]) for ct in range(CT)])
            pe.wait_ge(gs_ready, 1)
            turn("glus", [(aux("glus")[0:NB * DEC, 0, ct * P:(ct + 1) * P], gsm[:, ct, :]) for ct in range(CT)])
            jobs("out", half_of(mid), lambda kt: pe.wait_ge(mid_ready, MID0["mix"] + kt + 1))
            sum_squares("post2")
            jobs_normed("q", "pre3", KT)
            for e in range(4):
                wait_use_freed(pe, pl.base["q"][1] + 4 + e)

            def sample_scores(b):
                name = f"ss{b}"
                wait_slot(pe, pl.aux[name][1])
                wait_freed(pe, f"kta{b}")
                wait_freed(pe, f"ktb{b}")
                for t in range(MT):
                    for hd in range(HEADS):
                        for d in range(2):
                            ins = pe.matmul(aux(name)[:, t, hd * DEC:(hd + 1) * DEC], kts[:, b % 2, 2 * hd + d, t * P:(t + 1) * P],
                                            f[:, 2 * hd + d, SEQ + b * DEC:SEQ + (b + 1) * DEC], start=d == 0, stop=d == 1)
                ins.then_inc(filled, 1)

            def turn_probs(i):
                pe.wait_ge(p_ready, 4 * i + 4)
                turn(f"pt{i}", [(eight(aux(f"pt{i}"))[:, 2 * hd + t, :], prob[:, i % 2, hd, t * P:(t + 1) * P])
                                for hd in range(HEADS) for t in range(MT)])

            for i in range(4):
                name = f"sc{i}"
                wait_slot(pe, pl.aux[name][1])
                for hd in range(HEADS):
                    for d in range(2):
                        ins = pe.matmul(aux(name)[:, hd // 2, (hd % 2) * MEM:(hd % 2 + 1) * MEM],
                                        f[:, 2 * hd + d, i * P:(i + 1) * P], kT[:, 2 * hd + d, :], start=d == 0, stop=d == 1)
                ins.then_inc(filled, 1)
                for b in (2 * i, 2 * i + 1):
                    pe.wait_ge(ld_k[b % 4], 16 * (b // 4 + 1))
                    keys = kring[:, b % 4] if b % 4 < 3 else k3[:, :, :]
                    for t, x in enumerate("ab"):
                        turn(f"kt{x}{b}", [(eight(aux(f"kt{x}{b}"))[:, ft, :], keys[:, t, ft * P:(ft + 1) * P]) for ft in range(KT)])
                    if b:
                        sample_scores(b - 1)
                if i:
                    turn_probs(i - 1)
            sample_scores(7)
            turn_probs(3)
            wait_freed(pe, "ss7")
            turn("sroll", [(aux("sroll")[:, r, t * P:(t + 1) * P], sT[:, t, r * P:(r + 1) * P]) for r in range(2) for t in range(MT)])

            def head_out(o):
                name = f"pv{o}"
                wait_slot(pe, pl.aux[name][1])
                for t in range(MT):
                    ins = pe.matmul(aux(name)[:, 0, :], vtok[:, t, o * P:(o + 1) * P], pT[:, o // 2 * 2 + t, :], start=t == 0, stop=t == 1)
                ins.then_inc(filled, 1)

            for i in range(4):
                wait_freed(pe, f"pt{i}")
            head_out(0)
            head_out(1)
            pe.wait_ge(sp_ready, 2)
            turn("sprob", [(aux("sprob")[:, t, r * P:(r + 1) * P], psm[:, r, t * P:(t + 1) * P]) for r in range(2) for t in range(MT)])
            for o in range(2, 8):
                head_out(o)
            wait_slot(pe, pl.aux["pvs"][1])
            wait_freed(pe, "sprob")
            for b in range(NB):
                pe.wait_ge(ld_v[b % 5], 16 * (b // 5 + 1))
                vals = vx[:, b - 3] if 3 <= b < 5 else kring[:, b % 5]
                for o in range(KT):
                    c = o * NB * DEC + b * DEC
                    p0 = b * 32 + (o // 2) * DEC
                    for t in range(MT):
                        ins = pe.matmul(aux("pvs")[:, 0, c:c + DEC], vals[:, t, o * P:(o + 1) * P], pTs[:, t, p0:p0 + DEC],
                                        start=t == 0, stop=t == 1)
                ins.then_inc(vs_used if b < NB - 1 else filled, 1)

            def attended(kt):
                wait_freed(pe, f"pv{kt}")
                if kt == 0:
                    wait_freed(pe, "pvs")
            jobs("o", half_of(mid), attended)
            sum_squares("post3")
            ffn("ffn2", "pre4")
            sum_squares("post4")
            for i in range(4):
                wait_slot(pe, pl.aux[f"y{i}"][1])
            for kt in range(KT):
                pe.wait_ge(sums["post4"]["done"], kt + 1)
                for i in range(4):
                    ins = pe.transpose(flat(aux(f"y{i}"))[:, kt * P:(kt + 1) * P], h[:, kt, i * P:(i + 1) * P], ident[:, :])
                    if kt == KT - 1:
                        ins.then_inc(filled, 1)
            turn("y4", [(flat(aux("y4"))[0:NB * DEC, kt * P:(kt + 1) * P], h[:, kt, SEQ:T]) for kt in range(KT)])


_INS = ["x_prompt", "x_sample", "mem_prompt", "cache_mem_k", "cache_mem_v", "state_conv",
        "ffn1_g_pre", "ffn1_w_gate", "ffn1_w_up", "ffn1_w_down", "ffn1_g_post",
        "mix_g_pre", "mix_w_in", "sgu_ln_g", "sgu_ln_b", "sgu_w_s", "sgu_b_s",
        "conv_w", "conv_b", "conv_ln_g", "conv_ln_b", "mix_w_out", "mix_g_post",
        "mem_g", "xattn_g_pre", "xattn_w_q", "xattn_w_k", "xattn_w_v", "xattn_w_o", "xattn_g_post",
        "ffn2_g_pre", "ffn2_w_gate", "ffn2_w_up", "ffn2_w_down", "ffn2_g_post"]
_OUTS = [(1, 512, 1024), (8, 8, 1024), (1, 1, 256, 4, 256), (1, 1, 256, 4, 256), (1, 1, 30, 512), (1, 8, 30, 512),
         (1, 1, 128, 512), (1, 8, 8, 512)]


def kernel(**inputs):
    import numpy as _np
    import concourse.bacc as _bacc
    from concourse import mybir as _mybir
    from concourse.bass_utils import run_bass_kernel_spmd as _run

    nc = _bacc.Bacc("TRN2", target_bir_lowering=False, num_devices=1)
    arrays, aps = {}, {}
    for name in _INS:
        x = _np.ascontiguousarray(inputs[name])
        arrays[f"in_{name}_dram"] = x
        aps[name] = nc.dram_tensor(f"in_{name}_dram", x.shape, _mybir.dt.from_np(x.dtype), kind="ExternalInput").ap()
    outs = [nc.dram_tensor(f"out_{i}_dram", shape, _mybir.dt.float32, kind="ExternalOutput").ap()
            for i, shape in enumerate(_OUTS)]
    build(nc, aps, outs)
    r = _run(nc, [arrays], core_ids=[0])
    return tuple(r.results[0][f"out_{i}_dram"] for i in range(len(_OUTS)))
```

```python
from contextlib import ExitStack

import concourse.bass as bass
from concourse import mybir

F32 = mybir.dt.float32
F32R = mybir.dt.float32r
ACT = mybir.ActivationFunctionType
ALU = mybir.AluOpType
AX_X = mybir.AxisListType.X
ds = bass.ds

PARTS = 2
PDT = F32R
PRODUCTS = [(0, 0), (0, 1), (1, 0)]

P = 128
D = 1024
KT = D // P
FFN = 4096
SEQ = 512
NB = 8
DEC = 8
T = SEQ + NB * DEC
HALF = T // 2
BLOCKS = FFN // D
MEM = 256
MT = MEM // P
HEADS = 4
SGW = 512
CW = 512
CT = CW // P
TAPS = 31
LEFT = TAPS - 1
GLU_S = LEFT + SEQ
GLU_W = GLU_S + NB * (LEFT + DEC)
EPS = 1e-6
TT = 5
JOBS_PER_BLOCK = 3 * KT
RAW = 2


def token_tile(i):
    return i * P, (P if i < 4 else NB * DEC)


class Plan:

    def __init__(self):
        self.n = 0
        self.jobs = 0
        self.aux = {}
        self.base = {}

    def job_run(self, name, count):
        self.base[name] = (self.jobs, self.n)
        self.jobs += count
        self.n += count

    def use(self, *names):
        for name in names:
            self.aux[name] = (len(self.aux), self.n)
            self.n += 1


def make_plan():
    pl = Plan()
    pl.use("x0", "x1", "gains", "x2", "x3", "x4", "convw", "spatial", "pre1")
    pl.job_run("ffn1", BLOCKS * JOBS_PER_BLOCK)
    pl.use("post1", "mem0", "mem1", "pre2")
    pl.job_run("glu0", 4)
    pl.use("state0", "state1")
    pl.job_run("glu1", 4)
    pl.use("rcol")
    pl.job_run("k0", 2)
    pl.job_run("sv0", 1)
    pl.job_run("sv1", 1)
    pl.use("vt0")
    pl.job_run("k2", 2)
    pl.job_run("sv2", 1)
    pl.use("vt1")
    pl.job_run("sv3", 1)
    pl.use("vt2")
    pl.job_run("u0", 1)
    pl.use("vt3")
    pl.job_run("u1", 1)
    pl.job_run("u2", 1)
    pl.job_run("u3", 1)
    pl.job_run("k4", 4)
    pl.job_run("v0", 6)
    pl.use("cmean", "sg0", "sg1", "cvar", "sg2", "sg3")
    pl.job_run("v6", 2)
    pl.use("ktok0", "ktok1")
    pl.job_run("out", 8)
    pl.use("post2", "vtok0", "vtok1", "glup", "glus", "pre3")
    pl.job_run("q", 8)
    for i in range(4):
        pl.use(f"sc{i}")
        for b in (2 * i, 2 * i + 1):
            pl.use(f"kta{b}", f"ktb{b}")
            if b:
                pl.use(f"ss{b - 1}")
        if i:
            pl.use(f"pt{i - 1}")
    pl.use("ss7", "pt3", "pv0", "pv1", "pv2", "sprob", *[f"pv{o}" for o in range(3, 8)], "pvs", "pvt")
    pl.job_run("o", 8)
    pl.use("post3", "pre4")
    pl.job_run("ffn2", BLOCKS * JOBS_PER_BLOCK)
    pl.use("post4", *[f"y{i}" for i in range(TT)])
    return pl


def build(nc, a, out):
    pl = make_plan()
    y_prompt, y_sample, mem_k_o, mem_v_o, cs_p, cs_s, cv_p, cv_s = out
    w2 = {n: a[n].rearrange("l r c -> (l r) c") for n in (
        "ffn1_w_gate", "ffn1_w_up", "ffn1_w_down", "ffn2_w_gate", "ffn2_w_up", "ffn2_w_down", "mix_w_in",
        "mix_w_out", "xattn_w_q", "xattn_w_k", "xattn_w_v", "xattn_w_o")}
    x_p = a["x_prompt"].rearrange("b s d -> (b s) d")
    x_s = a["x_sample"].rearrange("b s d -> (b s) d")
    ck = a["cache_mem_k"].rearrange("l b m h d -> (l b) m (h d)")
    cv = a["cache_mem_v"].rearrange("l b m h d -> (l b) m (h d)")

    ctx = ExitStack()
    with ctx:
        def sb(name, shape, dt=F32):
            return ctx.enter_context(nc.sbuf_tensor(name, shape, dt))

        def views(name, *tiles):
            size = 0
            found = {}
            for group in tiles:
                used = 0
                with ExitStack() as inner:
                    for n, shape, dt in group:
                        found[n] = inner.enter_context(nc.sbuf_tensor(n, shape, dt))
                        words = 1
                        for s in shape[1:]:
                            words *= s
                        used += words
                size = max(size, used)
            sb(name, [P, size])
            return found

        def sem(name):
            return ctx.enter_context(nc.semaphore(name))

        ident = sb("ident", [P, P])
        ones = sb("ones", [P, P])
        epst = sb("epst", [P, 3])
        gvec = sb("gvec", [P, 84])
        convw = sb("convw", [P, CT, TAPS + 1])
        wsT = sb("wsT", [P, 4, P])
        bd = sb("bd", [NB * DEC, 4, NB * DEC])
        bsb = sb("bsb", [P, 4, P])
        osm = sb("osm", [P, CW])
        gsm = sb("gsm", [P, CT, NB * DEC])
        small = sb("small", [P, 112])
        mx, sm = small[:, 0:16], small[:, 16:32]
        smx, ssm = small[:, 32:34], small[:, 34:36]
        mss = small[:, 36:38]
        bst, bag = small[:, 40:70], small[:, 70:80]
        vrs, rc = small[:, 80:85], small[:, 85:90]
        h = sb("h", [P, KT, T])
        kT = sb("kT", [P, KT, MEM])
        vtok = sb("vtok", [P, MT, D])
        R = sb("R", [P, T])
        acc = sb("acc", [P, T])
        raw = sb("raw", [P, RAW, KT, 256])
        wp = sb("wp", [P, 2, PARTS, KT, P], PDT)
        rn = views("region_n", [("n", [P, PARTS, KT, T], PDT)],
                   [("pT", [P, 8, SEQ], F32), ("kts", [P, 2, KT, MEM], F32)],
                   [("pT_", [P, 8, SEQ], F32), ("vx", [P, 2, MT, D], F32)],
                   [("vT", [P, KT, MEM], F32), ("ktok", [P, MT, D], F32)])
        rm = views("region_mid", [("mid", [P, PARTS, KT, T], PDT)],
                   [("prob", [P, 2, HEADS, MEM], F32), ("k3", [P, MT, D], F32), ("qs", [P, NB, KT, HEADS * DEC], F32)],
                   [("spare0", [P, 4, T], F32), ("lng", [P, SGW], F32), ("lnb", [P, SGW], F32), ("straw", [120, 2, CW], F32),
                    ("spare1", [P, 8 * T - 2 * SGW - 2 * CW], F32), ("memT", [P, KT, MEM], F32)])
        rf = views("region_f", [("f", [P, KT, T], F32)],
                   [("ps", [P, MT, HEADS, NB * 72], F32)],
                   [("wsr", [P, 4, P], F32), ("graw", [84, P], F32), ("cwraw", [TAPS, CW], F32)])
        rx = views("region_x", [("xin", [P, TT, D], F32)],
                   [("sv", [P, TT, SGW], F32), ("glu", [P, CT, GLU_W], F32)],
                   [("memraw", [P, MT, D], F32)], [("kring", [P, 3, MT, D], F32)], [("ytok", [P, TT, D], F32)])
        rt = views("region_t", [("sq", [P, 2, T], F32), ("sil", [P, 2, T], F32)],
                   [("psm", [P, 2, MEM], F32), ("os", [NB * DEC, D], F32)])
        n, pT, kts, vx, vT, ktok = (rn[k] for k in ("n", "pT", "kts", "vx", "vT", "ktok"))
        mid, prob, k3, qs, memT = rm["mid"], rm["prob"], rm["k3"], rm["qs"], rm["memT"]
        lng, lnb, straw = rm["lng"], rm["lnb"], rm["straw"]
        f, ps, wsr, graw, cwraw = (rf[k] for k in ("f", "ps", "wsr", "graw", "cwraw"))
        xin, memraw, sv, glu, kring, ytok = (rx[k] for k in ("xin", "memraw", "sv", "glu", "kring", "ytok"))
        sq, sil, psm, os_ = (rt[k] for k in ("sq", "sil", "psm", "os"))
        slots = [ctx.enter_context(nc.psum_tensor(f"slot{i}", [P, 2, 512], F32)) for i in range(4)]

        HI0 = {"ffn1": 0, "mix": KT * BLOCKS, "att": KT * BLOCKS + 8, "ffn2": KT * BLOCKS + 8 + KT + 1}
        MID0 = {"ffn1": 0, "mix": KT * BLOCKS, "ffn2": KT * BLOCKS + 8}
        GATE0 = {"ffn1": 0, "glu0": KT * BLOCKS, "glu1": KT * BLOCKS + 2, "ffn2": KT * BLOCKS + 4}
        memjunk = sq[:, :, :].rearrange("p a b -> p (a b)")[:, 0:D]
        ROOTS = {"plain": (1.0, 0), "half": (4.0, 1), "query": (float(D // HEADS), 2)}
        GAINS = ["ffn1_g_pre", "ffn1_g_post", "mix_g_pre", "mix_g_post", "mem_g", "xattn_g_pre",
                 "xattn_g_post", "ffn2_g_pre", "ffn2_g_post"]
        gain = {name: [gvec[:, 8 * i + t:8 * i + t + 1] for t in range(KT)] for i, name in enumerate(GAINS)}
        CV0 = 8 * len(GAINS)
        convb, clg, clb = ([gvec[:, CV0 + 4 * i + t:CV0 + 4 * i + t + 1] for t in range(CT)] for i in range(3))

        slot_free = [sem(f"slot_free{i}") for i in range(4)]
        job_done = sem("job_done")
        filled = sem("filled")
        loaded = [sem(f"loaded{i}") for i in range(RAW)]
        whi, wlo = sem("whi"), sem("wlo")
        ld_small, ld_cw, ld_ws, ld_bs, ld_ln, ld_st = (sem(f"ld_{x}") for x in ("small", "cw", "ws", "bs", "ln", "st"))
        ld_rest = sem("ld_rest")
        ld_mem, ld_xs, ld_bd = sem("ld_mem"), sem("ld_xs"), sem("ld_bd")
        ld_x = [sem(f"ld_x{i}") for i in range(4)]
        ld_k = [sem(f"ld_k{i}") for i in range(4)]
        ld_v = [sem(f"ld_v{i}") for i in range(5)]
        id_set, const_set, masked, bd_zero, glu_zero, eps_set = (
            sem(x) for x in ("id_set", "const_set", "masked", "bd_zero", "glu_zero", "eps_set"))
        mem_sq, mem_rt, mem_rs, mem_n = (sem(x) for x in ("mem_sq", "mem_rt", "mem_rs", "mem_n"))
        gate_out, gate_scaled, k_stored, v_stored = (sem(x) for x in ("gate_out", "gate_scaled", "k_stored", "v_stored"))
        f_zero = sem("f_zero")
        gated, mid_hi, mid_ready = sem("gated"), sem("mid_hi"), sem("mid_ready")
        sums = {}
        for s in ("pre1", "post1", "pre2", "cmean", "cvar", "post2", "pre3", "post3", "pre4", "post4"):
            parts = ["squared", "recip"]
            if s.startswith("p"):
                parts.append("added")
            if not s.startswith("post"):
                parts.append("summed")
            if s.startswith("post"):
                parts += ["scaled", "done"]
            if s.startswith("pre"):
                parts += ["hi", "ready"]
            sums[s] = {x: sem(f"{s}_{x}") for x in parts}
        sv_st, sv_mv, sv_rt, sv_rs, sv_n, sv_g, sv_b = (
            sem(x) for x in ("sv_st", "sv_mv", "sv_rt", "sv_rs", "sv_n", "sv_g", "sv_b"))
        conv_step, cc_ready, cn_ready, act_b = (sem(x) for x in ("conv_step", "cc_ready", "cn_ready", "act_b"))
        mx_ready, rs_ready, p_ready = sem("mx_ready"), sem("rs_ready"), sem("p_ready")
        smx_ready, srs_ready, sp_ready = sem("smx_ready"), sem("srs_ready"), sem("sp_ready")
        qs_zero, qs_ready, ps_zero, s_exp, os_ready = (
            sem(x) for x in ("qs_zero", "qs_ready", "ps_zero", "s_exp", "os_ready"))
        vs_used, gs_ready = sem("vs_used"), sem("gs_ready")
        stored, y_stored = sem("stored"), sem("y_stored")
        y_turned, y_out_a, y_out_v = (sem(x) for x in ("y_turned", "y_out_a", "y_out_v"))

        def slot(u):
            return slots[u % 4]

        def aux(name):
            return slot(pl.aux[name][1])

        def flat(s):
            return s[:, :, :].rearrange("p a b -> p (a b)")

        def eight(s):
            return flat(s).rearrange("p (t c) -> p t c", c=P)

        def halves(ap):
            return ap.rearrange("p (a b) -> p a b", a=2)

        def wait_aux(eng, name):
            eng.wait_ge(filled, pl.aux[name][0] + 1)

        def wait_slot(pe, u, plus=0):
            if u >= 4:
                pe.wait_ge(slot_free[u % 4], u // 4 + plus)

        def wait_use_freed(eng, u):
            eng.wait_ge(slot_free[u % 4], u // 4 + 1)

        def wait_freed(eng, name):
            wait_use_freed(eng, pl.aux[name][1])

        def free(ins, u):
            ins.then_inc(slot_free[u % 4], 1)

        def free_aux(ins, name):
            free(ins, pl.aux[name][1])

        VECTORS = ([(8 * k, 8, a[name].rearrange("l (t p) -> (l t) p", p=P)) for k, name in enumerate(GAINS)]
                   + [(CV0 + 4 * k, 4, a[name].rearrange("l (t p) -> (l t) p", p=P))
                      for k, name in enumerate(("conv_b", "conv_ln_g", "conv_ln_b"))])

        mix_in_cols = [1536, 1024, 1792, 1280, 512, 768, 0, 256]
        mix_in = [("mix_w_in", c) for c in mix_in_cols]
        keys = [("xattn_w_k", c * 256) for c in range(4)]
        between = (mix_in[0:4] + keys[0:1] + mix_in[4:5] + keys[1:2] + mix_in[5:8] + keys[2:4]
                   + [("xattn_w_v", c * 256) for c in range(4)]
                   + [("mix_w_out", c * 256) for c in range(4)]
                   + [("xattn_w_q", c * 256) for c in range(4)] + [("xattn_w_o", c * 256) for c in range(4)])
        def static_slab(s):
            name, c = between[s - pl.base["glu0"][0] // 2]
            return w2[name].rearrange("(t p) c -> p t c", p=P)[:, :, c:c + 256]

        KV = [j for name, count in (("k0", 2), ("k2", 2), ("k4", 4), ("v0", 6), ("v6", 2))
              for j in range(pl.base[name][0], pl.base[name][0] + count)]

        def is_kv(J):
            return J in KV

        def prepared(J):
            return J - sum(j < J for j in KV)

        def two_before(J):
            J -= 2
            while is_kv(J):
                J -= 2
            return J

        def two_behind(J):
            J += 2
            while is_kv(J):
                J += 2
            return J

        def per_body(b, j, per_block, per_pair):
            return b * per_block + j * per_pair

        block = ctx.enter_context(nc.Block())

        @block.sync
        def _(sp):
            def load_slab(s, src, b=0, j=0):
                if not (s < RAW and isinstance(b, int) and isinstance(j, int) and b + j == 0):
                    before = 2 * (s - RAW)
                    if is_kv(before):
                        sp.wait_ge(job_done, before + 2)
                    else:
                        sp.wait_ge(wlo, prepared(before) + 2 + per_body(b, j, JOBS_PER_BLOCK, 8))
                sp.dma_start(raw[:, s % RAW], src).then_inc(loaded[s % RAW], 16)

            def load_static(name, count):
                s0 = pl.base[name][0] // 2
                for s in range(s0, s0 + count):
                    load_slab(s, static_slab(s))

            def load_ffn(name):
                s0 = pl.base[name][0] // 2
                gate, up = (w2[f"{name}_w_{x}"].rearrange("(t p) c -> p t c", p=P) for x in ("gate", "up"))
                down = w2[f"{name}_w_down"].rearrange("(b t p) c -> p b t c", p=P, t=KT)

                def gate_up(b, j):
                    for i in range(4):
                        w = up if i % 2 else gate
                        load_slab(s0 + i, w[:, :, ds(b * D + j * 512 + 256 * (i // 2), 256)], b, j)

                def down_slabs(b):
                    for i in range(4):
                        src = down[:, ds(b, 1), :, 256 * i:256 * i + 256].rearrange("p o t c -> p (o t) c")
                        load_slab(s0 + 8 + i, src, b)

                gate_up(0, 0)
                if name == "ffn1":
                    for i in range(TT):
                        wait_freed(sp, f"x{i}")
                    sp.dma_start(memraw[:, :, :], a["mem_prompt"].rearrange("b (t p) d -> p (b t) d", p=P))\
                        .then_inc(ld_mem, 16)
                gate_up(0, 1)
                down_slabs(0)
                with sp.Fori(1, BLOCKS) as b:
                    with sp.Fori(0, 2) as j:
                        gate_up(b, j)
                    down_slabs(b)

            for i in range(4):
                sp.dma_start(xin[:, i], x_p[i * P:(i + 1) * P, :]).then_inc(ld_x[i], 16)
            sp.dma_start(xin[0:NB * DEC, 4], x_s).then_inc(ld_xs, 16)
            sp.dma_start(wsr[:, :, :], a["sgu_w_s"].rearrange("l h i j -> i (l h) j")).then_inc(ld_ws, 16)
            sp.wait_ge(ld_small, 16 * 6)
            load_ffn("ffn1")
            load_static("glu0", 28)
            load_ffn("ffn2")
            for i in range(4):
                sp.wait_ge(y_out_a, i + 1)
                sp.dma_start(y_prompt[0, i * P:(i + 1) * P, 0:512], ytok[:, i, 0:512]).then_inc(y_stored, 16)
            for i in range(4):
                if i % 2:
                    sp.wait_ge(y_out_v, i // 2 + 1)
                else:
                    sp.wait_ge(y_out_a, 4 + i // 2 + 1)
                sp.dma_start(y_prompt[0, i * P:(i + 1) * P, 512:D], ytok[:, i, 512:D]).then_inc(y_stored, 16)
            sp.wait_ge(y_out_a, 7)
            sp.dma_start(y_sample.rearrange("b s d -> (b s) d"), ytok[0:NB * DEC, 4]).then_inc(y_stored, 16)
            sp.wait_ge(y_stored, 16 * 9)
            sp.wait_ge(stored, 16 * 5)
            sp.wait_ge(k_stored, 16)
            sp.wait_ge(v_stored, 16)

        @block.gpsimd
        def _(pool):
            nc.gpsimd.memset(epst[:, 1:2], 4.0 * EPS).then_inc(eps_set, 1)
            nc.gpsimd.memset(epst[:, 2:3], EPS * (D // HEADS)).then_inc(eps_set, 1)
            nc.gpsimd.memset(epst[:, 0:1], EPS).then_inc(eps_set, 1)
            nc.gpsimd.memset(ident[:, :], 0.0).then_inc(id_set, 1)
            nc.gpsimd.memset(ones[:, :], 1.0).then_inc(const_set, 1)
            pool.wait_ge(id_set, 1)
            nc.gpsimd.affine_select(out=ident[:, :], in_=ident[:, :], compare_op=ALU.not_equal, fill=1.0, base=0,
                                    pattern=[[-1, P]], channel_multiplier=1).then_inc(id_set, 1)
            for row, rows, src in VECTORS[6:]:
                pool.dma_start(graw[row:row + rows, :], src).then_inc(ld_rest, 16)
            pool.dma_start(cwraw[:, :], a["conv_w"].rearrange("l k c -> (l k) c")).then_inc(ld_cw, 16)
            pool.dma_start(bsb[:, :, :], a["sgu_b_s"].partition_broadcast(P).rearrange("p l h i -> p (l h) i")).then_inc(ld_bs, 16)
            nc.gpsimd.memset(bd[:, :, :], 0.0).then_inc(bd_zero, 1)
            wait_freed(pool, "spatial")
            nc.gpsimd.affine_select(out=wsT[:, :, :], in_=wsT[:, :, :], compare_op=ALU.is_ge, fill=0.0, base=0,
                                    pattern=[[0, 4], [1, P]], channel_multiplier=-1).then_inc(masked, 1)
            pool.wait_ge(masked, 1)
            pool.wait_ge(bd_zero, 1)
            for b in range(NB):
                o = slice(b * DEC, (b + 1) * DEC)
                pool.dma_start(bd[o, :, o], wsT[0:DEC, :, 0:DEC]).then_inc(ld_bd, 16)
            for name in ("gains", "convw", "spatial"):
                wait_freed(pool, name)
            nc.gpsimd.memset(f[:, :, :], 0.0).then_inc(f_zero, 1)
            for i in range(TT):
                wait_freed(pool, f"x{i}")
            nc.gpsimd.memset(glu[:, :, 0:LEFT], 0.0).then_inc(glu_zero, 1)
            pool.wait_ge(job_done, pl.base["glu0"][0])
            pool.dma_start(straw[:, :, :], a["state_conv"].rearrange("l (g b) k c -> (b k) (l g) c", g=2)).then_inc(ld_st, 16)
            pool.dma_start(lng[:, :], a["sgu_ln_g"].partition_broadcast(P).rearrange("p l c -> p (l c)")).then_inc(ld_ln, 16)
            pool.dma_start(lnb[:, :], a["sgu_ln_b"].partition_broadcast(P).rearrange("p l c -> p (l c)")).then_inc(ld_ln, 16)
            pool.dma_start(cs_s[0, :, 0:LEFT - DEC, :], a["state_conv"][0, :, DEC:LEFT, :]).then_inc(stored, 16)
            pool.wait_ge(ld_ln, 32)
            for i in range(TT):
                m = token_tile(i)[1]
                pool.wait_ge(sv_n, i + 1)
                nc.gpsimd.tensor_tensor(sv[0:m, i], sv[0:m, i], lng[0:m, :], ALU.mult).then_inc(sv_g, 1)
                pool.wait_ge(sv_g, i + 1)
                nc.gpsimd.tensor_tensor(sv[0:m, i], sv[0:m, i], lnb[0:m, :], ALU.add).then_inc(sv_b, 1)
            pool.wait_ge(sv_b, TT)
            pool.dma_start(cv_p[0, 0, :, :], sv[:, 3]).then_inc(stored, 16)
            pool.dma_start(cv_s.rearrange("l b s c -> (l b s) c"), sv[0:NB * DEC, 4]).then_inc(stored, 16)
            for name, dst, rows, done in (("ktok", mem_k_o, ktok, k_stored), ("vtok", mem_v_o, vtok, v_stored)):
                for t in range(MT):
                    wait_freed(pool, f"{name}{t}")
                pool.dma_start(dst.rearrange("l b (t p) h d -> p (l b t) (h d)", p=P), rows[:, :, :]).then_inc(done, 16)
            wait_freed(pool, "glup")
            pool.dma_start(cs_p[0, 0, :, :], osm[64:64 + LEFT, :]).then_inc(stored, 16)
            wait_freed(pool, "glus")
            pool.dma_start(cs_s[0, :, LEFT - DEC:LEFT, :], osm[0:NB * DEC, :]).then_inc(stored, 16)
            pool.wait_ge(stored, 16 * 5)
            for b in range(NB):
                if b < 3:
                    pool.wait_ge(job_done, pl.base["out"][0] + 1)
                elif b == 3:
                    pool.wait_ge(job_done, pl.base["out"][0] + 8)
                else:
                    wait_aux(pool, f"ktb{b - 4}")
                dst = kring[:, b % 4] if b % 4 < 3 else k3[:, :, :]
                pool.dma_start(dst, ck[b].rearrange("(t p) d -> p t d", p=P)).then_inc(ld_k[b % 4], 16)
                if b == 3:
                    nc.gpsimd.memset(qs[:, :, :, :], 0.0).then_inc(qs_zero, 1)
            for b in range(NB):
                if b < 3:
                    wait_aux(pool, f"ktb{4 + b}")
                elif b < 5:
                    wait_aux(pool, f"ss{3 + b}")
                    if b == 4:
                        nc.gpsimd.memset(ps[:, :, :, :], 0.0).then_inc(ps_zero, 1)
                else:
                    pool.wait_ge(vs_used, b - 5 + 1)
                dst = vx[:, b - 3] if 3 <= b < 5 else kring[:, b % 5]
                pool.dma_start(dst, cv[b].rearrange("(t p) d -> p t d", p=P)).then_inc(ld_v[b % 5], 16)
            pool.wait_ge(sums["post3"]["done"], KT)
            nc.gpsimd.memset(f[:, :, :], 0.0).then_inc(f_zero, 1)

        @block.scalar
        def _(act):
            def prepare(J, b=0, j=0):
                if is_kv(J) or isinstance(b, int) and J + JOBS_PER_BLOCK * b >= pl.jobs:
                    return
                s = J // 2
                act.wait_ge(loaded[s % RAW], 16 * (s // RAW + 1) + per_body(b, j, 16 * 12 // RAW, 16 * 4 // RAW))
                if J >= 2:
                    act.wait_ge(job_done, two_before(J) + 1 + per_body(b, j, JOBS_PER_BLOCK, 8))
                nc.scalar.activation(wp[:, J % 2, 0], raw[:, s % RAW, :, (J % 2) * P:(J % 2 + 1) * P], ACT.Copy)\
                    .then_inc(whi, 1)

            def copy_job(name, i, dst, cols=None):
                J, u = pl.base[name][0] + i, pl.base[name][1] + i
                if not is_kv(J):
                    prepare(two_behind(J))
                elif name == "v6":
                    prepare(J + 2)
                act.wait_ge(job_done, J + 1)
                src = slot(u)[:, 0, 0:cols] if cols else slot(u)[:, :, 0:HALF]
                free(nc.scalar.activation(dst if cols else halves(dst), src, ACT.Copy), u)

            def square(name, t, src):
                if t >= 2:
                    act.wait_ge(sums[name]["added"], max(t - 2, 1))
                nc.scalar.activation(sq[:, t % 2] if src.ndim == 2 else halves(sq[:, t % 2]), src, ACT.Square)\
                    .then_inc(sums[name]["squared"], 1)

            def root(name, n_features, kind="plain"):
                k, col = ROOTS[kind]
                wait_aux(act, name)
                free_aux(nc.scalar.activation(halves(R[:, :]), aux(name)[:, :, 0:HALF], ACT.Sqrt, scale=k / n_features,
                                              bias=epst[:, col:col + 1]), name)

            def warm(func):
                i = warmed[0] = warmed[0] + 1
                nc.scalar.activation(small[:, 90 + i:91 + i], epst[:, 0:1], func)

            warmed = [0]

            def pre_norm(post, pre, g, job, kind="plain"):
                for t in range(KT):
                    if post:
                        act.wait_ge(sums[post]["done"], t + 1)
                    elif t in (0, 3):
                        prepare(t // 3)
                    nc.scalar.activation(n[:, 0, t], h[:, t], ACT.Copy, scale=gain[g][t]).then_inc(sums[pre]["hi"], 1)
                    if t >= 2:
                        act.wait_ge(sums[pre]["added"], t // 2)
                    nc.scalar.activation(sq[:, t % 2], h[:, t], ACT.Square).then_inc(sums[pre]["squared"], 1)
                prepare(pl.base[job][0] + 2)
                root(pre, D, kind)

            def gates(name, i, func, b=0, j=0, ahead=False):
                J, u = pl.base[name][0] + i, pl.base[name][1] + i
                for e in range(2):
                    if e or not ahead:
                        prepare(J + e + 2, b, j)
                    act.wait_ge(slot_free[(u + e) % 4], (u + e) // 4 + 1 + per_body(b, j, 6, 2))
                    nc.scalar.activation(sil[:, e], sil[:, e], func).then_inc(gate_out, 1)

            def ffn(name, post, beside=None):
                J0, u0 = pl.base[name]

                def gate_up(b, j, ahead=False):
                    for i in (0, 4):
                        gates(name, i, ACT.Silu, b, j, ahead and i == 0)
                        for e in range(2):
                            prepare(J0 + i + e + 4, b, j)
                            vu = u0 + i + 2 + e
                            act.wait_ge(slot_free[vu % 4], vu // 4 + 1 + per_body(b, j, 6, 2))
                            nc.scalar.activation(mid[:, 0, ds(j * 4 + (i // 2 + e), 1)].rearrange("p o t -> p (o t)"),
                                                 sil[:, e], ACT.Copy).then_inc(mid_hi, 1)

                def down(b):
                    for i in range(KT):
                        prepare(J0 + 16 + i + 2, b)

                gate_up(0, 0, True)
                gate_up(0, 1)
                if beside:
                    beside()
                down(0)
                with act.Fori(1, BLOCKS - 1) as b:
                    with act.Fori(0, 2) as j:
                        gate_up(b, j)
                    down(b)
                with act.Fori(0, 2) as j:
                    gate_up(BLOCKS - 1, j)
                for i in range(KT):
                    prepare(J0 + 16 + i + 2, BLOCKS - 1)
                    wait_use_freed(act, u0 + (BLOCKS - 1) * JOBS_PER_BLOCK + 16 + i)
                    square(post, i, f[:, i])
                    if i == 0:
                        warm(ACT.Sqrt)
                root(post, D, "half")

            act.wait_ge(eps_set, 3)
            warm(ACT.Copy)
            for row, rows, src in VECTORS[:6]:
                act.dma_start(graw[row:row + rows, :], src).then_inc(ld_small, 16)
            for i in range(TT):
                o, m = token_tile(i)
                if i % 2 == 0:
                    wait_aux(act, f"x{i}")
                    free_aux(nc.scalar.activation(h[:, :, o:o + m], eight(aux(f"x{i}"))[:, :, 0:m], ACT.Copy), f"x{i}")
                if i == 1:
                    wait_aux(act, "gains")
                    free_aux(nc.scalar.activation(gvec[:, :], aux("gains")[:, 0, 0:84], ACT.Copy), "gains")
            for i in (1, 3):
                wait_freed(act, f"x{i}")
            wait_freed(act, "x4")
            wait_aux(act, "convw")
            free_aux(nc.scalar.activation(convw[:, :, 0:TAPS], eight(aux("convw"))[:, 0:CT, 0:TAPS], ACT.Copy), "convw")
            wait_aux(act, "spatial")
            free_aux(nc.scalar.activation(wsT[:, :, :], eight(aux("spatial"))[:, 0:4, :], ACT.Copy), "spatial")
            pre_norm(None, "pre1", "ffn1_g_pre", "ffn1")

            def memory_roots():
                act.wait_ge(ld_mem, 16)
                for t in range(MT):
                    if t:
                        act.wait_ge(mem_sq, t)
                    nc.scalar.activation(memjunk, memraw[:, t], ACT.Square, accum_out=mss[:, t:t + 1]).then_inc(mem_sq, 1)
                act.wait_ge(mem_sq, MT)
                nc.scalar.activation(mss, mss, ACT.Sqrt, scale=1.0 / D, bias=epst[:, 0:1]).then_inc(mem_rt, 1)
            ffn("ffn1", "post1", memory_roots)
            for t in range(MT):
                wait_aux(act, f"mem{t}")
                for kt in range(KT):
                    ins = nc.scalar.activation(memT[:, kt, t * P:(t + 1) * P], eight(aux(f"mem{t}"))[:, kt, :], ACT.Copy,
                                               scale=gain["mem_g"][kt])
                free_aux(ins, f"mem{t}")
            pre_norm("post1", "pre2", "mix_g_pre", "glu0")
            gates("glu0", 0, ACT.Sigmoid, ahead=True)
            for e in range(2):
                prepare(pl.base["glu0"][0] + 4 + e)
            for r in range(2):
                wait_aux(act, f"state{r}")
                if r == 0:
                    act.wait_ge(glu_zero, 1)
                for ct in range(CT):
                    dst = glu[:, ct, GLU_S + 38 * 4 * r:GLU_S + 38 * 4 * (r + 1)].rearrange("p (b k) -> p b k", b=4)[:, :, 0:LEFT]
                    src = aux(f"state{r}")[:, 0, ct * P:ct * P + 120].rearrange("p (b k) -> p b k", b=4)
                    ins = nc.scalar.activation(dst, src, ACT.Copy)
                free_aux(ins, f"state{r}")
            gates("glu1", 0, ACT.Sigmoid)
            for e in range(2):
                prepare(two_behind(pl.base["glu1"][0] + 2 + e))
            wait_aux(act, "rcol")
            ins = nc.scalar.activation(rc[:, 0:4].unsqueeze(2), aux("rcol")[:, 0, :].rearrange("p (t c) -> p t c", c=P)[:, :, 0:1],
                                       ACT.Copy)
            free_aux(nc.scalar.activation(rc[0:NB * DEC, 4:5], aux("rcol")[0:NB * DEC, 1, 0:1], ACT.Copy), "rcol")
            def v_turned(t):
                wait_aux(act, f"vt{t}")
                if t == 0:
                    wait_freed(act, "rcol")
                for i in range(TT):
                    m = token_tile(i)[1]
                    ins = nc.scalar.activation(sv[0:m, i, t * P:(t + 1) * P], flat(aux(f"vt{t}"))[0:m, i * P:(i + 1) * P],
                                               ACT.Copy, scale=rc[0:m, i:i + 1])
                free_aux(ins, f"vt{t}")

            for t in range(2):
                copy_job("k0", t, kT[:, t], MEM)
            for t in range(4):
                if t >= 2:
                    wait_aux(act, f"vt{t - 2}")
                copy_job(f"sv{t}", 0, sq[:, t % 2])
                if t:
                    v_turned(t - 1)
                if t == 1:
                    for e in range(2):
                        copy_job("k2", e, kT[:, 2 + e], MEM)
            prepare(pl.base["u0"][0] + 2)
            v_turned(3)
            prepare(pl.base["u1"][0] + 2)
            for e in range(2, 4):
                wait_use_freed(act, pl.base["glu1"][1] + e)
            for ct in range(CT):
                src = glu[:, ct, GLU_S:GLU_W].rearrange("p (b k) -> p b k", b=NB)[:, :, LEFT:LEFT + DEC]
                ins = nc.scalar.activation(gsm[:, ct].rearrange("p (b k) -> p b k", b=NB), src, ACT.Copy)
            ins.then_inc(gs_ready, 1)
            copy_job("k4", 0, kT[:, 4], MEM)
            act.wait_ge(sv_mv, TT)
            nc.scalar.activation(vrs[:, 0:4], bag[:, 1:8:2], ACT.Sqrt, bias=epst[:, 0:1])
            nc.scalar.activation(vrs[0:64, 4:5], bag[0:64, 9:10], ACT.Sqrt, bias=epst[0:64, 0:1]).then_inc(sv_rt, 1)
            for t in range(1, 4):
                copy_job("k4", t, kT[:, 4 + t], MEM)
            for t in range(6):
                copy_job("v0", t, vT[:, t], MEM)
            for t in range(CT):
                if t < CT - 1:
                    act.wait_ge(cc_ready, t + 1)
                else:
                    wait_freed(act, "cmean")
                if t >= 2:
                    act.wait_ge(sums["cvar"]["summed"], t - 1)
                nc.scalar.activation(sq[:, t % 2], f[:, 4 + t], ACT.Square).then_inc(sums["cvar"]["squared"], 1)
            for t in range(4):
                if t == 1:
                    root("cvar", CW)
                act.wait_ge(gated, t + 1)
                nc.scalar.activation(mid[:, 0, t], sil[:, t % 2], ACT.Copy).then_inc(mid_hi, 1)
            for t in range(2):
                copy_job("v6", t, vT[:, 6 + t], MEM)
            for t in range(CT):
                act.wait_ge(cn_ready, t + 1)
                nc.scalar.activation(f[:, 4 + t], f[:, 4 + t], ACT.Silu, scale=clg[t], bias=clb[t]).then_inc(act_b, 1)
            for t in range(CT):
                act.wait_ge(act_b, t + 1)
                nc.scalar.activation(mid[:, 0, 4 + t], f[:, 4 + t], ACT.Copy).then_inc(mid_hi, 1)
            def rows_turned(name, rows):
                for t in range(MT):
                    wait_aux(act, f"{name}{t}")
                    free_aux(nc.scalar.activation(rows[:, t], flat(aux(f"{name}{t}")), ACT.Copy), f"{name}{t}")

            rows_turned("ktok", ktok)

            def project(job, post):
                for t in range(KT):
                    J, u = pl.base[job][0] + t, pl.base[job][1] + t
                    prepare(J + 2)
                    act.wait_ge(job_done, J + 1)
                    square(post, t, slot(u)[:, :, 0:HALF])
                    if t == 0:
                        warm(ACT.Sqrt)
                    free(nc.scalar.activation(halves(f[:, t]), slot(u)[:, :, 0:HALF], ACT.Copy), u)
                root(post, D)

            project("out", "post2")
            rows_turned("vtok", vtok)
            wait_aux(act, "glup")
            free_aux(nc.scalar.activation(osm[64:64 + LEFT, :], aux("glup")[0:LEFT, 0, :], ACT.Copy), "glup")
            wait_aux(act, "glus")
            free_aux(nc.scalar.activation(osm[0:NB * DEC, :], aux("glus")[0:NB * DEC, 0, :], ACT.Copy), "glus")
            act.wait_ge(k_stored, 16)
            pre_norm("post2", "pre3", "xattn_g_pre", "q", "query")
            warm(ACT.Exp)
            act.wait_ge(qs_zero, 1)
            for t in range(KT):
                if t:
                    prepare(pl.base["q"][0] + t + 2)
                wait_use_freed(act, pl.base["q"][1] + t)
                c = t // 2 * DEC
                nc.scalar.activation(qs[:, :, t, c:c + DEC], f[:, t, SEQ:T].rearrange("p (b k) -> p b k", b=NB), ACT.Copy)\
                    .then_inc(qs_ready, 1)

            def keys_turned(b):
                wait_aux(act, f"kta{b}")
                free_aux(nc.scalar.activation(kts[:, b % 2, :, 0:P], eight(aux(f"kta{b}")), ACT.Copy), f"kta{b}")

            def probs_turned(i):
                wait_aux(act, f"pt{i}")
                free_aux(nc.scalar.activation(pT[:, :, i * P:(i + 1) * P], eight(aux(f"pt{i}")), ACT.Copy), f"pt{i}")

            for i in range(4):
                act.wait_ge(mx_ready, i + 1)
                if i >= 2:
                    wait_aux(act, f"pt{i - 2}")
                for hd in range(HEADS):
                    ins = nc.scalar.activation(prob[:, i % 2, hd], aux(f"sc{i}")[:, hd // 2, (hd % 2) * MEM:(hd % 2 + 1) * MEM],
                                               ACT.Exp, bias=mx[:, 4 * i + hd:4 * i + hd + 1],
                                               accum_out=sm[:, 4 * i + hd:4 * i + hd + 1])
                free_aux(ins, f"sc{i}")
                for b in (2 * i, 2 * i + 1):
                    if b >= 2:
                        wait_aux(act, f"ss{b - 2}")
                    keys_turned(b)
                if i:
                    probs_turned(i - 1)
            probs_turned(3)

            def out_high(o):
                wait_aux(act, f"pv{o}")
                ins = nc.scalar.activation(mid[:, 0, o, 0:SEQ], aux(f"pv{o}")[:, 0, :], ACT.Copy)
                ins.then_inc(mid_hi, 1)

            for r in range(2):
                act.wait_ge(smx_ready, r + 1)
                nc.scalar.activation(psm[:, r], psm[:, r], ACT.Exp, bias=smx[:, r:r + 1],
                                     accum_out=ssm[:, r:r + 1]).then_inc(s_exp, 1)
            for o in range(3):
                out_high(o)
            wait_aux(act, "sprob")
            act.wait_ge(ps_zero, 1)
            for t in range(MT):
                ins = nc.scalar.activation(ps[:, t].rearrange("p h (b c) -> p h b c", b=NB)[:, :, :, 0:DEC],
                                           aux("sprob")[:, t, 0:MEM].rearrange("p (b h c) -> p h b c", b=NB, h=HEADS), ACT.Copy)
            free_aux(ins, "sprob")
            for o in range(3, 8):
                out_high(o)
            wait_aux(act, "pvs")
            nc.scalar.activation(os_[:, 0:512], aux("pvs")[0:NB * DEC, 0, :], ACT.Copy).then_inc(os_ready, 1)
            wait_aux(act, "pvt")
            ins = nc.scalar.activation(mid[:, 0, :, SEQ:T], aux("pvt")[:, 0, :].rearrange("p (o t) -> p o t", o=KT), ACT.Copy)
            ins.then_inc(mid_hi, 1)
            project("o", "post3")
            pre_norm("post3", "pre4", "ffn2_g_pre", "ffn2")
            ffn("ffn2", "post4")
            for i in range(4):
                act.wait_ge(y_turned, i + 1)
                nc.scalar.activation(ytok[:, i, 0:512], aux(f"y{i}")[:, 0, :], ACT.Copy).then_inc(y_out_a, 1)
            for i in (0, 2):
                act.wait_ge(y_turned, 4 + i + 1)
                nc.scalar.activation(ytok[:, i, 512:D], aux(f"y{i}")[:, 1, :], ACT.Copy).then_inc(y_out_a, 1)
            act.wait_ge(y_turned, 9)
            nc.scalar.activation(ytok[0:NB * DEC, 4], flat(aux("y4"))[0:NB * DEC, :], ACT.Copy).then_inc(y_out_a, 1)

        @block.vector
        def _(dve):
            V = nc.vector

            def prepare(J, b=0, j=0):
                if is_kv(J) or isinstance(b, int) and J + JOBS_PER_BLOCK * b >= pl.jobs:
                    return
                s = J // 2
                dve.wait_ge(whi, prepared(J) + 1 + per_body(b, j, JOBS_PER_BLOCK, 8))
                V.tensor_tensor(wp[:, J % 2, 1], raw[:, s % RAW, :, (J % 2) * P:(J % 2 + 1) * P],
                                wp[:, J % 2, 0].bitcast(F32), ALU.subtract).then_inc(wlo, 1)

            def add_square(name, t):
                if t == 0 or t == KT - 1:
                    return
                dve.wait_ge(sums[name]["squared"], t + 1)
                if t > 1:
                    dve.wait_ge(sums[name]["added"], t - 1)
                V.tensor_tensor(acc[:, :], sq[:, 0] if t == 1 else acc[:, :], sq[:, t % 2], ALU.add)\
                    .then_inc(sums[name]["added"], 1)

            def reciprocal(name):
                wait_freed(dve, name)
                V.reciprocal(R[:, :], R[:, :]).then_inc(sums[name]["recip"], 1)
                dve.wait_ge(sums[name]["recip"], 1)

            def low_part(pre, g, t):
                dve.wait_ge(sums[pre]["hi"], t + 1)
                V.scalar_tensor_tensor(out=n[:, 1, t], in0=h[:, t], scalar=gain[g][t], in1=n[:, 0, t].bitcast(F32),
                                       op0=ALU.mult, op1=ALU.subtract).then_inc(sums[pre]["ready"], 1)
                if t % 2:
                    dve.wait_ge(sums[pre]["squared"], t + 1)
                    if t > 1:
                        dve.wait_ge(sums[pre]["summed"], t // 2)
                    V.tensor_tensor(acc[:, :], sq[:, 0], sq[:, 1], ALU.add).then_inc(sums[pre]["added"], 1)

            def post_norm(post, g, pre=None, gpre=None):
                reciprocal(post)
                for t in range(KT + 2):
                    if t < KT:
                        V.scalar_tensor_tensor(out=f[:, t], in0=f[:, t], scalar=gain[g][t], in1=R[:, :],
                                               op0=ALU.mult, op1=ALU.mult).then_inc(sums[post]["scaled"], 1)
                    if 1 <= t <= KT:
                        dve.wait_ge(sums[post]["scaled"], t)
                        V.tensor_tensor(h[:, t - 1], h[:, t - 1], f[:, t - 1], ALU.add).then_inc(sums[post]["done"], 1)
                    if pre and t >= 2:
                        low_part(pre, gpre, t - 2)

            def pre_sum(pre, job):
                prepare(pl.base[job][0] + 2)
                reciprocal(pre)

            def take_scaled(dst, J, u, b=0, j=0):
                dve.wait_ge(job_done, J + 1 + per_body(b, j, JOBS_PER_BLOCK, 8))
                free(V.tensor_tensor(halves(dst), slot(u)[:, :, 0:HALF], halves(R[:, :]), ALU.mult), u)

            def scale_gate(name, i, e, b=0, j=0):
                dve.wait_ge(gate_out, GATE0[name] + i // 2 + e + 1 + per_body(b, j, KT, 4))
                V.tensor_tensor(sil[:, e], sil[:, e], R[:, :], ALU.mult).then_inc(gate_scaled, 1)

            def ffn(name, post, beside=None):
                J0, u0 = pl.base[name]

                def gate_up(b, j, first=False, ahead=False):
                    for i in (0, 4):
                        for e in range(2):
                            if i or not first:
                                dve.wait_ge(mid_ready, MID0[name] + i // 2 + e - 1 + per_body(b, j, KT, 4))
                            take_scaled(sil[:, e], J0 + i + e, u0 + i + e, b, j)
                            if i or e or not ahead:
                                prepare(J0 + i + e + 2, b, j)
                        for e in range(2):
                            scale_gate(name, i, e, b, j)
                        for e in range(2):
                            J, u = J0 + i + 2 + e, u0 + i + 2 + e
                            tile = ds(j * 4 + (i // 2 + e), 1)
                            dve.wait_ge(gate_scaled, GATE0[name] + i // 2 + e + 1 + per_body(b, j, KT, 4))
                            dve.wait_ge(job_done, J + 1 + per_body(b, j, JOBS_PER_BLOCK, 8))
                            free(V.tensor_tensor(halves(sil[:, e]), slot(u)[:, :, 0:HALF], halves(sil[:, e]), ALU.mult), u)
                            prepare(J + 2, b, j)
                            dve.wait_ge(mid_hi, HI0[name] + i // 2 + e + 1 + per_body(b, j, KT, 4))
                            V.tensor_tensor(mid[:, 1, tile].rearrange("p o t -> p (o t)"), sil[:, e],
                                            mid[:, 0, tile].rearrange("p o t -> p (o t)").bitcast(F32), ALU.subtract)\
                                .then_inc(mid_ready, 1)

                def down(b, last=False):
                    for i in range(KT):
                        J, u = J0 + 16 + i, u0 + 16 + i
                        dve.wait_ge(job_done, J + 1 + per_body(b, 0, JOBS_PER_BLOCK, 8))
                        dve.wait_ge(slot_free[(u0 + 15) % 4], (u0 + 15) // 4 + 1 + per_body(b, 0, 6, 2))
                        free(V.tensor_tensor(halves(f[:, i]), slot(u)[:, :, 0:HALF], halves(f[:, i]), ALU.add), u)
                        prepare(J + 2, b)
                        if last:
                            add_square(post, i)

                gate_up(0, 0, name == "ffn1", True)
                gate_up(0, 1)
                down(0)
                if beside:
                    beside()
                with dve.Fori(1, BLOCKS - 1) as b:
                    with dve.Fori(0, 2) as j:
                        gate_up(b, j)
                    down(b)
                with dve.Fori(0, 2) as j:
                    gate_up(BLOCKS - 1, j)
                down(BLOCKS - 1, True)

            for i in (1, 3):
                o, m = token_tile(i)
                wait_aux(dve, f"x{i}")
                free_aux(V.tensor_copy(h[:, :, o:o + m], eight(aux(f"x{i}"))[:, :, 0:m]), f"x{i}")
            for i in range(TT):
                wait_freed(dve, f"x{i}")
            wait_freed(dve, "gains")
            for t in range(KT):
                if t in (0, 3):
                    prepare(t // 3)
                low_part("pre1", "ffn1_g_pre", t)
            pre_sum("pre1", "ffn1")

            def memory_rows():
                dve.wait_ge(mem_rt, 1)
                V.reciprocal(mss, mss).then_inc(mem_rs, 1)
                dve.wait_ge(mem_rs, 1)
                for t in range(MT):
                    V.tensor_scalar(memraw[:, t], memraw[:, t], mss[:, t:t + 1], None, ALU.mult).then_inc(mem_n, 1)
            dve.wait_ge(f_zero, 1)
            ffn("ffn1", "post1", memory_rows)
            post_norm("post1", "ffn1_g_post", "pre2", "mix_g_pre")
            pre_sum("pre2", "glu0")

            def glu_gate(g, e):
                J, u = pl.base[f"glu{g}"]
                take_scaled(sil[:, e], J + e, u + e)
                if g or e:
                    prepare(J + e + 2)

            def glu_value(g, e):
                J, u = pl.base[f"glu{g}"]
                ct = 2 * g + e
                src = slot(u + 2 + e)
                dve.wait_ge(gate_scaled, GATE0[f"glu{g}"] + e + 1)
                dve.wait_ge(job_done, J + 2 + e + 1)
                V.tensor_tensor(glu[:, ct, LEFT:LEFT + HALF], src[:, 0, 0:HALF], sil[:, e, 0:HALF], ALU.mult)
                rest = SEQ - HALF
                V.tensor_tensor(glu[:, ct, LEFT + HALF:LEFT + SEQ], src[:, 1, 0:rest], sil[:, e, HALF:SEQ], ALU.mult)
                dst = glu[:, ct, GLU_S:GLU_W].rearrange("p (b k) -> p b k", b=NB)[:, :, LEFT:LEFT + DEC]
                free(V.tensor_tensor(dst, src[:, 1, rest:HALF].rearrange("p (b k) -> p b k", b=NB),
                                     sil[:, e, SEQ:T].rearrange("p (b k) -> p b k", b=NB), ALU.mult), u + 2 + e)
                prepare(two_behind(J + 2 + e))

            def scale_gates(g):
                for e in range(2):
                    scale_gate(f"glu{g}", 0, e)

            def conv(ct, beside, first=0, last=TAPS):
                wait_use_freed(dve, pl.base[f"glu{ct // 2}"][1] + 2 + ct % 2)
                samples = glu[:, ct, GLU_S:GLU_W].rearrange("p (b k) -> p b k", b=NB)
                for k in range(first, last):
                    for step in beside.get(k, ()):
                        step()
                    done = 2 * (ct * TAPS + k)
                    w = convw[:, ct, k:k + 1]
                    ps_ = [(f[:, 4 + ct, 0:SEQ], glu[:, ct, k:k + SEQ]),
                           (f[:, 4 + ct, SEQ:T].rearrange("p (b k) -> p b k", b=NB), samples[:, :, k:k + DEC])]
                    for e, (dst, src) in enumerate(ps_):
                        if k == 0:
                            V.tensor_scalar(dst, src, w, convb[ct], ALU.mult, ALU.add).then_inc(conv_step, 1)
                        else:
                            dve.wait_ge(conv_step, done - 2 + e + 1)
                            V.scalar_tensor_tensor(out=dst, in0=src, scalar=w, in1=dst, op0=ALU.mult, op1=ALU.add)\
                                .then_inc(conv_step, 1)

            def after(name, i=0):
                return lambda: prepare(two_behind(pl.base[name][0] + i))

            def take_u(t):
                def step():
                    J, u = pl.base[f"u{t}"]
                    take_scaled(f[:, t], J, u)
                    if t < 2:
                        prepare(J + 2)
                return step

            for e in range(2):
                glu_gate(0, e)
            scale_gates(0)
            for e in range(2):
                glu_value(0, e)
            wait_freed(dve, "state1")
            dve.wait_ge(glu_zero, 1)
            wait_freed(dve, "convw")
            conv(0, {3: [lambda: glu_gate(1, 0)], 11: [lambda: glu_gate(1, 1)], 15: [lambda: scale_gates(1)],
                     19: [lambda: glu_value(1, 0)], 27: [lambda: glu_value(1, 1)]})
            conv(1, {7: [after("sv0")], 14: [after("sv1")], 29: [after("sv2")]})
            conv(2, {5: [after("sv3")], 12: [take_u(0)], 19: [take_u(1)], 26: [take_u(2)]})
            conv(3, {2: [take_u(3)]}, 0, 6)
            wait_freed(dve, "vt3")
            for i in range(TT):
                m = token_tile(i)[1]
                V.bn_stats(bst[0:m, 6 * i:6 * i + 6], sv[0:m, i]).then_inc(sv_st, 1)
            for i in range(TT):
                m = token_tile(i)[1]
                dve.wait_ge(sv_st, i + 1)
                V.bn_aggr(bag[0:m, 2 * i:2 * i + 2], bst[0:m, 6 * i:6 * i + 6]).then_inc(sv_mv, 1)
            dve.wait_ge(sv_rt, 1)
            V.reciprocal(vrs[:, 0:4], vrs[:, 0:4])
            V.reciprocal(vrs[0:64, 4:5], vrs[0:64, 4:5]).then_inc(sv_rs, 1)
            dve.wait_ge(sv_rs, 1)
            for i in range(TT):
                m = token_tile(i)[1]
                V.tensor_scalar(sv[0:m, i], sv[0:m, i], bag[0:m, 2 * i:2 * i + 1], vrs[0:m, i:i + 1], ALU.subtract, ALU.mult)\
                    .then_inc(sv_n, 1)
            conv(3, {}, 6)
            wait_aux(dve, "cmean")
            for t in range(CT):
                ins = V.scalar_tensor_tensor(out=halves(f[:, 4 + t]), in0=aux("cmean")[:, :, 0:HALF], scalar=-1.0 / CW,
                                             in1=halves(f[:, 4 + t]), op0=ALU.mult, op1=ALU.add)
                if t < CT - 1:
                    ins.then_inc(cc_ready, 1)
                else:
                    free_aux(ins, "cmean")

            def gated_low(t):
                dve.wait_ge(mid_hi, HI0["mix"] + t + 1)
                V.tensor_tensor(mid[:, 1, t], sil[:, t % 2], mid[:, 0, t].bitcast(F32), ALU.subtract).then_inc(mid_ready, 1)

            dve.wait_ge(ld_bs, 16)
            for t in range(4):
                wait_aux(dve, f"sg{t}")
                if t >= 2:
                    dve.wait_ge(mid_ready, MID0["mix"] + t - 1)
                s = sil[:, t % 2]
                V.tensor_tensor(s[:, 0:SEQ].rearrange("p (c i) -> p c i", c=4), aux(f"sg{t}")[:, 0, :].rearrange("p (c i) -> p c i", c=4),
                                bsb[:, t:t + 1, :].to_broadcast([P, 4, P]), ALU.add)
                free_aux(V.tensor_tensor(s[:, SEQ:T].rearrange("p (b i) -> p b i", b=NB),
                                         aux(f"sg{t}")[:, 1, 0:NB * DEC].rearrange("p (b i) -> p b i", b=NB),
                                         bsb[:, t:t + 1, 0:DEC].to_broadcast([P, NB, DEC]), ALU.add), f"sg{t}")
                wait_freed(dve, f"sg{t}")
                V.tensor_tensor(s, s, f[:, t], ALU.mult).then_inc(gated, 1)
                if t:
                    gated_low(t - 1)
            gated_low(3)
            reciprocal("cvar")
            for t in range(CT):
                V.tensor_tensor(f[:, 4 + t], f[:, 4 + t], R[:, :], ALU.mult).then_inc(cn_ready, 1)
            for t in range(2):
                prepare(pl.base["out"][0] + t)
            for t in range(CT):
                dve.wait_ge(mid_hi, HI0["mix"] + 4 + t + 1)
                V.tensor_tensor(mid[:, 1, 4 + t], f[:, 4 + t], mid[:, 0, 4 + t].bitcast(F32), ALU.subtract)\
                    .then_inc(mid_ready, 1)

            def project(job, post):
                for t in range(KT):
                    prepare(pl.base[job][0] + t + 2)
                    add_square(post, t)

            project("out", "post2")
            post_norm("post2", "mix_g_post", "pre3", "xattn_g_pre")
            pre_sum("pre3", "q")
            for t in range(KT):
                J, u = pl.base["q"]
                take_scaled(f[:, t], J + t, u + t)
                if t:
                    prepare(J + t + 2)

            def keys_turned(b):
                wait_aux(dve, f"ktb{b}")
                free_aux(V.tensor_copy(kts[:, b % 2, :, P:2 * P], eight(aux(f"ktb{b}"))), f"ktb{b}")

            def sample_scores(b):
                wait_aux(dve, f"ss{b}")
                r = b % 4 * 32
                free_aux(V.tensor_copy(psm[r:r + 32, b // 4], aux(f"ss{b}")[0:32, 0, 0:MEM]), f"ss{b}")

            def scale_rows(i):
                c = slice(4 * i, 4 * i + 4)
                wait_freed(dve, f"sc{i}")
                V.reciprocal(sm[:, c], sm[:, c]).then_inc(rs_ready, 1)
                dve.wait_ge(rs_ready, i + 1)
                for hd in range(HEADS):
                    V.tensor_scalar(prob[:, i % 2, hd], prob[:, i % 2, hd], sm[:, 4 * i + hd:4 * i + hd + 1], None, ALU.mult)\
                        .then_inc(p_ready, 1)

            for i in range(4):
                wait_aux(dve, f"sc{i}")
                V.tensor_reduce(mx[:, 4 * i:4 * i + 4], flat(aux(f"sc{i}")).rearrange("p (h m) -> p h m", h=HEADS),
                                AX_X, ALU.max, negate=True).then_inc(mx_ready, 1)
                for b in (2 * i, 2 * i + 1):
                    if b >= 2:
                        wait_aux(dve, f"ss{b - 2}")
                    keys_turned(b)
                    if b % 2 == 0:
                        scale_rows(i)
                    if b:
                        sample_scores(b - 1)
            sample_scores(7)
            for b in range(4, 8):
                wait_freed(dve, f"ss{b}")
            for r in range(2):
                V.tensor_reduce(smx[:, r:r + 1], psm[:, r], AX_X, ALU.max, negate=True).then_inc(smx_ready, 1)
            for r in range(2):
                dve.wait_ge(s_exp, r + 1)
                V.reciprocal(ssm[:, r:r + 1], ssm[:, r:r + 1]).then_inc(srs_ready, 1)
                dve.wait_ge(srs_ready, r + 1)
                V.tensor_scalar(psm[:, r], psm[:, r], ssm[:, r:r + 1], None, ALU.mult).then_inc(sp_ready, 1)
            for o in range(KT):
                dve.wait_ge(mid_hi, HI0["att"] + o + 1)
                free_aux(V.tensor_tensor(mid[:, 1, o, 0:SEQ], aux(f"pv{o}")[:, 0, :], mid[:, 0, o, 0:SEQ].bitcast(F32),
                                         ALU.subtract), f"pv{o}")
            wait_aux(dve, "pvs")
            dve.wait_ge(os_ready, 1)
            free_aux(V.tensor_copy(os_[:, 512:D], aux("pvs")[0:NB * DEC, 1, :]), "pvs")
            dve.wait_ge(mid_hi, HI0["att"] + KT + 1)
            free_aux(V.tensor_tensor(mid[:, 1, :, SEQ:T], aux("pvt")[:, 0, :].rearrange("p (o t) -> p o t", o=KT),
                                     mid[:, 0, :, SEQ:T].bitcast(F32), ALU.subtract), "pvt")
            project("o", "post3")
            post_norm("post3", "xattn_g_post", "pre4", "ffn2_g_pre")
            pre_sum("pre4", "ffn2")
            dve.wait_ge(f_zero, 2)
            ffn("ffn2", "post4")
            post_norm("post4", "ffn2_g_post")
            for i in (1, 3):
                dve.wait_ge(y_turned, 4 + i + 1)
                V.tensor_copy(ytok[:, i, 512:D], aux(f"y{i}")[:, 1, :]).then_inc(y_out_v, 1)

        @block.tensor
        def _(pe):
            def job_products(J, u, X, kt):
                for k, (wi, xi) in enumerate(PRODUCTS):
                    for half in range(2):
                        ins = pe.matmul(slot(u)[:, half, 0:HALF], wp[:, J % 2, wi, kt], X(xi, kt, half),
                                        start=kt == 0 and k == 0, stop=kt == KT - 1 and k == len(PRODUCTS) - 1)
                if kt == KT - 1:
                    ins.then_inc(job_done, 1)

            def job(name, i, X, need=None, b=0, j=0):
                J, u = pl.base[name][0] + i, pl.base[name][1] + i
                wait_slot(pe, u, per_body(b, j, 6, 2))
                pe.wait_ge(wlo, prepared(J) + 1 + per_body(b, j, JOBS_PER_BLOCK, 8))
                for kt in range(KT):
                    if need:
                        need(kt)
                    job_products(J, u, X, kt)

            def memory_jobs(name, count):
                for i in range(count):
                    J, u = pl.base[name][0] + i, pl.base[name][1] + i
                    s = J // 2
                    wait_slot(pe, u)
                    pe.wait_ge(loaded[s % RAW], 16 * (s // RAW + 1))
                    for kt in range(KT):
                        ins = pe.matmul(slot(u)[:, 0, 0:MEM], raw[:, s % RAW, kt, (J % 2) * P:(J % 2 + 1) * P], memT[:, kt, :],
                                        start=kt == 0, stop=kt == KT - 1)
                    ins.then_inc(job_done, 1)

            def half_of(tile):
                return lambda part, kt, half: tile[:, part, kt, half * HALF:(half + 1) * HALF]

            def jobs(name, X, need=None, count=KT, **kw):
                for i in range(count):
                    job(name, i, X, need if i == 0 else None, **kw)

            def turn(name, tiles):
                wait_slot(pe, pl.aux[name][1])
                for dst, src in tiles:
                    m = src.shape[0]
                    ins = pe.transpose(dst, src, ident[0:m, 0:m])
                ins.then_inc(filled, 1)

            def sum_tile(name, t, count, src):
                if t == 0:
                    wait_slot(pe, pl.aux[name][1])
                for half in range(2):
                    ins = pe.matmul(aux(name)[:, half, 0:HALF], ones[:, :], src[:, half * HALF:(half + 1) * HALF],
                                    start=t == 0, stop=t == count - 1)
                if t < count - 1:
                    ins.then_inc(sums[name]["summed"], 1)
                else:
                    ins.then_inc(filled, 1)

            def sum_squares(name):
                wait_slot(pe, pl.aux[name][1])
                pe.wait_ge(sums[name]["added"], KT - 2)
                for half in range(2):
                    pe.matmul(aux(name)[:, half, 0:HALF], ones[:, :], acc[:, half * HALF:(half + 1) * HALF],
                              start=True, stop=False)
                pe.wait_ge(sums[name]["squared"], KT)
                for half in range(2):
                    ins = pe.matmul(aux(name)[:, half, 0:HALF], ones[:, :], sq[:, (KT - 1) % 2, half * HALF:(half + 1) * HALF],
                                    start=False, stop=True)
                ins.then_inc(filled, 1)

            def jobs_normed(name, pre, count):
                J, u = pl.base[name]
                for t in range(KT + 2):
                    if t in (0, 2):
                        wait_slot(pe, u + t // 2)
                    if t == 0:
                        pe.wait_ge(wlo, prepared(J) + 1)
                    if t < KT:
                        pe.wait_ge(sums[pre]["ready"], t + 1)
                        job_products(J, u, half_of(n), t)
                    if t >= 2 and t % 2 == 0:
                        pe.wait_ge(sums[pre]["added"], t // 2)
                        sum_tile(pre, t // 2 - 1, KT // 2, acc)
                    if t == 2:
                        pe.wait_ge(wlo, prepared(J + 1) + 1)
                    if t >= 2:
                        job_products(J + 1, u + 1, half_of(n), t - 2)
                for i in range(2, count):
                    job(name, i, half_of(n))

            def ffn(name, pre):
                def product_ready(b):
                    return lambda kt: pe.wait_ge(mid_ready, MID0[name] + kt + 1 + per_body(b, 0, KT, 4))

                def down(b):
                    for i in range(KT):
                        job(name, 16 + i, half_of(mid), product_ready(b) if i == 0 else None, b=b)

                jobs_normed(name, pre, 16)
                down(0)
                with pe.Fori(1, BLOCKS) as b:
                    with pe.Fori(0, 2) as j:
                        for i in range(8):
                            job(name, i, half_of(n), b=b, j=j)
                    down(b)

            pe.wait_ge(id_set, 2)
            pe.wait_ge(const_set, 1)
            for i in range(TT):
                m = token_tile(i)[1]
                pe.wait_ge(ld_x[i] if i < 4 else ld_xs, 16)
                turn(f"x{i}", [(eight(aux(f"x{i}"))[:, kt, 0:m], xin[0:m, i, kt * P:(kt + 1) * P]) for kt in range(KT)])
                if i == 1:
                    pe.wait_ge(ld_small, 16 * 6)
                    pe.wait_ge(ld_rest, 16 * 6)
                    turn("gains", [(aux("gains")[:, 0, 0:84], graw[:, :])])
            pe.wait_ge(ld_cw, 16)
            turn("convw", [(eight(aux("convw"))[:, ct, 0:TAPS], cwraw[:, ct * P:(ct + 1) * P]) for ct in range(CT)])
            pe.wait_ge(ld_ws, 16)
            turn("spatial", [(eight(aux("spatial"))[:, hd, :], wsr[:, hd, :]) for hd in range(4)])
            ffn("ffn1", "pre1")
            sum_squares("post1")
            for t in range(MT):
                pe.wait_ge(mem_n, t + 1)
                turn(f"mem{t}", [(eight(aux(f"mem{t}"))[:, kt, :], memraw[:, t, kt * P:(kt + 1) * P]) for kt in range(KT)])
            jobs_normed("glu0", "pre2", 4)
            pe.wait_ge(ld_st, 16)
            for r in range(2):
                turn(f"state{r}", [(eight(aux(f"state{r}"))[:, ct, 0:120], straw[:, r, ct * P:(ct + 1) * P]) for ct in range(CT)])
            jobs("glu1", half_of(n), None, 4)
            pieces = []
            for i in range(TT):
                o, m = token_tile(i)
                pieces.append((flat(aux("rcol"))[0:m, i * P:(i + 1) * P], R[:, o:o + m]))
            pe.wait_ge(sums["pre2"]["recip"], 1)
            turn("rcol", pieces)
            wait_freed(pe, "mem0")
            wait_freed(pe, "mem1")
            memory_jobs("k0", 2)

            def turn_v(t):
                wait_use_freed(pe, pl.base[f"sv{t}"][1])
                pieces = []
                for i in range(TT):
                    o, m = token_tile(i)
                    pieces.append((flat(aux(f"vt{t}"))[0:m, i * P:(i + 1) * P], sq[:, t % 2, o:o + m]))
                turn(f"vt{t}", pieces)

            jobs("sv0", half_of(n), None, 1)
            for t in range(1, 4):
                jobs(f"sv{t}", half_of(n), None, 1)
                turn_v(t - 1)
                if t == 1:
                    memory_jobs("k2", 2)
            jobs("u0", half_of(n), None, 1)
            turn_v(3)
            for t in range(1, 4):
                jobs(f"u{t}", half_of(n), None, 1)

            memory_jobs("k4", 4)

            def spatial(heads):
                pe.wait_ge(sv_b, TT)
                pe.wait_ge(masked, 1)
                pe.wait_ge(ld_bd, 16 * NB)
                for hd in heads:
                    name, cols = f"sg{hd}", slice(hd * P, (hd + 1) * P)
                    wait_slot(pe, pl.aux[name][1])
                    for c in range(4):
                        pe.matmul(aux(name)[:, 0, c * P:(c + 1) * P], sv[:, c, cols], wsT[:, hd, :], start=True, stop=True)
                    pe.matmul(aux(name)[:, 1, 0:NB * DEC], sv[0:NB * DEC, 4, cols], bd[:, hd, :], start=True, stop=True)\
                        .then_inc(filled, 1)

            memory_jobs("v0", 6)
            for t in range(CT):
                pe.wait_ge(conv_step, 2 * (t + 1) * TAPS)
                sum_tile("cmean", t, CT, f[:, 4 + t])
            spatial((0, 1))
            for t in range(CT):
                pe.wait_ge(sums["cvar"]["squared"], t + 1)
                sum_tile("cvar", t, CT, sq[:, t % 2])
            spatial((2, 3))
            memory_jobs("v6", 2)
            def turn_rows(name, src):
                for t in range(MT):
                    turn(f"{name}{t}", [(eight(aux(f"{name}{t}"))[:, ft, :], src[:, ft, t * P:(t + 1) * P]) for ft in range(KT)])

            turn_rows("ktok", kT)
            jobs("out", half_of(mid), lambda kt: pe.wait_ge(mid_ready, MID0["mix"] + kt + 1))
            sum_squares("post2")
            for e in range(2):
                wait_use_freed(pe, pl.base["v0"][1] + 4 + e)
                wait_use_freed(pe, pl.base["v6"][1] + e)
            turn_rows("vtok", vT)
            for e in range(4):
                wait_use_freed(pe, pl.base["glu1"][1] + e)
            turn("glup", [(aux("glup")[0:LEFT, 0, ct * P:(ct + 1) * P], glu[:, ct, SEQ:SEQ + LEFT]) for ct in range(CT)])
            pe.wait_ge(gs_ready, 1)
            turn("glus", [(aux("glus")[0:NB * DEC, 0, ct * P:(ct + 1) * P], gsm[:, ct, :]) for ct in range(CT)])
            jobs_normed("q", "pre3", KT)
            for e in range(4):
                wait_use_freed(pe, pl.base["q"][1] + 4 + e)

            def sample_scores(b):
                name = f"ss{b}"
                wait_slot(pe, pl.aux[name][1])
                pe.wait_ge(qs_ready, KT)
                wait_freed(pe, f"kta{b}")
                wait_freed(pe, f"ktb{b}")
                for ft in range(KT):
                    ins = pe.matmul(aux(name)[0:HEADS * DEC, 0, 0:MEM], qs[:, b, ft, :], kts[:, b % 2, ft, :],
                                    start=ft == 0, stop=ft == KT - 1)
                ins.then_inc(filled, 1)

            def turn_probs(i):
                pe.wait_ge(p_ready, 4 * i + 4)
                turn(f"pt{i}", [(eight(aux(f"pt{i}"))[:, 2 * hd + t, :], prob[:, i % 2, hd, t * P:(t + 1) * P])
                                for hd in range(HEADS) for t in range(MT)])

            for i in range(4):
                name = f"sc{i}"
                wait_slot(pe, pl.aux[name][1])
                for hd in range(HEADS):
                    for d in range(2):
                        ins = pe.matmul(aux(name)[:, hd // 2, (hd % 2) * MEM:(hd % 2 + 1) * MEM],
                                        f[:, 2 * hd + d, i * P:(i + 1) * P], kT[:, 2 * hd + d, :], start=d == 0, stop=d == 1)
                ins.then_inc(filled, 1)
                for b in (2 * i, 2 * i + 1):
                    pe.wait_ge(ld_k[b % 4], 16 * (b // 4 + 1))
                    keys = kring[:, b % 4] if b % 4 < 3 else k3[:, :, :]
                    for t, x in enumerate("ab"):
                        turn(f"kt{x}{b}", [(eight(aux(f"kt{x}{b}"))[:, ft, :], keys[:, t, ft * P:(ft + 1) * P]) for ft in range(KT)])
                    if b:
                        sample_scores(b - 1)
                if i:
                    turn_probs(i - 1)
            sample_scores(7)
            turn_probs(3)

            def head_out(o):
                name = f"pv{o}"
                wait_slot(pe, pl.aux[name][1])
                for t in range(MT):
                    ins = pe.matmul(aux(name)[:, 0, :], vtok[:, t, o * P:(o + 1) * P], pT[:, o // 2 * 2 + t, :], start=t == 0, stop=t == 1)
                ins.then_inc(filled, 1)

            for i in range(4):
                wait_freed(pe, f"pt{i}")
            for o in range(3):
                head_out(o)
            pe.wait_ge(sp_ready, 2)
            turn("sprob", [(aux("sprob")[:, t, r * P:(r + 1) * P], psm[:, r, t * P:(t + 1) * P]) for r in range(2) for t in range(MT)])
            for o in range(3, 8):
                head_out(o)
            wait_slot(pe, pl.aux["pvs"][1])
            wait_freed(pe, "sprob")
            for b in range(NB):
                pe.wait_ge(ld_v[b % 5], 16 * (b // 5 + 1))
                vals = vx[:, b - 3] if 3 <= b < 5 else kring[:, b % 5]
                for hd in range(HEADS):
                    c = slice(hd * 256, (hd + 1) * 256)
                    for t in range(MT):
                        ins = pe.matmul(flat(aux("pvs"))[0:NB * DEC, c], ps[:, t, hd, b * 64:(b + 1) * 64], vals[:, t, c],
                                        start=b == 0 and t == 0 and hd % 2 == 0,
                                        stop=b == NB - 1 and t == MT - 1 and hd % 2 == 1)
                ins.then_inc(vs_used if b < NB - 1 else filled, 1)
            wait_freed(pe, "pvs")
            turn("pvt", [(aux("pvt")[:, 0, o * 64:(o + 1) * 64], os_[:, o * P:(o + 1) * P]) for o in range(KT)])

            def attended(kt):
                wait_freed(pe, f"pv{kt}")
                if kt == 0:
                    wait_freed(pe, "pvt")
            jobs("o", half_of(mid), attended)
            sum_squares("post3")
            ffn("ffn2", "pre4")
            sum_squares("post4")
            for i in range(4):
                wait_slot(pe, pl.aux[f"y{i}"][1])
            for kt in range(KT):
                pe.wait_ge(sums["post4"]["done"], kt + 1)
                for i in range(4):
                    ins = pe.transpose(flat(aux(f"y{i}"))[:, kt * P:(kt + 1) * P], h[:, kt, i * P:(i + 1) * P], ident[:, :])
                    if kt in (3, KT - 1):
                        ins.then_inc(y_turned, 1)
            pe.wait_ge(y_out_a, 5)
            for kt in range(KT):
                ins = pe.transpose(flat(aux("y4"))[0:NB * DEC, kt * P:(kt + 1) * P], h[:, kt, SEQ:T], ident[:, :])
            ins.then_inc(y_turned, 1)


_INS = ["x_prompt", "x_sample", "mem_prompt", "cache_mem_k", "cache_mem_v", "state_conv",
        "ffn1_g_pre", "ffn1_w_gate", "ffn1_w_up", "ffn1_w_down", "ffn1_g_post",
        "mix_g_pre", "mix_w_in", "sgu_ln_g", "sgu_ln_b", "sgu_w_s", "sgu_b_s",
        "conv_w", "conv_b", "conv_ln_g", "conv_ln_b", "mix_w_out", "mix_g_post",
        "mem_g", "xattn_g_pre", "xattn_w_q", "xattn_w_k", "xattn_w_v", "xattn_w_o", "xattn_g_post",
        "ffn2_g_pre", "ffn2_w_gate", "ffn2_w_up", "ffn2_w_down", "ffn2_g_post"]
_OUTS = [(1, 512, 1024), (8, 8, 1024), (1, 1, 256, 4, 256), (1, 1, 256, 4, 256), (1, 1, 30, 512), (1, 8, 30, 512),
         (1, 1, 128, 512), (1, 8, 8, 512)]


def kernel(**inputs):
    import numpy as _np
    import concourse.bacc as _bacc
    from concourse import mybir as _mybir
    from concourse.bass_utils import run_bass_kernel_spmd as _run

    nc = _bacc.Bacc("TRN2", target_bir_lowering=False, num_devices=1)
    arrays, aps = {}, {}
    for name in _INS:
        x = _np.ascontiguousarray(inputs[name])
        arrays[f"in_{name}_dram"] = x
        aps[name] = nc.dram_tensor(f"in_{name}_dram", x.shape, _mybir.dt.from_np(x.dtype), kind="ExternalInput").ap()
    outs = [nc.dram_tensor(f"out_{i}_dram", shape, _mybir.dt.float32, kind="ExternalOutput").ap()
            for i, shape in enumerate(_OUTS)]
    build(nc, aps, outs)
    r = _run(nc, [arrays], core_ids=[0])
    return tuple(r.results[0][f"out_{i}_dram"] for i in range(len(_OUTS)))
```
